# Optimizing a Trainium2 kernel written in Bass

```python
import jax, jax.numpy as jnp
from jax import lax
import numpy as np

D_MODEL = 1024
BATCH = 1
SEQ = 1024
DEPTH = 1
DEC_BATCH = 1
DEC_SEQ = 32
PAST_LEN = 128

CHUNK = 64
D_POOL = 512
N_POOL_GROUPS = 4
POOL_GROUP = D_POOL // N_POOL_GROUPS
POOL_WINDOWS = (2, 4, 8, 16)
POOL_HIST = max(POOL_WINDOWS) - 1
D_CONV = 512
CONV_WIDTH = 31
CONV_HIST = CONV_WIDTH - 1
N_EXPERT_GROUPS = 4
EXPERTS_PER_GROUP = 8
TOP_K_INNER = 2
D_EXPERT = 256
IN_COLS = D_POOL + 2 * D_CONV + 2 * D_MODEL
RMS_EPS = 1e-6
LN_EPS = 1e-5

kernel_name = "gated_pool_conformer_hiermoe_stream"

def rmsnorm(x, g):
    xf = x.astype(jnp.float32)
    y = xf * lax.rsqrt(jnp.mean(xf * xf, axis=-1, keepdims=True) + RMS_EPS)
    return (y * g.astype(jnp.float32)).astype(x.dtype)

def pool_mixer(u, hist, past, w_grp, scale):
    B, L, _ = u.shape
    seq = jnp.concatenate([hist.astype(u.dtype), u], axis=1).astype(jnp.float32)
    cs = jnp.pad(jnp.cumsum(seq, axis=1), ((0, 0), (1, 0), (0, 0)))
    t = jnp.arange(L, dtype=jnp.float32)
    means = []
    for gi, w in enumerate(POOL_WINDOWS):
        c0, c1 = gi * POOL_GROUP, (gi + 1) * POOL_GROUP
        end = cs[:, POOL_HIST + 1:POOL_HIST + 1 + L, c0:c1]
        start = cs[:, POOL_HIST + 1 - w:POOL_HIST + 1 - w + L, c0:c1]
        cnt = jnp.minimum(jnp.float32(w), past + t + 1.0)
        means.append((end - start) / cnt[None, :, None])
    mean = jnp.stack(means, axis=2)
    diff = mean - u.astype(jnp.float32).reshape(B, L, N_POOL_GROUPS, POOL_GROUP)
    y = jnp.einsum('blgc,gcd->blgd', diff.astype(u.dtype), w_grp).reshape(B, L, D_POOL)
    return y * scale

def conv_module(v, hist, w_dw, b_dw, ln_g, ln_b):
    seq = jnp.concatenate([hist.astype(v.dtype), v], axis=1)
    y = lax.conv_general_dilated(seq, w_dw[:, None, :], window_strides=(1,), padding='VALID',
                                 dimension_numbers=('NWC', 'WIO', 'NWC'),
                                 feature_group_count=D_CONV)
    yf = (y + b_dw).astype(jnp.float32)
    mu = jnp.mean(yf, axis=-1, keepdims=True)
    var = jnp.mean(jnp.square(yf - mu), axis=-1, keepdims=True)
    yn = (yf - mu) * lax.rsqrt(var + LN_EPS) * ln_g.astype(jnp.float32) + ln_b.astype(jnp.float32)
    return jax.nn.silu(yn).astype(v.dtype)

def hier_moe(h, w_rg, b_rg, w_re, b_re, w_gate, w_up, w_down):
    B, L, _ = h.shape
    hf = h.reshape(B * L, D_MODEL)
    lg = (hf @ w_rg).astype(jnp.float32) + b_rg.astype(jnp.float32)
    pg = jax.nn.softmax(lg, axis=-1)
    g_top = jnp.argmax(lg, axis=-1)
    p_sel = jnp.take_along_axis(pg, g_top[:, None], axis=-1)[:, 0]
    le = ((hf @ w_re).astype(jnp.float32) + b_re.astype(jnp.float32)).reshape(-1, N_EXPERT_GROUPS, EXPERTS_PER_GROUP)
    le_sel = jnp.take_along_axis(le, g_top[:, None, None], axis=1)[:, 0]
    top_v, top_i = lax.top_k(le_sel, TOP_K_INNER)
    w2 = jax.nn.softmax(top_v, axis=-1) * p_sel[:, None]
    combine = jnp.sum(jax.nn.one_hot(top_i, EXPERTS_PER_GROUP, dtype=jnp.float32) * w2[..., None], axis=1)
    y = jnp.zeros((B * L, D_MODEL), jnp.float32)
    for g in range(N_EXPERT_GROUPS):
        cg = combine * (g_top == g).astype(jnp.float32)[:, None]
        a = jnp.einsum('td,edf->tef', hf, w_gate[g])
        b = jnp.einsum('td,edf->tef', hf, w_up[g])
        act = (jax.nn.silu(a) * b) * cg[..., None]
        y = y + jnp.einsum('tef,efd->td', act, w_down[g]).astype(jnp.float32)
    return y.astype(h.dtype).reshape(B, L, D_MODEL)

def layer(x, pool_hist, conv_hist, past, p):
    h = rmsnorm(x, p['g_mix'])
    z = h @ p['w_in']
    o = 0
    u_pool = z[..., o:o + D_POOL]; o += D_POOL
    ga = z[..., o:o + D_CONV]; o += D_CONV
    gb = z[..., o:o + D_CONV]; o += D_CONV
    gate_pool = z[..., o:o + D_MODEL]; o += D_MODEL
    gate_conv = z[..., o:o + D_MODEL]
    v = ga * jax.nn.sigmoid(gb)
    y_pool = pool_mixer(u_pool, pool_hist, past, p['w_pool_grp'], p['pool_scale']) @ p['w_pool_out']
    y_conv = conv_module(v, conv_hist, p['w_dw'], p['b_dw'], p['ln_g'], p['ln_b']) @ p['w_conv_out']
    merged = jax.nn.sigmoid(gate_pool) * y_pool + jax.nn.sigmoid(gate_conv) * y_conv
    x = x + merged @ p['w_out']
    x = x + hier_moe(rmsnorm(x, p['g_ffn']), p['w_rg'], p['b_rg'], p['w_re'], p['b_re'],
                     p['w_gate'], p['w_up'], p['w_down'])
    new_pool = jnp.concatenate([pool_hist.astype(u_pool.dtype), u_pool], axis=1)[:, -POOL_HIST:]
    new_conv = jnp.concatenate([conv_hist.astype(v.dtype), v], axis=1)[:, -CONV_HIST:]
    return x, new_pool, new_conv

def setup_inputs(seed: int = 0) -> dict:
    key = jax.random.key(seed)
    ks = jax.random.split(key, 24)
    n = lambda k, s, sc: jax.random.normal(k, s, jnp.float32) * sc
    G, E, F = N_EXPERT_GROUPS, EXPERTS_PER_GROUP, D_EXPERT
    return {
        'x_prompt': n(ks[0], (BATCH, SEQ, D_MODEL), 1.0),
        'x_sample': n(ks[1], (DEC_BATCH, DEC_SEQ, D_MODEL), 1.0),
        'state_pool': n(ks[2], (DEPTH, DEC_BATCH, POOL_HIST, D_POOL), 1.0),
        'state_conv': n(ks[3], (DEPTH, DEC_BATCH, CONV_HIST, D_CONV), 0.5),
        'g_mix': 1.0 + n(ks[4], (DEPTH, D_MODEL), 0.05),
        'w_in': n(ks[5], (DEPTH, D_MODEL, IN_COLS), D_MODEL ** -0.5),
        'w_pool_grp': n(ks[6], (DEPTH, N_POOL_GROUPS, POOL_GROUP, POOL_GROUP), POOL_GROUP ** -0.5),
        'pool_scale': 1.0 + n(ks[7], (DEPTH, D_POOL), 0.1),
        'w_pool_out': n(ks[8], (DEPTH, D_POOL, D_MODEL), D_POOL ** -0.5),
        'w_dw': n(ks[9], (DEPTH, CONV_WIDTH, D_CONV), CONV_WIDTH ** -0.5),
        'b_dw': n(ks[10], (DEPTH, D_CONV), 0.02),
        'ln_g': 1.0 + n(ks[11], (DEPTH, D_CONV), 0.05),
        'ln_b': n(ks[12], (DEPTH, D_CONV), 0.02),
        'w_conv_out': n(ks[13], (DEPTH, D_CONV, D_MODEL), D_CONV ** -0.5),
        'w_out': n(ks[14], (DEPTH, D_MODEL, D_MODEL), D_MODEL ** -0.5),
        'g_ffn': 1.0 + n(ks[15], (DEPTH, D_MODEL), 0.05),
        'w_rg': n(ks[16], (DEPTH, D_MODEL, G), D_MODEL ** -0.5),
        'b_rg': n(ks[17], (DEPTH, G), 0.01),
        'w_re': n(ks[18], (DEPTH, D_MODEL, G * E), D_MODEL ** -0.5),
        'b_re': n(ks[19], (DEPTH, G * E), 0.01),
        'w_gate': n(ks[20], (DEPTH, G, E, D_MODEL, F), D_MODEL ** -0.5),
        'w_up': n(ks[21], (DEPTH, G, E, D_MODEL, F), D_MODEL ** -0.5),
        'w_down': n(ks[22], (DEPTH, G, E, F, D_MODEL), F ** -0.5),
        'g_final': 1.0 + n(ks[23], (D_MODEL,), 0.05),
    }

def reference(x_prompt, x_sample, state_pool, state_conv, g_mix, w_in, w_pool_grp, pool_scale, w_pool_out,
              w_dw, b_dw, ln_g, ln_b, w_conv_out, w_out, g_ffn, w_rg, b_rg, w_re, b_re, w_gate, w_up, w_down,
              g_final):
    xp, xs = x_prompt, x_sample
    Bp = x_prompt.shape[0]
    npp, ncp, nps, ncs = [], [], [], []
    for l in range(DEPTH):
        p = {'g_mix': g_mix[l], 'w_in': w_in[l], 'w_pool_grp': w_pool_grp[l], 'pool_scale': pool_scale[l],
             'w_pool_out': w_pool_out[l], 'w_dw': w_dw[l], 'b_dw': b_dw[l], 'ln_g': ln_g[l], 'ln_b': ln_b[l],
             'w_conv_out': w_conv_out[l], 'w_out': w_out[l], 'g_ffn': g_ffn[l], 'w_rg': w_rg[l], 'b_rg': b_rg[l],
             'w_re': w_re[l], 'b_re': b_re[l], 'w_gate': w_gate[l], 'w_up': w_up[l], 'w_down': w_down[l]}
        zp = jnp.zeros((Bp, POOL_HIST, D_POOL), xp.dtype)
        zc = jnp.zeros((Bp, CONV_HIST, D_CONV), xp.dtype)
        xp, pp, cp = layer(xp, zp, zc, 0, p)
        xs, ps, cs = layer(xs, state_pool[l], state_conv[l], PAST_LEN, p)
        npp.append(pp); ncp.append(cp); nps.append(ps); ncs.append(cs)
    y_prompt = rmsnorm(xp, g_final)
    y_sample = rmsnorm(xs, g_final)
    new_pool_prompt = jnp.stack(npp, axis=0)
    new_conv_prompt = jnp.stack(ncp, axis=0)
    new_pool_sample = jnp.stack(nps, axis=0)
    new_conv_sample = jnp.stack(ncs, axis=0)
    return (y_prompt, y_sample, new_pool_prompt, new_conv_prompt, new_pool_sample, new_conv_sample)


_drawn_inputs = setup_inputs


def setup_inputs(seed=0):
    import zlib

    import numpy as np

    out = dict(_drawn_inputs(seed))
    spreads = {}
    factors = {'ln_b': 4.574, 'b_re': 3.455, 'b_rg': 5.94}
    for name, (base, spread) in spreads.items():
        noise = np.random.default_rng([zlib.crc32(name.encode()), seed]).standard_normal(out[name].shape)
        drawn = base * np.exp(spread * noise) if base else spread * noise
        out[name] = __import__('jax').numpy.asarray(drawn.astype(out[name].dtype))
    for name, factor in factors.items():
        out[name] = (out[name] * factor).astype(out[name].dtype)
    return out
```

```python
from contextlib import ExitStack

import concourse.bass as bass
from concourse import mybir

ACT = mybir.ActivationFunctionType
ALU = mybir.AluOpType
AX = mybir.AxisListType
F32 = mybir.dt.float32
F32R = mybir.dt.float32r
U32 = mybir.dt.uint32
I32 = mybir.dt.int32

P = 128
D = 1024
KD = D // P
SEQ = 1024
DEC = 32
T = SEQ + DEC
TILES = (T + P - 1) // P
LAST = T - (TILES - 1) * P
CH = T // 3
CHUNKS = 3
D_POOL = 512
D_CONV = 512
GR = D_POOL // P
PH = 15
CW = 31
HIST = CW - 1
UW = PH + SEQ + PH + DEC
VW = HIST + SEQ + HIST + DEC
CWID = SEQ + HIST + DEC
G = 4
E = 8
GE = G * E
F = 256
KF = F // P
NR = G + GE
PASSES = (T + P - 1) // P
SLOTS = PASSES * GE * P
NOWHERE = 1.0e6
WB = 4
RMS_EPS = 1e-6
LN_EPS = 1e-5


def build(nc, I, O):
    with ExitStack() as ctx:
        def sem(name):
            return ctx.enter_context(nc.semaphore(name))

        cursor = [16512]

        def region(nbytes):
            o = cursor[0]
            cursor[0] += (nbytes + 31) // 32 * 32
            assert cursor[0] <= 229344, cursor
            return o

        def at(name, shape, dt, offset):
            return nc.alloc_sbuf_tensor_at(name, shape, dt, offset=offset)

        def small(name, shape, dt=F32):
            n = 4
            for s in shape[1:]:
                n *= s
            return at(name, shape, dt, region(n))

        HT = KD * T
        r_h = region((2 * HT + P - DEC) * 4)
        r_m = region(max(KD * T, TILES * D) * 4)
        r_uv = region(GR * (UW + VW) * 4)
        r_yp = region(2 * GR * T * 4)
        r_w = region(6 * KD * P * 4)
        r_s = region(2 * T * 4)
        r_wo = region(KD * P * 4)

        hT = at("hT", [P, 2 * HT + P - DEC], F32R, r_h)
        h_hi = hT[:, 0:HT].rearrange("p (k t) -> p k t", k=KD)
        h_lo = hT[:, HT:2 * HT].rearrange("p (k t) -> p k t", k=KD)

        U = at("U", [P, GR, UW], F32, r_uv)
        V = at("V", [P, GR, VW], F32, r_uv + GR * UW * 4)
        C = at("C", [P, GR, CWID], F32, r_uv)

        xs = at("xs", [P, 2, D], F32, r_yp)
        xn = at("xn", [P, 2, D], F32, r_yp + 8 * D)
        g_mix_b = at("g_mix_b", [P, D], F32, r_yp + 16 * D)
        squares = at("squares", [P, D], F32, r_s)

        w_raw = at("w_raw", [P, 2, KD, P], F32, r_w)
        w_hi = at("w_hi", [P, 2, KD, P], F32R, r_w + 2 * KD * P * 4)
        w_lo = at("w_lo", [P, 2, KD, P], F32R, r_w + 4 * KD * P * 4)

        hist_in = at("hist_in", [CW, 3, D_CONV], F32, r_m)
        vec_in = at("vec_in", [4 * GR, P], F32, r_m + 3 * D_CONV * 4)
        win = at("win", [P, 2, UW], F32, r_yp)
        diff = at("diff", [P, T], F32, r_yp + (8 * UW + 31) // 32 * 32)
        d_hi = at("d_hi", [P, GR, T], F32R, r_m)
        d_lo = at("d_lo", [P, GR, T], F32R, r_m + GR * T * 4)
        y_hi = at("y_hi", [P, GR, T], F32R, r_yp)
        y_lo = at("y_lo", [P, GR, T], F32R, r_yp + GR * T * 4)
        a_hi = at("a_hi", [P, GR, T], F32R, r_uv + GR * UW * 4)
        a_lo = at("a_lo", [P, GR, T], F32R, r_uv)
        M = at("M", [P, KD, T], F32, r_m)
        x1 = at("x1", [P, TILES, D], F32, r_m)
        S = at("S", [P, 2, T], F32, r_s)
        ln_sq = at("ln_sq", [P, GR, 512], F32, r_s)
        ln_rstd = at("ln_rstd", [P, 512], F32, r_s)
        xr = at("xr", [P, 2, 512], F32, r_s)
        wo_raw = at("wo_raw", [P, 2, 512], F32, r_wo)
        wo_hi = [at("wo_hi0", [P, KD, 512], F32R, r_yp), at("wo_hi1", [P, KD, 512], F32R, r_uv)]
        wo_lo = [at("wo_lo0", [P, KD, 512], F32R, r_yp + KD * 2048), at("wo_lo1", [P, KD, 512], F32R, r_uv + KD * 2048)]
        state_out = at("state_out", [32, 4, D_CONV], F32, r_s)

        ident = small("ident", [P, P])
        w_dw = small("w_dw", [P, GR, CW])
        vecs = small("vecs", [P, 4 * GR])
        ln_mean = small("ln_mean", [P, P])
        inv_cnt = small("inv_cnt", [P, 16])
        eps_ln = small("eps_ln", [P, 1])
        sumsq = small("sumsq", [P, TILES])
        rstd = small("rstd", [P, TILES])
        eps_rms = small("eps_rms", [P, 1])

        tab_init = at("tab_init", [P, SLOTS * 2 // P], F32, r_m + 8192)
        h2 = at("h2", [P, 2, D], F32, r_w)
        h2T = at("h2T", [P, 2, KD, P], F32, r_w + 8192)
        g_ffn_b = at("g_ffn_b", [P, D], F32, r_w + 16384)
        w_r = at("w_r", [P, KD, NR], F32, r_w + 20480)
        b_r = at("b_r", [P, NR], F32, r_w + 21632)
        L = at("L", [P, TILES, NR], F32, r_w + 21792)
        squares2 = at("squares2", [P, D], F32, r_s + 4096)
        cur = [r_wo]

        def const(name, shape, dt=F32, start=None):
            if start is not None:
                cur[0] = start
            n = 4
            for v in shape[1:]:
                n *= v
            o = cur[0]
            cur[0] += (n + 31) // 32 * 32
            return at(name, shape, dt, o)

        tri = const("tri", [P, P], start=r_wo)
        io_i = const("io_i", [P, GE], I32)
        io = const("io", [P, GE])
        thr = const("thr", [P, PASSES - 1])
        ebase = const("ebase", [P, GE])
        pay_i = const("pay_i", [P, TILES, 2, 2], I32)
        pay = const("pay", [P, TILES, 2, 2])
        valid = const("valid", [P, 1])
        assert cur[0] <= r_wo + 4096
        N9 = [P, TILES]
        gmax = const("gmax", N9, start=r_w + 8192)
        gmin = const("gmin", N9)
        zsum = const("zsum", N9)
        m1 = const("m1", N9)
        m2 = const("m2", N9)
        i1 = const("i1", N9)
        ex = const("ex", N9)
        den = const("den", N9)
        rank = const("rank", [P, TILES, 2])
        eb = const("eb", [P, TILES, 2])
        rnd = const("rnd", [P, TILES, 2])
        slot_f = const("slot_f", [P, TILES, 2])
        slot_u = const("slot_u", [P, TILES, 2], U32)
        tg = const("tg", [P, TILES, G])
        og = const("og", [P, TILES, G])
        dg = const("dg", [P, TILES, G])
        les = const("les", [P, TILES, E])
        te = const("te", [P, TILES, E])
        oe = [const("oe0", [P, TILES, E]), const("oe1", [P, TILES, E])]
        ge8 = const("ge8", [P, 2 * TILES, PASSES - 1])
        nmax = const("nmax", [P, 1])
        np_f = const("np_f", [P, 1])
        assert cur[0] <= r_w + 16384
        Ek = [const("Ek0", [P, TILES, G, E], start=r_s), const("Ek1", [P, TILES, G, E])]
        A = const("A", [P, TILES, GE])
        tmp32 = const("tmp32", [P, TILES, G, E])
        Acum = const("Acum", [P, TILES + 1, GE])
        tab = const("tab", [P, P, 2])
        assert cur[0] <= r_s + 8448
        w_off = [r_h, r_h + 24576, r_uv, r_yp]
        wgu = [at(f"wgu{u}", [P, KD, 2 * F], F32, w_off[u]) for u in range(WB)]
        wdn = [at(f"wdn{u}", [P, KF, D], F32, w_off[u] + 16384) for u in range(WB)]
        X = at("X", [P, 4, D], F32, r_h + 49152)
        Y = at("Y", [P, 2, D], F32, r_uv + 24576)
        XT = at("XT", [P, 2, KD, P], F32, r_yp + 24576)
        sg = at("sg", [P, 2, F], F32, r_w)
        act_ = at("act_", [P, 2, F], F32, r_w + 2048)
        AT = at("AT", [P, 2, KF, P], F32, r_w + 4096)
        yy = at("yy", [P, 2, 2, D], F32, r_w + 8192)
        wts = const("wts", [P, TILES, 2], start=r_h + 65536)
        g_idx = const("g_idx", [P, GE])
        s_idx = const("s_idx", [P, GE])
        g_now = const("g_now", [P, 4], U32)
        s_now = const("s_now", [P, 2], U32)
        np_i = const("np_i", [P, 1], I32)
        assert cur[0] <= r_m
        g_fin_b = at("g_fin_b", [P, D], F32, r_wo)
        sq3 = at("sq3", [P, 2, D], F32, r_s)

        H2 = nc.dram_tensor("H2", (T, D), F32, kind="Internal").ap()
        TAB = nc.dram_tensor("TAB", (SLOTS, 2), F32, kind="Internal").ap()
        YK = nc.dram_tensor("YK", (2 * T, D), F32, kind="Internal").ap()

        ps = ctx.enter_context(nc.psum_tensor("ps", [P, 8, 512], F32))

        s_const = sem("s_const")
        s_x = [sem("s_x0"), sem("s_x1")]
        s_w = [sem("s_w0"), sem("s_w1")]
        s_hist = sem("s_hist")
        s_ident = sem("s_ident")
        s_eps = sem("s_eps")
        s_zero = sem("s_zero")
        s_std = sem("s_std")
        s_sq = sem("s_sq")
        s_rstd = sem("s_rstd")
        s_xn = sem("s_xn")
        s_xT = sem("s_xT")
        s_hhi = sem("s_hhi")
        s_hlo = sem("s_hlo")
        s_histT = sem("s_histT")
        s_histC = sem("s_histC")
        s_whi = sem("s_whi")
        s_wlo = sem("s_wlo")
        s_mm = sem("s_mm")
        s_free = [sem("s_free0"), sem("s_free1")]
        s_sT = sem("s_sT")
        s_sC = sem("s_sC")
        s_out = sem("s_out")
        s_tail = sem("s_tail")
        s_pool = sem("s_pool")
        s_inv = sem("s_inv")
        s_diff = sem("s_diff")
        s_conv = sem("s_conv")
        s_grp = sem("s_grp")
        s_yhi = sem("s_yhi")
        s_ylo = sem("s_ylo")
        s_mean = sem("s_mean")
        s_cen = sem("s_cen")
        s_csq = sem("s_csq")
        s_var = sem("s_var")
        s_lstd = sem("s_lstd")
        s_lrec = sem("s_lrec")
        s_norm = sem("s_norm")
        s_silu = sem("s_silu")
        s_ahi = sem("s_ahi")
        s_alo = sem("s_alo")
        s_sy = sem("s_sy")
        s_mhi = sem("s_mhi")
        s_mlo = sem("s_mlo")
        s_wo = sem("s_wo")
        s_wohi = sem("s_wohi")
        s_wolo = sem("s_wolo")
        s_o = sem("s_o")
        s_xr = [sem("s_xr0"), sem("s_xr1")]
        s_res = sem("s_res")
        s_ti = sem("s_ti")
        s_rc = sem("s_rc")
        s_rb = sem("s_rb")
        s_sq2 = sem("s_sq2")
        s_std2 = sem("s_std2")
        s_rs2 = sem("s_rs2")
        s_h2 = sem("s_h2")
        s_h2st = [sem("s_h2st0"), sem("s_h2st1")]
        s_h2T = sem("s_h2T")
        s_h2c = sem("s_h2c")
        s_lg = sem("s_lg")
        s_rt = sem("s_rt")
        s_ra = sem("s_ra")
        s_re = sem("s_re")
        s_cum = sem("s_cum")
        s_rk = sem("s_rk")
        s_np = sem("s_np")
        s_slot = sem("s_slot")
        s_tabw = sem("s_tabw")
        s_tabi = sem("s_tabi")
        s_tabl = sem("s_tabl")
        s_tabT = sem("s_tabT")
        s_ix = sem("s_ix")
        s_tx = sem("s_tx")
        s_xtA = sem("s_xtA")
        s_xtD = sem("s_xtD")
        s_gu = sem("s_gu")
        s_sg = sem("s_sg")
        s_act = sem("s_act")
        s_ta = sem("s_ta")
        s_at = sem("s_at")
        s_down = sem("s_down")
        s_yA = sem("s_yA")
        s_yD = sem("s_yD")
        s_gc = sem("s_gc")
        s_f1 = sem("s_f1")
        s_tab0 = sem("s_tab0")
        s_sc = sem("s_sc")
        s_gfin = sem("s_gfin")
        s_fq = sem("s_fq")
        s_fs = sem("s_fs")
        s_fr = sem("s_fr")
        s_fa = sem("s_fa")
        s_fo = sem("s_fo")
        s_one = sem("s_one")
        s_tri = sem("s_tri")
        s_ct = sem("s_ct")
        s_wl = [sem(f"s_wl{u}") for u in range(WB)]
        s_xg = [sem(f"s_xg{u}") for u in range(4)]
        s_ys = [sem("s_ys0"), sem("s_ys1")]
        s_yy = [sem("s_yy0"), sem("s_yy1")]

        w_in_v = I["w_in"][0].rearrange("(k p) m -> p k m", p=P)
        xp = I["x_prompt"][0]
        block = ctx.enter_context(nc.Block())

        def x_rows(t):
            return (xp[t * P:(t + 1) * P, :], P) if t < TILES - 1 else (I["x_sample"][0], LAST)

        def wait(eng, s, v):
            if not isinstance(v, int) or v > 0:
                eng.wait_ge(s, v)

        def groups(eng, step, p):
            for u in range(WB):
                step(p, 0, u)
            with eng.Fori(1, GE // WB - 1) as i:
                for u in range(WB):
                    step(p, i, u)
            for u in range(WB):
                step(p, GE // WB - 1, u)

        def rounds(eng, one):
            one(0)
            eng.wait_ge(s_np, 1)
            n = eng.value_load(np_i[0:1, 0:1], min_val=1, max_val=PASSES)
            with eng.If(n > 1):
                with eng.Fori(1, n) as p:
                    one(p)
            return n

        def runs(c, hist):
            a, b = c * CH, (c + 1) * CH
            out = []
            if a < SEQ:
                e = min(b, SEQ)
                out.append((0, hist + a, e - a))
            if b > SEQ:
                s = max(a, SEQ)
                out.append((s - a, 2 * hist + s, b - s))
            return out

        NU, NV = GR, 2 * GR
        NG = NU + NV
        NB = NG + 1
        NC = NB + 2 * KD
        NP = NC + 2 * KD
        GATE_P = D_POOL + 2 * D_CONV
        GATE_C = GATE_P + D
        A_TAPS = 7
        B_TAPS = 3
        w_po_v = I["w_pool_out"][0].rearrange("(k p) m -> p k m", p=P)
        w_co_v = I["w_conv_out"][0].rearrange("(k p) m -> p k m", p=P)
        w_out_v = I["w_out"][0].rearrange("(k p) m -> p k m", p=P)
        LN_PIECES = [(0, 512), (512, 512), (SEQ + HIST, DEC)]
        C_RUNS = [(0, 0, SEQ), (SEQ + HIST, SEQ, DEC)]
        BIAS, LN_G, LN_B, SCALE = 0, GR, 2 * GR, 3 * GR

        @block.sync
        def _(sp):
            sp.dma_start(g_mix_b[:], I["g_mix"][0].partition_broadcast(P)).then_inc(s_const, 16)
            for t in range(TILES):
                src, n = x_rows(t)
                if t >= 2:
                    sp.wait_ge(s_xn, t - 1)
                sp.dma_start(xs[0:n, t % 2, :], src).then_inc(s_x[t % 2], 16)
                if t == 1:
                    for q, v in enumerate(("b_dw", "ln_g", "ln_b", "pool_scale")):
                        sp.dma_start(vec_in[q * GR:(q + 1) * GR, :],
                                     I[v][0].rearrange("(g p) -> g p", p=P)).then_inc(s_hist, 16)
                    sp.dma_start(hist_in[:, 2, :], I["w_dw"][0]).then_inc(s_hist, 16)
                    sp.dma_start(hist_in[0:PH, 0, :], I["state_pool"][0, 0]).then_inc(s_hist, 16)
                    sp.dma_start(hist_in[0:HIST, 1, :], I["state_conv"][0, 0]).then_inc(s_hist, 16)
                    for s in range(2):
                        sp.dma_start(w_raw[:, s], w_in_v[:, :, s * P:(s + 1) * P]).then_inc(s_w[s], 16)

            def panel(n, s, col, src=w_in_v, K=KD):
                sp.wait_ge(s_wlo, n - 1)
                sp.dma_start(w_raw[:, s, 0:K], src[:, :, bass.ds(col, P)]).then_inc(s_w[s], 16)

            sp.wait_ge(s_ti, 1)
            sp.dma_start(TAB.rearrange("(p a) c -> p (a c)", p=P), tab_init[:]).then_inc(s_tabi, 16)
            panel(2, 0, 2 * P)
            panel(3, 1, 3 * P)
            with sp.Fori(1, GR + 1) as j:
                panel(NU - 2 + 2 * j, 0, 2 * GR * P - P + j * P)
                panel(NU - 1 + 2 * j, 1, GR * P - P + j * P)
            sp.wait_ge(s_whi, NG - 1)
            sp.wait_ge(s_wlo, NG - 1)
            sp.dma_start(w_raw[:, 0, 0:GR], I["w_pool_grp"][0].rearrange("g c d -> c g d")).then_inc(s_w[0], 16)
            sp.wait_ge(s_sC, 1)
            sp.dma_start(O["new_pool_prompt"][0, 0], state_out[0:PH, 0, :]).then_inc(s_tail, 16)
            sp.dma_start(O["new_pool_sample"][0, 0], state_out[0:PH, 1, :]).then_inc(s_tail, 16)
            with sp.Fori(1, KD + 1) as j:
                panel(NB - 2 + 2 * j, 1, GATE_P - P + j * P)
                panel(NB - 1 + 2 * j, 0, j * P - P, w_po_v, GR)
                with sp.If(j < 2):
                    sp.wait_ge(s_sC, 2)
                    sp.dma_start(O["new_conv_prompt"][0, 0], state_out[0:HIST, 2, :]).then_inc(s_tail, 16)
                    sp.dma_start(O["new_conv_sample"][0, 0], state_out[0:HIST, 3, :]).then_inc(s_tail, 16)

            def wo_quarter(h, q):
                n = 4 * h + q - 1
                sp.wait_ge(s_wolo, n)
                sp.dma_start(wo_raw[:], w_out_v[:, bass.ds(2 * q - 2, 2), h * 512:(h + 1) * 512]).then_inc(s_wo, 16)

            with sp.Fori(1, KD // 2 + 1) as i:
                for jj in range(2):
                    j = 2 * i + jj - 1
                    panel(NC - 2 + 2 * j, 1, GATE_C - P + j * P)
                    panel(NC - 1 + 2 * j, 0, j * P - P, w_co_v, GR)
                wo_quarter(0, i)
            with sp.Fori(1, 5) as q:
                wo_quarter(1, q)
            sp.wait_ge(s_free[0], (NP + 1) // 2)
            sp.dma_start(g_ffn_b[:], I["g_ffn"][0].partition_broadcast(P)).then_inc(s_rc, 16)
            sp.dma_start(w_r[:, :, 0:G], I["w_rg"][0].rearrange("(p c) g -> p c g", p=P)).then_inc(s_rc, 16)
            sp.dma_start(w_r[:, :, G:NR], I["w_re"][0].rearrange("(p c) g -> p c g", p=P)).then_inc(s_rc, 16)
            sp.dma_start(b_r[:, 0:G], I["b_rg"][0].partition_broadcast(P)).then_inc(s_rc, 16)
            sp.dma_start(b_r[:, G:NR], I["b_re"][0].partition_broadcast(P)).then_inc(s_rc, 16)

            def h2_store(t):
                n = P if t < TILES - 1 else LAST
                sp.wait_ge(s_h2, t + 1)
                sp.dma_start(H2[t * P:t * P + n, :], h2[0:n, t % 2, :]).then_inc(s_h2st[t % 2], 16)

            def store(t):
                n = P if t < TILES - 1 else LAST
                dst = O["y_prompt"][0, t * P:(t + 1) * P, :] if t < TILES - 1 else O["y_sample"][0]
                sp.wait_ge(s_fo, t + 1)
                sp.dma_start(dst, x1[0:n, t, :]).then_inc(s_out, 16)

            gate_v = I["w_gate"][0].rearrange("g e (p c) f -> (g e) p c f", p=P)
            up_v = I["w_up"][0].rearrange("g e (p c) f -> (g e) p c f", p=P)
            down_v = I["w_down"][0].rearrange("g e (p c) d -> (g e) p c d", p=P)
            for n in range(2 * TILES):
                h, t = divmod(n, TILES)
                src, rows = x_rows(t)
                if n >= 2:
                    sp.wait_ge(s_res, n - 1)
                sp.dma_start(xr[0:rows, n % 2, :], src[:, h * 512:(h + 1) * 512]).then_inc(s_xr[n % 2], 16)
                if h == 1 and t >= 2:
                    h2_store(t - 2)
            h2_store(TILES - 2)
            h2_store(TILES - 1)

            def load(e, it, u):
                wait(sp, s_down, it - WB + 1)
                for src, dst in ((gate_v, wgu[u][:, :, 0:F]), (up_v, wgu[u][:, :, F:2 * F]), (down_v, wdn[u][:])):
                    s1 = src[e] if isinstance(e, int) else src[bass.ds(e, 1)].rearrange("a p k f -> (a p) k f")
                    sp.dma_start(dst, s1).then_inc(s_wl[u], 16)

            sp.wait_ge(s_o, 2 * TILES)

            def tab_load(p):
                sp.wait_ge(s_tab0, 1)
                sp.wait_ge(s_tabw, 16 * 2 * TILES)
                wait(sp, s_tabT, p)
                if isinstance(p, int):
                    src = TAB[p * GE * P:(p + 1) * GE * P, :]
                else:
                    src = TAB[bass.ds(p * (GE * P), GE * P), :]
                sp.dma_start(tab[0:GE, :, :], src.rearrange("(e s) c -> e s c", s=P)).then_inc(s_tabl, 16)
            for u in range(WB):
                load(u, u, u)
            tab_load(0)
            sp.dma_start(g_fin_b[:], I["g_final"].partition_broadcast(P)).then_inc(s_gfin, 16)
            with sp.Fori(1, GE // WB) as i:
                for u in range(WB):
                    load(i * WB + u, i * WB + u, u)
            sp.wait_ge(s_np, 1)
            n_pass = sp.value_load(np_i[0:1, 0:1], min_val=1, max_val=PASSES)
            with sp.If(n_pass > 1):
                with sp.Fori(1, n_pass) as p:
                    tab_load(p)
                    with sp.Fori(0, GE // WB) as i:
                        for u in range(WB):
                            load(i * WB + u, p * GE + i * WB + u, u)
            for b in range(2):
                sp.wait_ge(s_ys[b], n_pass * (8 * GE))
            for t in range(TILES):
                n = P if t < TILES - 1 else LAST
                if t >= 2:
                    sp.wait_ge(s_fa, t - 1)
                sp.dma_start(yy[0:n, t % 2], YK.rearrange("(k t) d -> t k d", k=2)[t * P:t * P + n]).then_inc(s_yy[t % 2], 16)
                if t >= 1:
                    store(t - 1)
            store(TILES - 1)
            sp.wait_ge(s_out, 16 * TILES)
            sp.wait_ge(s_tail, 64)

        @block.gpsimd
        def _(pool):
            pool.memset(ident[:], 0.0).then_inc(s_zero, 1)
            pool.memset(tab_init[:], NOWHERE).then_inc(s_ti, 1)
            pool.wait_ge(s_zero, 1)
            pool.affine_select(out=ident[:], in_=ident[:], compare_op=ALU.not_equal, fill=1.0,
                               base=0, pattern=[[-1, P]], channel_multiplier=1).then_inc(s_ident, 1)
            pool.memset(eps_rms[:], RMS_EPS).then_inc(s_eps, 1)
            pool.memset(U[:, :, 0:PH], 0.0)
            pool.memset(V[:, :, 0:HIST], 0.0).then_inc(s_ident, 1)
            pool.memset(eps_ln[:], LN_EPS)
            pool.memset(ln_mean[:], 1.0 / D_CONV).then_inc(s_ident, 1)
            for c in range(16):
                pool.memset(inv_cnt[:, c:c + 1], 1.0 / (c + 1))

            pool.wait_ge(s_hlo, TILES)
            pool.wait_ge(s_free[0], NU // 2)
            pool.wait_ge(s_free[1], NU // 2)
            pool.wait_ge(s_histC, 1)
            done = [0]

            def link(op):
                done[0] += 1
                op.then_inc(s_pool, 1)
                pool.wait_ge(s_pool, done[0])

            pool.wait_ge(s_tabi, 16)
            for g in range(GR):
                w = 2 << g
                src = U[:, g, :]
                for k in range(g + 1):
                    lag, lo = 1 << k, (2 << k) - 1
                    link(pool.tensor_tensor(win[:, k % 2, lo:UW], src[:, lo:UW], src[:, lo - lag:UW - lag], ALU.add))
                    src = win[:, k % 2, :]
                link(pool.tensor_tensor(diff[:, 0:w - 1], src[:, PH:PH + w - 1], inv_cnt[:, 0:w - 1], ALU.mult))
                pool.tensor_scalar(diff[:, w - 1:SEQ], src[:, PH + w - 1:PH + SEQ], 1.0 / w, None, ALU.mult)
                link(pool.tensor_scalar(diff[:, SEQ:T], src[:, UW - DEC:UW], 1.0 / w, None, ALU.mult))
                pool.tensor_tensor(diff[:, 0:SEQ], diff[:, 0:SEQ], U[:, g, PH:PH + SEQ], ALU.subtract)
                link(pool.tensor_tensor(diff[:, SEQ:T], diff[:, SEQ:T], U[:, g, UW - DEC:UW], ALU.subtract))
                link(pool.tensor_copy(d_hi[:, g, :], diff[:]))
                link(pool.tensor_tensor(d_lo[:, g, :], diff[:], d_hi[:, g, :].bitcast(F32), ALU.subtract))
                pool.sem_inc(s_diff, 1)

            pool.wait_ge(s_wolo, 8)
            link(pool.memset(tri[:], 1.0))
            pool.affine_select(out=tri[:], in_=tri[:], compare_op=ALU.is_gt, fill=0.0, base=0,
                               pattern=[[1, P]], channel_multiplier=-1)
            pool.iota(io_i[:], pattern=[[1, GE]], base=0, channel_multiplier=0)
            pool.iota(pay_i[:, :, :, 0], pattern=[[P, TILES], [0, 2]], base=0, channel_multiplier=1)
            link(pool.iota(pay_i[:, :, :, 1], pattern=[[P, TILES], [T, 2]], base=0, channel_multiplier=1))
            pool.tensor_copy(io[:], io_i[:])
            link(pool.tensor_copy(pay[:], pay_i[:]))
            pool.tensor_scalar(thr[:], io[:, 0:PASSES - 1], float(P), float(P), ALU.mult, ALU.add)
            pool.tensor_scalar(ebase[:], io[:], float(P), None, ALU.mult)
            link(pool.tensor_scalar(valid[:], pay[:, TILES - 1, 0, 0:1], float(T), None, ALU.is_lt))
            pool.wait_ge(s_var, len(LN_PIECES))
            pool.memset(ln_mean[:], 1.0).then_inc(s_one, 1)
            pool.wait_ge(s_o, 2 * TILES)
            pool.memset(X[:], 0.0).then_inc(s_ct, 1)
            pool.sem_inc(s_tri, 1)

            pool.wait_ge(s_slot, 1)
            pool.wait_ge(s_tabi, 16)
            for t in range(TILES):
                n = P if t < TILES - 1 else LAST
                for k in range(2):
                    pool.indirect_dma_start(out=TAB, out_offset=bass.IndirectOffsetOnAxis(ap=slot_u[0:n, t, k:k + 1], axis=0),
                                            in_=pay[0:n, t, k, :], in_offset=None).then_inc(s_tabw, 16)
            pool.wait_ge(s_h2st[0], 16 * ((TILES + 1) // 2))
            pool.wait_ge(s_h2st[1], 16 * (TILES // 2))
            pool.wait_ge(s_ct, 1)

            g_bound = pool.alloc_register("g_bound")
            s_bound = pool.alloc_register("s_bound")

            def gather(p, i, u):
                pool.wait_ge(s_gc, p * GE + i * WB + u + 1)
                pool.reg_add(g_bound, pool.zero_reg, T - 1)
                pool.indirect_dma_start(out=X[:, u, :], out_offset=None, in_=H2,
                                        in_offset=bass.IndirectOffsetOnAxis(ap=g_now[:, u:u + 1], axis=0),
                                        bounds_check=g_bound, oob_is_err=False).then_inc(s_xg[u], 16)

            def scatter(p, i, u):
                it, b = p * GE + i * WB + u, u % 2
                pool.wait_ge(s_yA, it + 1)
                pool.wait_ge(s_yD, it + 1)
                pool.reg_add(s_bound, pool.zero_reg, 2 * T - 1)
                pool.indirect_dma_start(out=YK, out_offset=bass.IndirectOffsetOnAxis(ap=s_now[:, b:b + 1], axis=0),
                                        in_=Y[:, b, :], in_offset=None,
                                        bounds_check=s_bound, oob_is_err=False).then_inc(s_ys[b], 16)

            def ahead(p, i, u):
                gather(p, i + (u + 3) // WB, (u + 3) % WB)
                scatter(p, i, u)

            def one(p):
                for u in range(3):
                    gather(p, 0, u)
                for u in range(WB):
                    ahead(p, 0, u)
                with pool.Fori(1, GE // WB - 1) as i:
                    for u in range(WB):
                        ahead(p, i, u)
                gather(p, GE // WB - 1, WB - 1)
                for u in range(WB):
                    scatter(p, GE // WB - 1, u)

            rounds(pool, one)

        @block.scalar
        def _(act):
            def h_hi_copy(t):
                n = P if t < TILES - 1 else LAST
                act.wait_ge(s_xT, t + 1)
                b = 2 * (t % 3)
                for q in range(2):
                    src = ps[:, b + q, :].rearrange("p (k t) -> p k t", k=4)[:, :, 0:n]
                    a = act.activation(h_hi[:, 4 * q:4 * q + 4, t * P:t * P + n], src, ACT.Copy)
                a.then_inc(s_hhi, 1)

            act.wait_ge(s_eps, 1)
            for t in range(TILES):
                n = P if t < TILES - 1 else LAST
                act.wait_ge(s_x[t % 2], 16 * (t // 2 + 1))
                if t >= 1:
                    act.wait_ge(s_sq, t)
                act.activation(squares[0:n, :], xs[0:n, t % 2, :], ACT.Square,
                               accum_out=sumsq[0:n, t:t + 1]).then_inc(s_sq, 1)
                act.wait_ge(s_sq, t + 1)
                act.activation(rstd[0:n, t:t + 1], sumsq[0:n, t:t + 1], ACT.Sqrt, scale=1.0 / D, bias=eps_rms[0:n, :]).then_inc(s_std, 1)
                if t >= 1:
                    h_hi_copy(t - 1)
            h_hi_copy(TILES - 1)

            def split_hi(n, s, K=KD):
                act.wait_ge(s_w[s], 8 * (n - s) + 16)
                act.activation(w_hi[:, s, 0:K], w_raw[:, s, 0:K], ACT.Copy).then_inc(s_whi, 1)

            split_hi(0, 0)
            split_hi(1, 1)

            with act.Fori(0, NU // 2) as i:
                for s in range(2):
                    n = 2 * i + s
                    for c in range(CHUNKS):
                        act.wait_ge(s_mm, 3 * n + c + 1)
                        for (a, pos, w) in runs(c, PH):
                            op = act.activation(U[:, bass.ds(n, 1), pos:pos + w], ps[:, 3 * s + c:3 * s + c + 1, a:a + w], ACT.Copy)
                    op.then_inc(s_free[s], 1)
                    split_hi(n + 2, s)
            with act.Fori(0, GR) as j:
                n = NU + 2 * j
                for c in range(CHUNKS):
                    act.wait_ge(s_mm, 3 * n + c + 1)
                    for (a, pos, w) in runs(c, HIST):
                        op = act.activation(V[:, bass.ds(j, 1), pos:pos + w], ps[:, c:c + 1, a:a + w], ACT.Sigmoid)
                op.then_inc(s_free[0], 1)
                with act.If(j < GR - 1):
                    split_hi(n + 2, 0)
                with act.Else():
                    split_hi(n + 2, 0, GR)
                act.wait_ge(s_mm, 3 * (n + 2))
                split_hi(n + 3, 1)

            act.wait_ge(s_diff, GR)
            for g in range(GR):
                act.wait_ge(s_grp, g + 1)
                for c in range(CHUNKS):
                    op = act.activation(y_hi[:, g, c * CH:(c + 1) * CH], ps[:, 3 * (g % 2) + c, 0:CH], ACT.Copy,
                                        scale=vecs[:, SCALE + g:SCALE + g + 1])
                op.then_inc(s_yhi, 1)
            split_hi(NB + 1, 0, GR)

            def gate(n, jj, j, free0, last=False):
                act.wait_ge(s_free[0], free0)
                for c in range(CHUNKS):
                    act.wait_ge(s_mm, 3 * n + c + 1)
                    op = act.activation(S[:, jj, c * CH:(c + 1) * CH], ps[:, 3 + c, 0:CH], ACT.Sigmoid)
                op.then_inc(s_free[1], 1)

            act.wait_ge(s_tail, 64)
            with act.Fori(0, KD // 2) as i:
                for jj in range(2):
                    j = 2 * i + jj
                    n = NB + 2 * j
                    gate(n, jj, j, NG // 2 + j)
                    split_hi(n + 2, 1)
                    act.wait_ge(s_mm, 3 * (n + 2))
                    split_hi(n + 3, 0, GR)

            for p, (a, w) in enumerate(LN_PIECES):
                act.wait_ge(s_cen, p + 1)
                if p == 0:
                    act.wait_ge(s_free[0], NC // 2 + 1)
                else:
                    act.wait_ge(s_norm, p)
                act.activation(ln_sq[:, :, 0:w], C[:, :, a:a + w], ACT.Square).then_inc(s_csq, 1)
                act.wait_ge(s_var, p + 1)
                act.activation(ln_rstd[:, 0:w], ps[:, 7, 0:w], ACT.Sqrt, bias=eps_ln[:]).then_inc(s_lstd, 1)
            act.wait_ge(s_norm, len(LN_PIECES))
            for g in range(GR):
                if g >= 2:
                    act.wait_ge(s_alo, g - 1)
                for (a, b, w) in C_RUNS:
                    op = act.activation(S[:, g % 2, b:b + w], C[:, g, a:a + w], ACT.Silu,
                                        scale=vecs[:, LN_G + g:LN_G + g + 1], bias=vecs[:, LN_B + g:LN_B + g + 1])
                op.then_inc(s_silu, 1)
                act.wait_ge(s_silu, g + 1)
                act.activation(a_hi[:, g, :], S[:, g % 2, :], ACT.Copy).then_inc(s_ahi, 1)
            act.wait_ge(s_alo, GR)
            with act.Fori(0, KD // 2) as i:
                for jj in range(2):
                    j = 2 * i + jj
                    n = NC + 2 * j
                    gate(n, jj, j, NC // 2 + j)
                    with act.If(n + 2 < NP):
                        split_hi(n + 2, 1)
                        act.wait_ge(s_mm, 3 * (n + 2))
                        split_hi(n + 3, 0, GR)
                act.wait_ge(s_wo, 16 * i + 16)
                act.activation(wo_hi[0][:, bass.ds(2 * i, 2), :], wo_raw[:], ACT.Copy).then_inc(s_wohi, 1)

            act.wait_ge(s_mm, 3 * NP)
            for k in range(KD):
                act.wait_ge(s_free[0], (NP - 1) // 2 - KD + k + 2)
                act.activation(h_hi[:, k, :], M[:, k, :], ACT.Copy).then_inc(s_mhi, 1)
            with act.Fori(0, 4) as q:
                act.wait_ge(s_wo, 16 * q + 80)
                act.activation(wo_hi[1][:, bass.ds(2 * q, 2), :], wo_raw[:], ACT.Copy).then_inc(s_wohi, 1)

            def h2_turned(t):
                n = P if t < TILES - 1 else LAST
                act.wait_ge(s_h2T, t + 1)
                wait(act, s_lg, t - 1)
                for q in range(2):
                    src = ps[:, 4 + q, :].rearrange("p (k t) -> p k t", k=4)[:, :, 0:n]
                    a = act.activation(h2T[:, t % 2, 4 * q:4 * q + 4, 0:n], src, ACT.Copy)
                a.then_inc(s_h2c, 1)

            for t in range(TILES):
                n = P if t < TILES - 1 else LAST
                act.wait_ge(s_res, TILES + t + 1)
                wait(act, s_sq2, t)
                act.activation(squares2[0:n, :], x1[0:n, t, :], ACT.Square, accum_out=sumsq[0:n, t:t + 1]).then_inc(s_sq2, 1)
                act.wait_ge(s_sq2, t + 1)
                act.activation(rstd[0:n, t:t + 1], sumsq[0:n, t:t + 1], ACT.Sqrt, scale=1.0 / D,
                               bias=eps_rms[0:n, :]).then_inc(s_std2, 1)
                if t >= 1:
                    h2_turned(t - 1)
            h2_turned(TILES - 1)
            act.wait_ge(s_ra, 1)
            act.activation(dg[:], dg[:], ACT.Exp).then_inc(s_re, 1)
            act.wait_ge(s_ra, 2)
            act.activation(ex[:], ex[:], ACT.Exp).then_inc(s_re, 1)

            def x_turned(it, b):
                act.wait_ge(s_tx, it + 1)
                wait(act, s_gu, it - 1)
                act.activation(XT[:, b, 0:4, :], ps[:, 0, :], ACT.Copy).then_inc(s_xtA, 1)

            def y_out(it, b, half):
                act.wait_ge(s_down, it + 1)
                wait(act, s_ys[b], 16 * half)
                act.activation(Y[:, b, 0:512], ps[:, 5, :], ACT.Copy).then_inc(s_yA, 1)

            def step(p, i, u):
                it = p * GE + i * WB + u
                b = u % 2
                act.wait_ge(s_gu, it + 1)
                wait(act, s_act, it - 1)
                act.activation(sg[:, b, :], ps[:, 2 + b, 0:F], ACT.Silu).then_inc(s_sg, 1)
                if not (isinstance(i, int) and i == 0 and u == 0):
                    y_out(it - 1, 1 - b, p * (GE // 2) + 2 * i + (u - 1) // 2)
                if not (isinstance(i, int) and i == GE // WB - 1 and u == WB - 1):
                    x_turned(it + 1, 1 - b)

            def one(p):
                x_turned(p * GE, 0)
                groups(act, step, p)
                y_out(p * GE + GE - 1, 1, p * (GE // 2) + GE // 2 - 1)

            rounds(act, one)
            for t in range(TILES):
                n = P if t < TILES - 1 else LAST
                act.wait_ge(s_fa, t + 1)
                wait(act, s_fq, t - 1)
                act.activation(sq3[0:n, t % 2, :], x1[0:n, t, :], ACT.Square, accum_out=sumsq[0:n, t:t + 1]).then_inc(s_fq, 1)
                act.wait_ge(s_fq, t + 1)
                act.activation(rstd[0:n, t:t + 1], sumsq[0:n, t:t + 1], ACT.Sqrt, scale=1.0 / D,
                               bias=eps_rms[0:n, :]).then_inc(s_fs, 1)

        @block.vector
        def _(dve):
            def h_lo_split(t):
                n = P if t < TILES - 1 else LAST
                dve.wait_ge(s_hhi, t + 1)
                b = 2 * (t % 3)
                for q in range(2):
                    src = ps[:, b + q, :].rearrange("p (k t) -> p k t", k=4)[:, :, 0:n]
                    d = dve.tensor_tensor(h_lo[:, 4 * q:4 * q + 4, t * P:t * P + n], src,
                                          h_hi[:, 4 * q:4 * q + 4, t * P:t * P + n].bitcast(F32), ALU.subtract)
                d.then_inc(s_hlo, 1)

            dve.wait_ge(s_const, 16)
            for t in range(TILES):
                n = P if t < TILES - 1 else LAST
                dve.wait_ge(s_std, t + 1)
                dve.reciprocal(rstd[0:n, t:t + 1], rstd[0:n, t:t + 1]).then_inc(s_rstd, 1)
                dve.wait_ge(s_rstd, t + 1)
                if t >= 2:
                    dve.wait_ge(s_xT, t - 1)
                dve.scalar_tensor_tensor(out=xn[0:n, t % 2, :], in0=xs[0:n, t % 2, :], scalar=rstd[0:n, t:t + 1],
                                         in1=g_mix_b[0:n, :], op0=ALU.mult, op1=ALU.mult).then_inc(s_xn, 1)
                if t >= 1:
                    h_lo_split(t - 1)
            h_lo_split(TILES - 1)
            dve.memset(hT[:, 2 * HT:].bitcast(F32), 0.0)

            dve.wait_ge(s_histT, 1)
            dve.wait_ge(s_ident, 2)
            dve.tensor_copy(U[:, :, PH + SEQ:PH + SEQ + PH],
                            ps[:, 6, :].rearrange("p (g t) -> p g t", g=GR)[:, :, 0:PH])
            dve.tensor_copy(w_dw[:], ps[:, 6, :].rearrange("p (g t) -> p g t", g=GR)[:, :, 32:32 + CW])
            dve.tensor_copy(vecs[:], ps[:, 7, 64:64 + 4 * GR])
            dve.tensor_copy(V[:, :, HIST + SEQ:HIST + SEQ + HIST],
                            ps[:, 7, :].rearrange("p (g t) -> p g t", g=GR)[:, :, 0:HIST]).then_inc(s_histC, 1)

            def split_lo(n, s, K=KD):
                dve.wait_ge(s_whi, n + 1)
                dve.tensor_tensor(w_lo[:, s, 0:K], w_raw[:, s, 0:K], w_hi[:, s, 0:K].bitcast(F32),
                                  ALU.subtract).then_inc(s_wlo, 1)

            split_lo(0, 0)
            split_lo(1, 1)
            with dve.Fori(0, NU // 2) as i:
                for s in range(2):
                    split_lo(2 * i + s + 2, s)
            dve.wait_ge(s_sT, 1)
            dve.tensor_copy(state_out[0:PH, 0, :], ps[0:PH, 6, :])
            dve.tensor_copy(state_out[0:PH, 1, :], ps[0:PH, 7, :]).then_inc(s_sC, 1)
            with dve.Fori(0, GR) as j:
                n = NU + 2 * j
                with dve.If(j < GR - 1):
                    split_lo(n + 2, 0)
                with dve.Else():
                    split_lo(n + 2, 0, GR)
                for c in range(CHUNKS):
                    dve.wait_ge(s_mm, 3 * (n + 1) + c + 1)
                    if c == 0:
                        dve.wait_ge(s_free[0], j + NU // 2 + 1)
                    for (a, pos, w) in runs(c, HIST):
                        op = dve.tensor_tensor(V[:, bass.ds(j, 1), pos:pos + w], V[:, bass.ds(j, 1), pos:pos + w],
                                               ps[:, 3 + c:4 + c, a:a + w], ALU.mult)
                op.then_inc(s_free[1], 1)
                split_lo(n + 3, 1)
                dve.wait_ge(s_diff, j + 1)
                dve.wait_ge(s_sT, 1)
                dve.wait_ge(s_free[1], j + NU // 2 + 1)
                cj = C[:, bass.ds(j, 1), :]
                for k in range(A_TAPS):
                    v = V[:, bass.ds(j, 1), k:k + CWID]
                    wk = w_dw[:, bass.ds(j, 1), k]
                    if k == 0:
                        op = dve.tensor_scalar(cj, v, wk, vecs[:, bass.ds(BIAS + j, 1)], ALU.mult, ALU.add)
                    else:
                        dve.wait_ge(s_conv, A_TAPS * j + k)
                        op = dve.scalar_tensor_tensor(out=cj, in0=v, scalar=wk, in1=cj, op0=ALU.mult, op1=ALU.add)
                    op.then_inc(s_conv, 1)

            dve.wait_ge(s_sT, 2)
            dve.tensor_copy(state_out[0:HIST, 2, :], ps[0:HIST, 6, :])
            dve.tensor_copy(state_out[0:HIST, 3, :], ps[0:HIST, 7, :]).then_inc(s_sC, 1)
            for g in range(GR):
                dve.wait_ge(s_yhi, g + 1)
                for c in range(CHUNKS):
                    op = dve.scalar_tensor_tensor(out=y_lo[:, g, c * CH:(c + 1) * CH], in0=ps[:, 3 * (g % 2) + c, 0:CH],
                                                  scalar=vecs[:, SCALE + g:SCALE + g + 1],
                                                  in1=y_hi[:, g, c * CH:(c + 1) * CH].bitcast(F32),
                                                  op0=ALU.mult, op1=ALU.subtract)
                op.then_inc(s_ylo, 1)
            dve.wait_ge(s_ylo, GR)
            dve.sem_inc(s_free[0], 1)
            split_lo(NB + 1, 0, GR)

            def taps(k0, k, base):
                for g in range(GR):
                    dve.wait_ge(s_conv, base + g + 1)
                    dve.scalar_tensor_tensor(out=C[:, g, :], in0=V[:, g, bass.ds(k0 + k, CWID)],
                                             scalar=w_dw[:, g, bass.ds(k0 + k, 1)], in1=C[:, g, :],
                                             op0=ALU.mult, op1=ALU.add).then_inc(s_conv, 1)

            with dve.Fori(0, KD // 2) as i:
                for jj in range(2):
                    j = 2 * i + jj
                    n = NB + 2 * j
                    dve.wait_ge(s_mm, 3 * (n + 1))
                    split_lo(n + 2, 1)
                    for k in range(B_TAPS):
                        taps(A_TAPS + B_TAPS * j, k, A_TAPS * GR + GR * (B_TAPS * j + k - 1))
                    dve.wait_ge(s_free[1], NG // 2 + 1 + j)
                    for c in range(CHUNKS):
                        dve.wait_ge(s_mm, 3 * (n + 1) + c + 1)
                        op = dve.tensor_tensor(M[:, bass.ds(j, 1), c * CH:(c + 1) * CH], S[:, jj:jj + 1, c * CH:(c + 1) * CH],
                                               ps[:, c:c + 1, 0:CH], ALU.mult)
                    op.then_inc(s_free[0], 1)
                    split_lo(n + 3, 0, GR)

            for p, (a, w) in enumerate(LN_PIECES):
                def wide(ap):
                    return ap.unsqueeze(1).to_broadcast((P, GR, w))
                dve.wait_ge(s_mean, p + 1)
                dve.tensor_tensor(C[:, :, a:a + w], C[:, :, a:a + w], wide(ps[:, 6, 0:w]), ALU.subtract).then_inc(s_cen, 1)
                dve.wait_ge(s_lstd, p + 1)
                dve.reciprocal(ln_rstd[:, 0:w], ln_rstd[:, 0:w]).then_inc(s_lrec, 1)
                dve.wait_ge(s_lrec, p + 1)
                dve.tensor_tensor(C[:, :, a:a + w], C[:, :, a:a + w], wide(ln_rstd[:, 0:w]), ALU.mult).then_inc(s_norm, 1)
            for g in range(GR):
                dve.wait_ge(s_ahi, g + 1)
                dve.tensor_tensor(a_lo[:, g, :], S[:, g % 2, :], a_hi[:, g, :].bitcast(F32), ALU.subtract).then_inc(s_alo, 1)
            with dve.Fori(0, KD // 2) as i:
                for jj in range(2):
                    j = 2 * i + jj
                    n = NC + 2 * j
                    with dve.If(n + 2 < NP):
                        split_lo(n + 2, 1)
                    dve.wait_ge(s_free[1], NC // 2 + 1 + j)
                    for c in range(CHUNKS):
                        dve.wait_ge(s_mm, 3 * (n + 1) + c + 1)
                        sc = S[:, jj:jj + 1, c * CH:(c + 1) * CH]
                        dve.tensor_tensor(sc, sc, ps[:, c:c + 1, 0:CH], ALU.mult).then_inc(s_sy, 1)
                    for c in range(CHUNKS):
                        sc = S[:, jj:jj + 1, c * CH:(c + 1) * CH]
                        mc = M[:, bass.ds(j, 1), c * CH:(c + 1) * CH]
                        dve.wait_ge(s_sy, 3 * j + c + 1)
                        op = dve.tensor_tensor(mc, mc, sc, ALU.add)
                    op.then_inc(s_free[0], 1)
                    with dve.If(n + 2 < NP):
                        split_lo(n + 3, 0, GR)
                dve.wait_ge(s_wohi, i + 1)
                dve.tensor_tensor(wo_lo[0][:, bass.ds(2 * i, 2), :], wo_raw[:], wo_hi[0][:, bass.ds(2 * i, 2), :].bitcast(F32),
                                  ALU.subtract).then_inc(s_wolo, 1)
            for k in range(KD):
                dve.wait_ge(s_mhi, k + 1)
                dve.tensor_tensor(h_lo[:, k, :], M[:, k, :], h_hi[:, k, :].bitcast(F32), ALU.subtract).then_inc(s_mlo, 1)
            with dve.Fori(0, 4) as q:
                dve.wait_ge(s_wohi, q + 5)
                dve.tensor_tensor(wo_lo[1][:, bass.ds(2 * q, 2), :], wo_raw[:], wo_hi[1][:, bass.ds(2 * q, 2), :].bitcast(F32),
                                  ALU.subtract).then_inc(s_wolo, 1)
            def h2_tile(t):
                n = P if t < TILES - 1 else LAST
                dve.wait_ge(s_std2, t + 1)
                dve.reciprocal(rstd[0:n, t:t + 1], rstd[0:n, t:t + 1]).then_inc(s_rs2, 1)
                dve.wait_ge(s_rs2, t + 1)
                if t == 0:
                    dve.wait_ge(s_rc, 16 * 5)
                wait(dve, s_h2T, t - 1)
                wait(dve, s_h2st[t % 2], 16 * (t // 2))
                dve.scalar_tensor_tensor(out=h2[0:n, t % 2, :].rearrange("r (c p) -> r p c", c=KD),
                                         in0=x1[0:n, t, :].rearrange("r (p c) -> r p c", c=KD), scalar=rstd[0:n, t:t + 1],
                                         in1=g_ffn_b[0:n, :].rearrange("r (p c) -> r p c", c=KD),
                                         op0=ALU.mult, op1=ALU.mult).then_inc(s_h2, 1)

            for n in range(2 * TILES):
                h, t = divmod(n, TILES)
                rows = P if t < TILES - 1 else LAST
                dve.wait_ge(s_o, n + 1)
                dve.wait_ge(s_xr[n % 2], 16 * (n // 2 + 1))
                dve.tensor_tensor(x1[0:rows, t, h * 512:(h + 1) * 512], xr[0:rows, n % 2, :], ps[0:rows, n % 4, :],
                                  ALU.add).then_inc(s_res, 1)
                if h == 1 and t >= 1:
                    h2_tile(t - 1)
            h2_tile(TILES - 1)

            done = [0]

            def link(op):
                done[0] += 1
                op.then_inc(s_rt, 1)
                dve.wait_ge(s_rt, done[0])

            def b3(ap, n):
                return ap.unsqueeze(2).to_broadcast((P, TILES, n))

            def row(ap, n):
                return ap[:, 0:n].unsqueeze(1).to_broadcast((P, TILES, n))

            dve.wait_ge(s_lg, TILES)
            dve.wait_ge(s_tri, 1)
            link(dve.memset(L[:], 0.0))
            dve.memset(tab[:], 0.0).then_inc(s_tab0, 1)
            lview = ps[:, 6, 0:TILES * NR].rearrange("p (t r) -> p t r", r=NR)
            dve.tensor_tensor(L[:, 0:TILES - 1, :], lview[:, 0:TILES - 1, :],
                              b_r[:].unsqueeze(1).to_broadcast((P, TILES - 1, NR)), ALU.add)
            link(dve.tensor_tensor(L[0:LAST, TILES - 1, :], lview[0:LAST, TILES - 1, :], b_r[0:LAST, :], ALU.add))
            lg = L[:, :, 0:G]
            le = L[:, :, G:NR].rearrange("p t (g e) -> p t g e", g=G)

            def first_max(vals, best, eq, pick, n):
                link(dve.tensor_reduce(best[:], vals, AX.X, ALU.max))
                link(dve.tensor_tensor(eq[:], vals, b3(best[:], n), ALU.is_equal))
                link(dve.scalar_tensor_tensor(out=eq[:], in0=eq[:], scalar=-2.0 * n, in1=row(io, n),
                                              op0=ALU.mult, op1=ALU.add))
                link(dve.tensor_reduce(gmin[:], eq[:], AX.X, ALU.min))
                link(dve.tensor_tensor(pick[:], eq[:], b3(gmin[:], n), ALU.is_equal))

            first_max(lg, gmax, tg, og, G)
            dve.tensor_tensor(dg[:], lg, b3(gmax[:], G), ALU.subtract).then_inc(s_ra, 1)
            link(dve.tensor_tensor(tmp32[:], le, og[:].unsqueeze(3).to_broadcast((P, TILES, G, E)), ALU.mult))
            link(dve.tensor_reduce(les[:], tmp32[:].rearrange("p t g e -> p t e g"), AX.X, ALU.add))
            first_max(les[:], m1, te, oe[0], E)
            link(dve.scalar_tensor_tensor(out=les[:], in0=oe[0][:], scalar=-1.0e30, in1=les[:], op0=ALU.mult, op1=ALU.add))
            first_max(les[:], m2, te, oe[1], E)
            dve.tensor_tensor(ex[:], m2[:], m1[:], ALU.subtract).then_inc(s_ra, 1)
            for k in range(2):
                link(dve.tensor_tensor(Ek[k][:], og[:].unsqueeze(3).to_broadcast((P, TILES, G, E)),
                                       oe[k][:].unsqueeze(2).to_broadcast((P, TILES, G, E)), ALU.mult))
            flat = [e[:].rearrange("p t g e -> p t (g e)") for e in Ek]
            link(dve.tensor_tensor(A[:], flat[0], flat[1], ALU.add))
            link(dve.tensor_scalar(A[:, TILES - 1, :], A[:, TILES - 1, :], valid[:], None, ALU.mult))
            link(dve.memset(Acum[:, 0, :], 0.0))
            for t in range(TILES):
                link(dve.tensor_tensor(Acum[:, t + 1, :], Acum[:, t, :], A[:, t, :], ALU.add))
            dve.sem_inc(s_cum, 1)
            dve.wait_ge(s_re, 2)
            link(dve.tensor_reduce(zsum[:], dg[:], AX.X, ALU.add))
            link(dve.tensor_scalar(den[:], ex[:], 1.0, None, ALU.add))
            link(dve.tensor_tensor(den[:], den[:], zsum[:], ALU.mult))
            link(dve.reciprocal(wts[:, :, 0], den[:]))
            link(dve.tensor_tensor(wts[:, :, 1], wts[:, :, 0], ex[:], ALU.mult))
            dve.wait_ge(s_rk, 1)
            link(dve.tensor_reduce(nmax[:], ps[:, 5, 0:GE], AX.X, ALU.max))
            link(dve.tensor_tensor(ge8[:, 0, :], nmax[:].to_broadcast((P, PASSES - 1)), thr[:], ALU.is_gt))
            link(dve.tensor_reduce(np_f[:], ge8[:, 0, :], AX.X, ALU.add))
            dve.tensor_scalar(np_i[:], np_f[:], 1.0, None, ALU.add).then_inc(s_np, 1)
            ranks = ps[:, 7, 0:TILES * GE].rearrange("p (t e) -> p t e", e=GE)
            tmpf = tmp32[:].rearrange("p t g e -> p t (g e)")
            for k in range(2):
                link(dve.tensor_tensor(tmpf, flat[k], ranks, ALU.mult))
                link(dve.tensor_reduce(rank[:, :, k], tmpf, AX.X, ALU.add))
                link(dve.tensor_tensor(tmpf, flat[k], row(ebase, GE), ALU.mult))
                link(dve.tensor_reduce(eb[:, :, k], tmpf, AX.X, ALU.add))
            r18 = rank[:].rearrange("p t k -> p (t k)")
            link(dve.tensor_tensor(ge8[:], r18.unsqueeze(2).to_broadcast((P, 2 * TILES, PASSES - 1)),
                                   thr[:].unsqueeze(1).to_broadcast((P, 2 * TILES, PASSES - 1)), ALU.is_ge))
            link(dve.tensor_reduce(rnd[:].rearrange("p t k -> p (t k)"), ge8[:], AX.X, ALU.add))
            link(dve.scalar_tensor_tensor(out=slot_f[:], in0=rnd[:], scalar=float(GE * P - P), in1=rank[:],
                                          op0=ALU.mult, op1=ALU.add))
            dve.tensor_tensor(slot_u[:], slot_f[:], eb[:], ALU.add).then_inc(s_slot, 1)

            def x_turned(it, b):
                dve.wait_ge(s_tx, it + 1)
                wait(dve, s_gu, it - 1)
                dve.tensor_copy(XT[:, b, 4:8, :], ps[:, 1, :]).then_inc(s_xtD, 1)

            def column(ap, e):
                return ap[:, e:e + 1] if isinstance(e, int) else ap[:, bass.ds(e, 1)]

            def g_column(e, u):
                dve.tensor_copy(g_now[:, u:u + 1], column(g_idx, e)).then_inc(s_gc, 1)

            def y_out(it, b, half, e):
                dve.wait_ge(s_down, it + 1)
                wait(dve, s_ys[b], 16 * half)
                dve.tensor_copy(s_now[:, b:b + 1], column(s_idx, e))
                dve.tensor_copy(Y[:, b, 512:1024], ps[:, 6, :]).then_inc(s_yD, 1)

            def step(p, i, u):
                it = p * GE + i * WB + u
                b = u % 2
                if not (isinstance(i, int) and i == GE // WB - 1 and u > 0):
                    g_column(i * WB + u + 3, (u + 3) % WB)
                dve.wait_ge(s_sg, it + 1)
                wait(dve, s_ta, it - 1)
                dve.tensor_tensor(act_[:, b, :].rearrange("r (c p) -> r p c", c=KF),
                                  sg[:, b, :].rearrange("r (p c) -> r p c", c=KF),
                                  ps[:, 2 + b, F:2 * F].rearrange("r (p c) -> r p c", c=KF), ALU.mult).then_inc(s_act, 1)
                if not (isinstance(i, int) and i == 0 and u == 0):
                    y_out(it - 1, 1 - b, p * (GE // 2) + 2 * i + (u - 1) // 2, i * WB + u - 1)
                if not (isinstance(i, int) and i == GE // WB - 1 and u == WB - 1):
                    x_turned(it + 1, 1 - b)
                dve.wait_ge(s_ta, it + 1)
                wait(dve, s_down, it - 1)
                dve.tensor_copy(AT[:, b, :, :], ps[:, 4, 0:KF * P].rearrange("p (c t) -> p c t", c=KF)).then_inc(s_at, 1)

            def one(p):
                dve.wait_ge(s_tabT, p + 1)
                if not isinstance(p, int):
                    for b in range(2):
                        dve.wait_ge(s_ys[b], p * (8 * GE))
                dve.tensor_copy(g_idx[:], ps[:, 7, 0:GE])
                dve.tensor_copy(s_idx[:], ps[:, 7, P:P + GE]).then_inc(s_ix, 1)
                dve.wait_ge(s_ix, p + 1)
                for u in range(3):
                    g_column(u, u)
                x_turned(p * GE, 0)
                groups(dve, step, p)
                y_out(p * GE + GE - 1, 1, p * (GE // 2) + GE // 2 - 1, GE - 1)

            rounds(dve, one)

            def final(t):
                n = P if t < TILES - 1 else LAST
                dve.wait_ge(s_fs, t + 1)
                dve.reciprocal(rstd[0:n, t:t + 1], rstd[0:n, t:t + 1]).then_inc(s_fr, 1)
                dve.wait_ge(s_fr, t + 1)
                dve.scalar_tensor_tensor(out=x1[0:n, t, :], in0=x1[0:n, t, :], scalar=rstd[0:n, t:t + 1],
                                         in1=g_fin_b[0:n, :], op0=ALU.mult, op1=ALU.mult).then_inc(s_fo, 1)

            dve.wait_ge(s_gfin, 16)
            for t in range(TILES):
                n = P if t < TILES - 1 else LAST
                dve.wait_ge(s_yy[t % 2], 16 * (t // 2 + 1))
                for k in range(2):
                    wait(dve, s_f1, t + k)
                    dve.scalar_tensor_tensor(out=x1[0:n, t, :], in0=yy[0:n, t % 2, k, :], scalar=wts[0:n, t, k:k + 1],
                                             in1=x1[0:n, t, :], op0=ALU.mult, op1=ALU.add).then_inc((s_f1, s_fa)[k], 1)
                if t >= 1:
                    final(t - 1)
            final(TILES - 1)

        @block.tensor
        def _(pe):
            pe.wait_ge(s_ident, 1)
            for t in range(TILES):
                n = P if t < TILES - 1 else LAST
                pe.wait_ge(s_xn, t + 1)
                if t >= 3:
                    pe.wait_ge(s_hlo, t - 2)
                for k in range(KD):
                    m = pe.transpose(ps[:, 2 * (t % 3) + k // 4, (k % 4) * P:(k % 4) * P + n],
                                     xn[0:n, t % 2, k * P:(k + 1) * P], ident[0:n, 0:n])
                m.then_inc(s_xT, 1)
            pe.wait_ge(s_hist, 16 * 7)
            for g in range(GR):
                pe.transpose(ps[:, 6, g * P:g * P + PH], hist_in[0:PH, 0, g * P:(g + 1) * P], ident[0:PH, 0:PH])
            for g in range(GR):
                pe.transpose(ps[:, 6, g * P + 32:g * P + 32 + CW], hist_in[:, 2, g * P:(g + 1) * P], ident[0:CW, 0:CW])
            pe.transpose(ps[:, 7, 64:64 + 4 * GR], vec_in[:], ident[0:4 * GR, 0:4 * GR])
            for g in range(GR):
                m = pe.transpose(ps[:, 7, g * P:g * P + HIST], hist_in[0:HIST, 1, g * P:(g + 1) * P], ident[0:HIST, 0:HIST])
            m.then_inc(s_histT, 1)
            pe.wait_ge(s_hlo, TILES)

            def product(bank, w, s, hi, lo, K, c):
                for k in range(K):
                    for q, (a, r) in enumerate(((w_hi, hi), (w_hi, lo), (w_lo, hi))):
                        m = pe.matmul(ps[:, bank, 0:CH], a[:, s, w + k, :], r[:, w + k, c * CH:(c + 1) * CH],
                                      start=(k == 0 and q == 0), stop=(k == K - 1 and q == 2))
                return m

            def panel(n, half, s, hi, lo, K):
                pe.wait_ge(s_whi, n + 1)
                pe.wait_ge(s_wlo, n + 1)
                if half is not None:
                    pe.wait_ge(s_free[s], half)
                for c in range(CHUNKS):
                    product(3 * s + c, 0, s, hi, lo, K, c).then_inc(s_mm, 1)

            def tails(src, n, starts):
                for q in range(2):
                    for g in range(GR):
                        m = pe.transpose(ps[0:n, 6 + q, g * P:(g + 1) * P], src[:, g, starts[q]:starts[q] + n], ident[:])
                m.then_inc(s_sT, 1)

            for s in range(2):
                panel(s, None, s, h_hi, h_lo, KD)
            for s in range(2):
                panel(2 + s, 1, s, h_hi, h_lo, KD)
            pe.wait_ge(s_free[0], NU // 2)
            pe.wait_ge(s_free[1], NU // 2)
            pe.wait_ge(s_histC, 1)
            tails(U, PH, (SEQ, UW - PH))
            with pe.Fori(NU // 2, NG // 2) as i:
                for s in range(2):
                    panel(2 * i + s, i, s, h_hi, h_lo, KD)
            pe.wait_ge(s_free[0], NG // 2)
            pe.wait_ge(s_free[1], NG // 2)
            pe.wait_ge(s_sC, 1)
            tails(V, HIST, (SEQ, VW - HIST))
            pe.wait_ge(s_whi, NG + 1)
            pe.wait_ge(s_wlo, NG + 1)
            for g in range(GR):
                pe.wait_ge(s_diff, g + 1)
                if g >= 2:
                    pe.wait_ge(s_ylo, g - 1)
                for c in range(CHUNKS):
                    m = product(3 * (g % 2) + c, g, 0, d_hi, d_lo, 1, c)
                m.then_inc(s_grp, 1)
            pe.sem_inc(s_mm, 3)
            pe.wait_ge(s_ylo, GR)
            with pe.Fori(0, KD) as j:
                panel(NB + 2 * j, NG // 2 + j, 1, h_hi, h_lo, KD)
                panel(NB + 1 + 2 * j, NG // 2 + 1 + j, 0, y_hi, y_lo, GR)
            pe.wait_ge(s_conv, CW * GR)
            for p, (a, w) in enumerate(LN_PIECES):
                for q, (src, s_wait, s_done) in enumerate(((C, s_norm, s_mean), (ln_sq, s_csq, s_var))):
                    if q or p:
                        pe.wait_ge(s_wait, p + q)
                    for g in range(GR):
                        m = pe.matmul(ps[:, 6 + q, 0:w], ln_mean[:], src[:, g, a:a + w] if q == 0 else src[:, g, 0:w],
                                      start=(g == 0), stop=(g == GR - 1))
                    m.then_inc(s_done, 1)
            pe.wait_ge(s_alo, GR)
            with pe.Fori(0, KD) as j:
                panel(NC + 2 * j, NC // 2 + j, 1, h_hi, h_lo, KD)
                panel(NC + 1 + 2 * j, NC // 2 + 1 + j, 0, a_hi, a_lo, GR)
            pe.wait_ge(s_mhi, KD)
            pe.wait_ge(s_mlo, KD)
            pe.wait_ge(s_free[1], NP // 2)

            def h2_turn(t):
                n = P if t < TILES - 1 else LAST
                pe.wait_ge(s_h2, t + 1)
                wait(pe, s_h2c, t)
                for c in range(KD):
                    m = pe.transpose(ps[:, 4 + c // 4, (c % 4) * P:(c % 4) * P + n], h2[0:n, t % 2, c * P:(c + 1) * P],
                                     ident[0:n, 0:n])
                m.then_inc(s_h2T, 1)

            def logits(t):
                n = P if t < TILES - 1 else LAST
                pe.wait_ge(s_h2c, t + 1)
                for c in range(KD):
                    m = pe.matmul(ps[0:n, 6, t * NR:(t + 1) * NR], h2T[:, t % 2, c, 0:n], w_r[:, c, :],
                                  start=(c == 0), stop=(c == KD - 1))
                m.then_inc(s_lg, 1)

            for n in range(2 * TILES):
                h, t = divmod(n, TILES)
                if t == 0:
                    pe.wait_ge(s_wohi, 4 * h + 4)
                    pe.wait_ge(s_wolo, 4 * h + 4)
                if n >= 4:
                    pe.wait_ge(s_res, n - 3)
                for k in range(KD):
                    o = k * T + t * P
                    hi, lo = hT[:, o:o + P], hT[:, HT + o:HT + o + P]
                    for q, (a, w) in enumerate(((hi, wo_hi), (lo, wo_hi), (hi, wo_lo))):
                        m = pe.matmul(ps[:, n % 4, :], a, w[h][:, k, :], start=(k == 0 and q == 0),
                                      stop=(k == KD - 1 and q == 2))
                m.then_inc(s_o, 1)
                if h == 1 and t >= 1:
                    h2_turn(t - 1)
                if h == 1 and t >= 2:
                    logits(t - 2)
            logits(TILES - 2)
            h2_turn(TILES - 1)
            logits(TILES - 1)
            pe.wait_ge(s_cum, 1)
            pe.wait_ge(s_one, 1)
            aflat = A[:].rearrange("p t e -> p (t e)")
            pe.matmul(ps[:, 7, 0:TILES * GE], tri[:], aflat, start=True, stop=False)
            pe.matmul(ps[:, 7, 0:TILES * GE], ln_mean[:], Acum[:, 0:TILES, :].rearrange("p t e -> p (t e)"),
                      start=False, stop=True)
            pe.matmul(ps[:, 5, 0:GE], ln_mean[:], Acum[:, TILES, :], start=True, stop=True).then_inc(s_rk, 1)

            def x_turn(it, u, quarter):
                pe.wait_ge(s_xg[u], 16 * (quarter + 1))
                wait(pe, s_xtA, it)
                wait(pe, s_xtD, it)
                for c in range(KD):
                    m = pe.transpose(ps[:, c // 4, (c % 4) * P:(c % 4 + 1) * P], X[:, u, c * P:(c + 1) * P], ident[:])
                m.then_inc(s_tx, 1)

            def down(it, u):
                pe.wait_ge(s_at, it + 1)
                wait(pe, s_yA, it)
                wait(pe, s_yD, it)
                for h in range(2):
                    for c in range(KF):
                        m = pe.matmul(ps[:, 5 + h, :], AT[:, u % 2, c, :], wdn[u][:, c, h * 512:(h + 1) * 512],
                                      start=(c == 0), stop=(c == KF - 1))
                m.then_inc(s_down, 1)

            def step(p, i, u):
                it = p * GE + i * WB + u
                b = u % 2
                pe.wait_ge(s_xtA, it + 1)
                pe.wait_ge(s_xtD, it + 1)
                wait(pe, s_act, it - 1)
                pe.wait_ge(s_wl[u], 48 * (p * (GE // WB) + i + 1))
                for c in range(KD):
                    m = pe.matmul(ps[:, 2 + b, :], XT[:, b, c, :], wgu[u][:, c, :], start=(c == 0), stop=(c == KD - 1))
                m.then_inc(s_gu, 1)
                if not (isinstance(i, int) and i == 0 and u == 0):
                    down(it - 1, (u - 1) % WB)
                if not (isinstance(i, int) and i == GE // WB - 1 and u == WB - 1):
                    x_turn(it + 1, (u + 1) % WB, p * (GE // WB) + i + (u + 1) // WB)
                pe.wait_ge(s_act, it + 1)
                wait(pe, s_at, it)
                for c in range(KF):
                    m = pe.transpose(ps[:, 4, c * P:(c + 1) * P], act_[:, b, c * P:(c + 1) * P], ident[:])
                m.then_inc(s_ta, 1)

            def one(p):
                pe.wait_ge(s_tabl, 16 * (p + 1))
                if isinstance(p, int):
                    pe.wait_ge(s_slot, 1)
                else:
                    pe.wait_ge(s_ix, p)
                for q in range(2):
                    m = pe.transpose(ps[:, 7, q * P:(q + 1) * P], tab[:, :, q], ident[:])
                m.then_inc(s_tabT, 1)
                x_turn(p * GE, 0, p * (GE // WB))
                groups(pe, step, p)
                down(p * GE + GE - 1, WB - 1)

            rounds(pe, one)


_INS = ['x_prompt', 'x_sample', 'state_pool', 'state_conv', 'g_mix', 'w_in', 'w_pool_grp', 'pool_scale',
        'w_pool_out', 'w_dw', 'b_dw', 'ln_g', 'ln_b', 'w_conv_out', 'w_out', 'g_ffn', 'w_rg', 'b_rg', 'w_re',
        'b_re', 'w_gate', 'w_up', 'w_down', 'g_final']
_OUTS = [('y_prompt', (1, SEQ, D)), ('y_sample', (1, DEC, D)), ('new_pool_prompt', (1, 1, PH, D_POOL)),
         ('new_conv_prompt', (1, 1, HIST, D_CONV)), ('new_pool_sample', (1, 1, PH, D_POOL)),
         ('new_conv_sample', (1, 1, HIST, D_CONV))]


def kernel(**inputs):
    import numpy as _np
    import concourse.bacc as _bacc
    from concourse.bass_utils import run_bass_kernel_spmd as _run

    nc = _bacc.Bacc("TRN2", target_bir_lowering=False, num_devices=1)
    arrays, ins, outs = {}, {}, {}
    for name in _INS:
        a = _np.ascontiguousarray(inputs[name])
        arrays[f"in_{name}"] = a
        ins[name] = nc.dram_tensor(f"in_{name}", a.shape, mybir.dt.from_np(a.dtype), kind="ExternalInput").ap()
    for name, shape in _OUTS:
        outs[name] = nc.dram_tensor(f"out_{name}", shape, F32, kind="ExternalOutput").ap()
    build(nc, ins, outs)
    r = _run(nc, [arrays], core_ids=[0])
    return tuple(r.results[0][f"out_{name}"] for name, _ in _OUTS)
```

```python
from contextlib import ExitStack

import concourse.bass as bass
from concourse import mybir

ACT = mybir.ActivationFunctionType
ALU = mybir.AluOpType
AX = mybir.AxisListType
F32 = mybir.dt.float32
F32R = mybir.dt.float32r
BF16 = mybir.dt.bfloat16
U32 = mybir.dt.uint32
I32 = mybir.dt.int32

P = 128
D = 1024
KD = D // P
SEQ = 1024
DEC = 32
LN_W = 272
T = SEQ + DEC
TILES = (T + P - 1) // P
LAST = T - (TILES - 1) * P
CH = T // 3
CHUNKS = 3
D_POOL = 512
D_CONV = 512
GR = D_POOL // P
PH = 15
CW = 31
HIST = CW - 1
UW = PH + SEQ + PH + DEC
VW = HIST + SEQ + HIST + DEC
CWID = SEQ + HIST + DEC
G = 4
E = 8
GE = G * E
F = 256
KF = F // P
NR = G + GE
CAP = 104
PASSES = (T + CAP - 1) // CAP
NOWHERE = 1.0e6
WB = 4
RMS_EPS = 1e-6
LN_EPS = 1e-5


def build(nc, I, O):
    with ExitStack() as ctx:
        def sem(name):
            return ctx.enter_context(nc.semaphore(name))

        cursor = [16512]

        def region(nbytes):
            o = cursor[0]
            cursor[0] += (nbytes + 31) // 32 * 32
            assert cursor[0] <= 229344, cursor
            return o

        def at(name, shape, dt, offset):
            return nc.alloc_sbuf_tensor_at(name, shape, dt, offset=offset)

        def small(name, shape, dt=F32):
            n = 4
            for s in shape[1:]:
                n *= s
            return at(name, shape, dt, region(n))

        HT = KD * T
        r_h = region((2 * HT + P - DEC) * 4)
        r_m = region(max(KD * T, TILES * D) * 4)
        r_uv = region(GR * (UW + VW) * 4)
        r_yp = region(2 * GR * T * 4)
        r_w = region(6 * KD * P * 4)
        r_s = region(2 * T * 4)
        r_wo = region(KD * P * 4)

        hT = at("hT", [P, 2 * HT + P - DEC], F32R, r_h)
        h_hi = hT[:, 0:HT].rearrange("p (k t) -> p k t", k=KD)
        h_lo = hT[:, HT:2 * HT].rearrange("p (k t) -> p k t", k=KD)

        U = at("U", [P, GR, UW], F32, r_uv)
        V = at("V", [P, GR, VW], F32, r_uv + GR * UW * 4)
        C = at("C", [P, GR, CWID], F32, r_uv)

        xs = at("xs", [P, 2, D], F32, r_yp)
        xn = at("xn", [P, 2, D], F32, r_yp + 8 * D)
        g_mix_b = at("g_mix_b", [P, D], F32, r_yp + 16 * D)
        squares = at("squares", [P, D], F32, r_s)

        w_raw = at("w_raw", [P, 2, KD, P], F32, r_w)
        w_hi = at("w_hi", [P, 2, KD, P], F32R, r_w + 2 * KD * P * 4)
        w_lo = at("w_lo", [P, 2, KD, P], F32R, r_w + 4 * KD * P * 4)

        hist_in = at("hist_in", [CW, 3, D_CONV], F32, r_m)
        vec_in = at("vec_in", [4 * GR, P], F32, r_m + 3 * D_CONV * 4)
        win = at("win", [P, 2, UW], F32, r_yp)
        diff = at("diff", [P, T], F32, r_yp + (8 * UW + 31) // 32 * 32)
        d_hi = at("d_hi", [P, GR, T], F32R, r_m)
        d_lo = at("d_lo", [P, GR, T], F32R, r_m + GR * T * 4)
        y_hi = at("y_hi", [P, GR, T], F32R, r_yp)
        y_lo = at("y_lo", [P, GR, T], F32R, r_yp + GR * T * 4)
        a_hi = at("a_hi", [P, GR, T], F32R, r_uv + GR * UW * 4)
        a_lo = at("a_lo", [P, GR, CWID], F32R, r_uv)
        M = at("M", [P, KD, T], F32, r_m)
        x1 = at("x1", [P, TILES, D], F32, r_m)
        S = at("S", [P, 2, T], F32, r_s)
        r_v = r_uv + GR * UW * 4
        ln_sq = at("ln_sq", [P, GR, LN_W], F32, r_v)
        ln_rstd = at("ln_rstd", [P, LN_W], F32, r_v + (GR * VW - LN_W) * 4)
        xr = at("xr", [P, 2, 512], F32, r_s)
        wo_raw = at("wo_raw", [P, 2, 512], F32, r_wo)
        wo_hi = [at("wo_hi0", [P, KD, 512], F32R, r_yp), at("wo_hi1", [P, KD, 512], F32R, r_uv)]
        wo_lo = [at("wo_lo0", [P, KD, 512], F32R, r_yp + KD * 2048), at("wo_lo1", [P, KD, 512], F32R, r_uv + KD * 2048)]
        state_out = at("state_out", [32, 4, D_CONV], F32, r_s)

        ident = small("ident", [P, P])
        w_dw = small("w_dw", [P, GR, CW])
        vecs = small("vecs", [P, 4 * GR])
        ln_mean = small("ln_mean", [P, P])
        inv_cnt = small("inv_cnt", [P, 16])
        eps_ln = small("eps_ln", [P, 1])
        sumsq = small("sumsq", [P, TILES])
        rstd = small("rstd", [P, TILES])
        eps_rms = small("eps_rms", [P, 1])

        h2 = at("h2", [P, 2, D], F32, r_w)
        h2T = at("h2T", [P, 2, KD, P], F32, r_w + 8192)
        g_ffn_b = at("g_ffn_b", [P, D], F32, r_w + 16384)
        w_r = at("w_r", [P, KD, NR], F32, r_w + 20480)
        b_r = at("b_r", [P, NR], F32, r_w + 21632)
        L = at("L", [P, TILES, NR], F32, r_w + 21792)
        squares2 = at("squares2", [P, D], F32, r_s + 4096)
        cur = [r_wo]

        def const(name, shape, dt=F32, start=None):
            if start is not None:
                cur[0] = start
            n = 2 if dt is BF16 else 4
            for v in shape[1:]:
                n *= v
            o = cur[0]
            cur[0] += (n + 31) // 32 * 32
            return at(name, shape, dt, o)

        tri = const("tri", [P, P], start=r_wo)
        io_i = const("io_i", [P, GE], I32)
        io = const("io", [P, GE])
        thr = const("thr", [P, PASSES - 1])
        tri_b = const("tri_b", [P, P], BF16)
        one_b = const("one_b", [P, P], BF16)
        row_i = const("row_i", [P, TILES, 2], I32)
        row_f = const("row_f", [P, TILES, 2])
        row_hi = const("row_hi", [P, TILES, 2], BF16)
        row_lo = const("row_lo", [P, TILES, 2])
        slot_i = const("slot_i", [P, CAP], I32)
        slot_f = const("slot_f", [P, CAP])
        valid = const("valid", [P, 1])
        assert cur[0] <= r_wo + 4096
        N9 = [P, TILES]
        gmax = const("gmax", N9, start=r_w + 8192)
        gmin = const("gmin", N9)
        zsum = const("zsum", N9)
        m1 = const("m1", N9)
        m2 = const("m2", N9)
        i1 = const("i1", N9)
        ex = const("ex", N9)
        den = const("den", N9)
        rank = const("rank", [P, TILES, 2])
        tg = const("tg", [P, TILES, G])
        og = const("og", [P, TILES, G])
        dg = const("dg", [P, TILES, G])
        les = const("les", [P, TILES, E])
        te = const("te", [P, TILES, E])
        oe = [const("oe0", [P, TILES, E]), const("oe1", [P, TILES, E])]
        ge8 = const("ge8", [P, PASSES - 1])
        nmax = const("nmax", [P, 1])
        np_f = const("np_f", [P, 1])
        assert cur[0] <= r_w + 16384
        Ek = [const("Ek0", [P, TILES, G, E], start=r_s), const("Ek1", [P, TILES, G, E])]
        A = const("A", [P, TILES, GE], BF16)
        tmp32 = const("tmp32", [P, TILES, G, E])
        slot_rows = const("slot_rows", [P, 2, TILES, 2, GE], BF16)
        assert cur[0] <= r_s + 8448
        w_off = [r_yp, r_h, r_h + 24576, r_uv]
        wgu = [at(f"wgu{u}", [P, 2, KD, F], F32, w_off[u]) for u in range(WB)]
        wdn = [at(f"wdn{u}", [P, KF, D], F32, w_off[u] + 16384) for u in range(WB)]
        X = at("X", [P, 4, D], F32, r_h + 49152)
        Y = at("Y", [P, 2, D], F32, r_uv + 24576)
        XT = at("XT", [P, 2, KD, P], F32, r_yp + 24576)
        where = at("where", [P, TILES, 2, CAP], BF16, r_yp + 24576)
        sg = at("sg", [P, 2, KF, P], F32, r_w)
        AT = at("AT", [P, 2, KF, P], F32, r_w + 2048)
        yy = at("yy", [P, TILES, 2, D], F32, r_uv)
        assert r_uv + TILES * 2 * D * 4 <= r_w + 24576
        wts = const("wts", [P, TILES, 2], start=r_h + 65536)
        g_idx = const("g_idx", [P, GE])
        wrap = const("wrap", [P, GE])
        found = const("found", [P, GE])
        s_idx = const("s_idx", [P, GE])
        g_now = const("g_now", [P, 4], U32)
        s_now = const("s_now", [P, 2], U32)
        np_i = const("np_i", [P, 1], I32)
        assert cur[0] <= r_m
        g_fin_b = at("g_fin_b", [P, D], F32, r_w + 16384)
        sq3 = at("sq3", [P, 2, D], F32, r_s)

        H2 = nc.dram_tensor("H2", (T, D), F32, kind="Internal").ap()
        YK = nc.dram_tensor("YK", (2 * T, D), F32, kind="Internal").ap()

        ps = ctx.enter_context(nc.psum_tensor("ps", [P, 8, 512], F32))

        s_const = sem("s_const")
        s_x = [sem("s_x0"), sem("s_x1")]
        s_w = [sem("s_w0"), sem("s_w1")]
        s_hist = sem("s_hist")
        s_ident = sem("s_ident")
        s_eps = sem("s_eps")
        s_zero = sem("s_zero")
        s_std = sem("s_std")
        s_sq = sem("s_sq")
        s_rstd = sem("s_rstd")
        s_xn = sem("s_xn")
        s_xT = sem("s_xT")
        s_hhi = sem("s_hhi")
        s_hlo = sem("s_hlo")
        s_histT = sem("s_histT")
        s_histC = sem("s_histC")
        s_whi = sem("s_whi")
        s_wlo = sem("s_wlo")
        s_mm = sem("s_mm")
        s_free = [sem("s_free0"), sem("s_free1")]
        s_sT = sem("s_sT")
        s_sC = sem("s_sC")
        s_out = sem("s_out")
        s_tail = sem("s_tail")
        s_pool = sem("s_pool")
        s_inv = sem("s_inv")
        s_diff = sem("s_diff")
        s_conv = sem("s_conv")
        s_grp = sem("s_grp")
        s_yhi = sem("s_yhi")
        s_ylo = sem("s_ylo")
        s_mean = sem("s_mean")
        s_cen = sem("s_cen")
        s_csq = sem("s_csq")
        s_var = sem("s_var")
        s_lstd = sem("s_lstd")
        s_lrec = sem("s_lrec")
        s_norm = sem("s_norm")
        s_silu = sem("s_silu")
        s_ahi = sem("s_ahi")
        s_alo = sem("s_alo")
        s_sy = sem("s_sy")
        s_mhi = sem("s_mhi")
        s_mlo = sem("s_mlo")
        s_wo = sem("s_wo")
        s_wohi = sem("s_wohi")
        s_wolo = sem("s_wolo")
        s_o = sem("s_o")
        s_xr = [sem("s_xr0"), sem("s_xr1")]
        s_res = sem("s_res")
        s_rc = sem("s_rc")
        s_sq2 = sem("s_sq2")
        s_std2 = sem("s_std2")
        s_rs2 = sem("s_rs2")
        s_h2 = sem("s_h2")
        s_h2st = [sem("s_h2st0"), sem("s_h2st1")]
        s_h2T = sem("s_h2T")
        s_h2c = sem("s_h2c")
        s_lg = sem("s_lg")
        s_rt = sem("s_rt")
        s_ra = sem("s_ra")
        s_re = sem("s_re")
        s_cum = sem("s_cum")
        s_rk = sem("s_rk")
        s_np = sem("s_np")
        s_where = sem("s_where")
        s_rows = sem("s_rows")
        s_prep = sem("s_prep")
        s_tx = sem("s_tx")
        s_xtA = sem("s_xtA")
        s_xtD = sem("s_xtD")
        s_gu = sem("s_gu")
        s_sg = sem("s_sg")
        s_act = sem("s_act")
        s_down = sem("s_down")
        s_yA = sem("s_yA")
        s_yD = sem("s_yD")
        s_gc = sem("s_gc")
        s_f1 = sem("s_f1")
        s_gfin = sem("s_gfin")
        s_fq = sem("s_fq")
        s_fs = sem("s_fs")
        s_fr = sem("s_fr")
        s_fa = sem("s_fa")
        s_fo = sem("s_fo")
        s_tri = sem("s_tri")
        s_ct = sem("s_ct")
        s_wl = [sem(f"s_wl{u}") for u in range(WB)]
        s_xg = [sem(f"s_xg{u}") for u in range(4)]
        s_ys = [sem("s_ys0"), sem("s_ys1")]
        s_yy = [sem(f"s_yy{t}") for t in range(TILES)]
        s_fx = sem("s_fx")

        w_in_v = I["w_in"][0].rearrange("(k p) m -> p k m", p=P)
        xp = I["x_prompt"][0]
        block = ctx.enter_context(nc.Block())

        def x_rows(t):
            return (xp[t * P:(t + 1) * P, :], P) if t < TILES - 1 else (I["x_sample"][0], LAST)

        def wait(eng, s, v):
            if not isinstance(v, int) or v > 0:
                eng.wait_ge(s, v)

        def groups(eng, step, p):
            for u in range(WB):
                step(p, 0, u)
            with eng.Fori(1, GE // WB - 1) as i:
                for u in range(WB):
                    step(p, i, u)
            for u in range(WB):
                step(p, GE // WB - 1, u)

        def rounds(eng, one):
            one(0)
            eng.wait_ge(s_np, 1)
            n = eng.value_load(np_i[0:1, 0:1], min_val=1, max_val=PASSES)
            with eng.If(n > 1):
                with eng.Fori(1, n) as p:
                    one(p)
            return n

        def runs(c, hist):
            a, b = c * CH, (c + 1) * CH
            out = []
            if a < SEQ:
                e = min(b, SEQ)
                out.append((0, hist + a, e - a))
            if b > SEQ:
                s = max(a, SEQ)
                out.append((s - a, 2 * hist + s, b - s))
            return out

        NU, NV = GR, 2 * GR
        NG = NU + NV
        NB = NG + 1
        NC = NB + 2 * KD
        NP = NC + 2 * KD
        GATE_P = D_POOL + 2 * D_CONV
        GATE_C = GATE_P + D
        A_TAPS = 11
        B_TAPS = (3, 2)
        assert A_TAPS + sum(B_TAPS) * KD // 2 == CW
        w_po_v = I["w_pool_out"][0].rearrange("(k p) m -> p k m", p=P)
        w_co_v = I["w_conv_out"][0].rearrange("(k p) m -> p k m", p=P)
        w_out_v = I["w_out"][0].rearrange("(k p) m -> p k m", p=P)
        LN_PIECES = [(a, min(LN_W, CWID - a)) for a in range(0, CWID, LN_W)]
        BIAS, LN_G, LN_B, SCALE = 0, GR, 2 * GR, 3 * GR

        @block.sync
        def _(sp):
            sp.dma_start(g_mix_b[:], I["g_mix"][0].partition_broadcast(P)).then_inc(s_const, 16)
            for t in range(TILES):
                src, n = x_rows(t)
                if t >= 2:
                    sp.wait_ge(s_xn, t - 1)
                sp.dma_start(xs[0:n, t % 2, :], src).then_inc(s_x[t % 2], 16)
                if t == 1:
                    for q, v in enumerate(("b_dw", "ln_g", "ln_b", "pool_scale")):
                        sp.dma_start(vec_in[q * GR:(q + 1) * GR, :],
                                     I[v][0].rearrange("(g p) -> g p", p=P)).then_inc(s_hist, 16)
                    sp.dma_start(hist_in[:, 2, :], I["w_dw"][0]).then_inc(s_hist, 16)
                    sp.dma_start(hist_in[0:PH, 0, :], I["state_pool"][0, 0]).then_inc(s_hist, 16)
                    sp.dma_start(hist_in[0:HIST, 1, :], I["state_conv"][0, 0]).then_inc(s_hist, 16)
                    for s in range(2):
                        sp.dma_start(w_raw[:, s], w_in_v[:, :, s * P:(s + 1) * P]).then_inc(s_w[s], 16)

            def panel(n, s, col, src=w_in_v, K=KD):
                sp.wait_ge(s_wlo, n - 1)
                sp.dma_start(w_raw[:, s, 0:K], src[:, :, bass.ds(col, P)]).then_inc(s_w[s], 16)

            panel(2, 0, 2 * P)
            panel(3, 1, 3 * P)
            with sp.Fori(1, GR + 1) as j:
                panel(NU - 2 + 2 * j, 0, 2 * GR * P - P + j * P)
                panel(NU - 1 + 2 * j, 1, GR * P - P + j * P)
            sp.wait_ge(s_whi, NG - 1)
            sp.wait_ge(s_wlo, NG - 1)
            sp.dma_start(w_raw[:, 0, 0:GR], I["w_pool_grp"][0].rearrange("g c d -> c g d")).then_inc(s_w[0], 16)
            sp.wait_ge(s_sC, 1)
            sp.dma_start(O["new_pool_prompt"][0, 0], state_out[0:PH, 0, :]).then_inc(s_tail, 16)
            sp.dma_start(O["new_pool_sample"][0, 0], state_out[0:PH, 1, :]).then_inc(s_tail, 16)
            with sp.Fori(1, KD + 1) as j:
                panel(NB - 2 + 2 * j, 1, GATE_P - P + j * P)
                panel(NB - 1 + 2 * j, 0, j * P - P, w_po_v, GR)
                with sp.If(j < 2):
                    sp.wait_ge(s_sC, 2)
                    sp.dma_start(O["new_conv_prompt"][0, 0], state_out[0:HIST, 2, :]).then_inc(s_tail, 16)
                    sp.dma_start(O["new_conv_sample"][0, 0], state_out[0:HIST, 3, :]).then_inc(s_tail, 16)

            def wo_quarter(h, q):
                n = 4 * h + q - 1
                sp.wait_ge(s_wolo, n)
                sp.dma_start(wo_raw[:], w_out_v[:, bass.ds(2 * q - 2, 2), h * 512:(h + 1) * 512]).then_inc(s_wo, 16)

            with sp.Fori(1, KD // 2 + 1) as i:
                for jj in range(2):
                    j = 2 * i + jj - 1
                    panel(NC - 2 + 2 * j, 1, GATE_C - P + j * P)
                    panel(NC - 1 + 2 * j, 0, j * P - P, w_co_v, GR)
                wo_quarter(0, i)
            with sp.Fori(1, 5) as q:
                wo_quarter(1, q)
            sp.wait_ge(s_free[0], (NP + 1) // 2)
            sp.dma_start(g_ffn_b[:], I["g_ffn"][0].partition_broadcast(P)).then_inc(s_rc, 16)
            sp.dma_start(w_r[:, :, 0:G], I["w_rg"][0].rearrange("(p c) g -> p c g", p=P)).then_inc(s_rc, 16)
            sp.dma_start(w_r[:, :, G:NR], I["w_re"][0].rearrange("(p c) g -> p c g", p=P)).then_inc(s_rc, 16)
            sp.dma_start(b_r[:, 0:G], I["b_rg"][0].partition_broadcast(P)).then_inc(s_rc, 16)
            sp.dma_start(b_r[:, G:NR], I["b_re"][0].partition_broadcast(P)).then_inc(s_rc, 16)

            def h2_store(t):
                n = P if t < TILES - 1 else LAST
                sp.wait_ge(s_h2, t + 1)
                sp.dma_start(H2[t * P:t * P + n, :], h2[0:n, t % 2, :]).then_inc(s_h2st[t % 2], 16)

            def store(t):
                n = P if t < TILES - 1 else LAST
                dst = O["y_prompt"][0, t * P:(t + 1) * P, :] if t < TILES - 1 else O["y_sample"][0]
                sp.wait_ge(s_fo, t + 1)
                sp.dma_start(dst, x1[0:n, t, :]).then_inc(s_out, 16)

            gate_v = I["w_gate"][0].rearrange("g e (p c) f -> (g e) p c f", p=P)
            up_v = I["w_up"][0].rearrange("g e (p c) f -> (g e) p c f", p=P)
            down_v = I["w_down"][0].rearrange("g e (c p) d -> (g e) p c d", p=P)

            def load(e, it, u, part=None):
                parts = ((gate_v, wgu[u][:, 0], s_gu), (up_v, wgu[u][:, 1], s_gu), (down_v, wdn[u][:], s_down))
                for src, dst, s_used in parts if part is None else parts[part:part + 1]:
                    if part is None:
                        wait(sp, s_used, it - WB + 1)
                    s1 = src[e] if isinstance(e, int) else src[bass.ds(e, 1)].rearrange("a p k f -> (a p) k f")
                    sp.dma_start(dst, s1).then_inc(s_wl[u], 16)

            for n in range(2 * TILES):
                h, t = divmod(n, TILES)
                src, rows = x_rows(t)
                if n >= 2:
                    sp.wait_ge(s_res, n - 1)
                sp.dma_start(xr[0:rows, n % 2, :], src[:, h * 512:(h + 1) * 512]).then_inc(s_xr[n % 2], 16)
                if h == 1 and t >= 2:
                    h2_store(t - 2)
                    if t % 2 == 0:
                        if t == 2:
                            sp.wait_ge(s_o, TILES)
                        if t < 8:
                            load(0, 0, 0, t // 2 - 1)
            h2_store(TILES - 2)
            h2_store(TILES - 1)
            sp.wait_ge(s_o, 2 * TILES)
            for u in range(1, WB):
                load(u, u, u)
            sp.dma_start(g_fin_b[:], I["g_final"].partition_broadcast(P)).then_inc(s_gfin, 16)
            with sp.Fori(1, GE // WB) as i:
                for u in range(WB):
                    load(i * WB + u, i * WB + u, u)
            sp.wait_ge(s_np, 1)
            n_pass = sp.value_load(np_i[0:1, 0:1], min_val=1, max_val=PASSES)
            with sp.If(n_pass > 1):
                with sp.Fori(1, n_pass) as p:
                    with sp.Fori(0, GE // WB) as i:
                        for u in range(WB):
                            load(i * WB + u, p * GE + i * WB + u, u)
            for b in range(2):
                sp.wait_ge(s_ys[b], n_pass * (8 * GE))
            for t in range(TILES):
                n = P if t < TILES - 1 else LAST
                sp.dma_start(yy[0:n, t], YK.rearrange("(k t) d -> t k d", k=2)[t * P:t * P + n]).then_inc(s_yy[t], 16)
            for t in range(TILES):
                store(t)
            sp.wait_ge(s_out, 16 * TILES)
            sp.wait_ge(s_tail, 64)

        @block.gpsimd
        def _(pool):
            pool.memset(ident[:], 0.0).then_inc(s_zero, 1)
            pool.wait_ge(s_zero, 1)
            pool.affine_select(out=ident[:], in_=ident[:], compare_op=ALU.not_equal, fill=1.0,
                               base=0, pattern=[[-1, P]], channel_multiplier=1).then_inc(s_ident, 1)
            pool.memset(eps_rms[:], RMS_EPS).then_inc(s_eps, 1)
            pool.memset(U[:, :, 0:PH], 0.0)
            pool.memset(V[:, :, 0:HIST], 0.0).then_inc(s_ident, 1)
            pool.memset(eps_ln[:], LN_EPS)
            pool.memset(ln_mean[:], 1.0 / D_CONV).then_inc(s_ident, 1)
            for c in range(16):
                pool.memset(inv_cnt[:, c:c + 1], 1.0 / (c + 1))

            pool.wait_ge(s_hlo, TILES)
            pool.wait_ge(s_free[0], NU // 2)
            pool.wait_ge(s_free[1], NU // 2)
            pool.wait_ge(s_histC, 1)
            done = [0]

            def link(op):
                done[0] += 1
                op.then_inc(s_pool, 1)
                pool.wait_ge(s_pool, done[0])

            for g in range(GR):
                w = 2 << g
                src = U[:, g, :]
                for k in range(g + 1):
                    lag, lo = 1 << k, (2 << k) - 1
                    link(pool.tensor_tensor(win[:, k % 2, lo:UW], src[:, lo:UW], src[:, lo - lag:UW - lag], ALU.add))
                    src = win[:, k % 2, :]
                link(pool.tensor_tensor(diff[:, 0:w - 1], src[:, PH:PH + w - 1], inv_cnt[:, 0:w - 1], ALU.mult))
                pool.tensor_scalar(diff[:, w - 1:SEQ], src[:, PH + w - 1:PH + SEQ], 1.0 / w, None, ALU.mult)
                link(pool.tensor_scalar(diff[:, SEQ:T], src[:, UW - DEC:UW], 1.0 / w, None, ALU.mult))
                pool.tensor_tensor(diff[:, 0:SEQ], diff[:, 0:SEQ], U[:, g, PH:PH + SEQ], ALU.subtract)
                link(pool.tensor_tensor(diff[:, SEQ:T], diff[:, SEQ:T], U[:, g, UW - DEC:UW], ALU.subtract))
                link(pool.tensor_copy(d_hi[:, g, :], diff[:]))
                link(pool.tensor_tensor(d_lo[:, g, :], diff[:], d_hi[:, g, :].bitcast(F32), ALU.subtract))
                pool.sem_inc(s_diff, 1)

            def split_lo(n, s, K):
                pool.wait_ge(s_whi, n + 1)
                pool.tensor_tensor(w_lo[:, s, 0:K], w_raw[:, s, 0:K], w_hi[:, s, 0:K].bitcast(F32),
                                   ALU.subtract).then_inc(s_wlo, 1)

            pool.wait_ge(s_wlo, NB + 1)
            with pool.Fori(0, KD - 1) as j:
                split_lo(NB + 1 + 2 * j, 0, GR)
                split_lo(NB + 2 + 2 * j, 1, KD)
            split_lo(NC - 1, 0, GR)

            pool.wait_ge(s_wolo, 8)
            link(pool.memset(tri[:], 1.0))
            pool.affine_select(out=tri[:], in_=tri[:], compare_op=ALU.is_gt, fill=0.0, base=0,
                               pattern=[[1, P]], channel_multiplier=-1)
            pool.iota(io_i[:], pattern=[[1, GE]], base=0, channel_multiplier=0)
            pool.iota(row_i[:], pattern=[[P, TILES], [T, 2]], base=1, channel_multiplier=1)
            link(pool.iota(slot_i[:], pattern=[[1, CAP]], base=0, channel_multiplier=0))
            pool.tensor_copy(io[:], io_i[:])
            pool.tensor_copy(tri_b[:], tri[:])
            pool.memset(one_b[:], 1.0)
            pool.tensor_copy(slot_f[:], slot_i[:])
            link(pool.tensor_copy(row_f[:], row_i[:]))
            pool.tensor_scalar(thr[:], io[:, 0:PASSES - 1], float(CAP), float(CAP), ALU.mult, ALU.add)
            link(pool.tensor_copy(row_hi[:], row_f[:]))
            link(pool.tensor_tensor(row_lo[:], row_f[:], row_hi[:], ALU.subtract))
            link(pool.tensor_scalar(valid[:], row_f[:, TILES - 1, 0:1], float(T + 1), None, ALU.is_lt))
            pool.wait_ge(s_o, 2 * TILES)
            pool.memset(X[:], 0.0).then_inc(s_ct, 1)
            pool.sem_inc(s_tri, 1)

            pool.wait_ge(s_h2st[0], 16 * ((TILES + 1) // 2))
            pool.wait_ge(s_h2st[1], 16 * (TILES // 2))
            pool.wait_ge(s_ct, 1)

            g_bound = pool.alloc_register("g_bound")
            s_bound = pool.alloc_register("s_bound")

            def gather(p, i, u):
                pool.wait_ge(s_gc, p * GE + i * WB + u + 1)
                pool.reg_add(g_bound, pool.zero_reg, T - 1)
                pool.indirect_dma_start(out=X[0:CAP, u, :], out_offset=None, in_=H2,
                                        in_offset=bass.IndirectOffsetOnAxis(ap=g_now[0:CAP, u:u + 1], axis=0),
                                        bounds_check=g_bound, oob_is_err=False).then_inc(s_xg[u], 16)

            def scatter(p, i, u):
                it, b = p * GE + i * WB + u, u % 2
                pool.wait_ge(s_yA, it + 1)
                pool.wait_ge(s_yD, it + 1)
                pool.reg_add(s_bound, pool.zero_reg, 2 * T - 1)
                pool.indirect_dma_start(out=YK, out_offset=bass.IndirectOffsetOnAxis(ap=s_now[0:CAP, b:b + 1], axis=0),
                                        in_=Y[0:CAP, b, :], in_offset=None,
                                        bounds_check=s_bound, oob_is_err=False).then_inc(s_ys[b], 16)

            def ahead(p, i, u):
                gather(p, i + (u + 3) // WB, (u + 3) % WB)
                scatter(p, i, u)

            def one(p):
                for u in range(3):
                    gather(p, 0, u)
                for u in range(WB):
                    ahead(p, 0, u)
                with pool.Fori(1, GE // WB - 1) as i:
                    for u in range(WB):
                        ahead(p, i, u)
                gather(p, GE // WB - 1, WB - 1)
                for u in range(WB):
                    scatter(p, GE // WB - 1, u)

            rounds(pool, one)
            pool.wait_ge(s_gfin, 16)
            for t in range(TILES):
                n = P if t < TILES - 1 else LAST
                pool.wait_ge(s_fx, t + 1)
                pool.tensor_tensor(x1[0:n, t, :], x1[0:n, t, :], g_fin_b[0:n, :], ALU.mult).then_inc(s_fo, 1)

        @block.scalar
        def _(act):
            def h_hi_copy(t):
                n = P if t < TILES - 1 else LAST
                act.wait_ge(s_xT, t + 1)
                b = 2 * (t % 3)
                for q in range(2):
                    src = ps[:, b + q, :].rearrange("p (k t) -> p k t", k=4)[:, :, 0:n]
                    a = act.activation(h_hi[:, 4 * q:4 * q + 4, t * P:t * P + n], src, ACT.Copy)
                a.then_inc(s_hhi, 1)

            act.wait_ge(s_eps, 1)
            for t in range(TILES):
                n = P if t < TILES - 1 else LAST
                act.wait_ge(s_x[t % 2], 16 * (t // 2 + 1))
                if t >= 1:
                    act.wait_ge(s_sq, t)
                act.activation(squares[0:n, :], xs[0:n, t % 2, :], ACT.Square,
                               accum_out=sumsq[0:n, t:t + 1]).then_inc(s_sq, 1)
                act.wait_ge(s_sq, t + 1)
                act.activation(rstd[0:n, t:t + 1], sumsq[0:n, t:t + 1], ACT.Sqrt, scale=1.0 / D, bias=eps_rms[0:n, :]).then_inc(s_std, 1)
                if t >= 1:
                    h_hi_copy(t - 1)
            h_hi_copy(TILES - 1)

            def split_hi(n, s, K=KD):
                act.wait_ge(s_w[s], 8 * (n - s) + 16)
                act.activation(w_hi[:, s, 0:K], w_raw[:, s, 0:K], ACT.Copy).then_inc(s_whi, 1)

            split_hi(0, 0)
            split_hi(1, 1)

            with act.Fori(0, NU // 2) as i:
                for s in range(2):
                    n = 2 * i + s
                    for c in range(CHUNKS):
                        act.wait_ge(s_mm, 3 * n + c + 1)
                        for (a, pos, w) in runs(c, PH):
                            op = act.activation(U[:, bass.ds(n, 1), pos:pos + w], ps[:, 3 * s + c:3 * s + c + 1, a:a + w], ACT.Copy)
                    op.then_inc(s_free[s], 1)
                    split_hi(n + 2, s)
            with act.Fori(0, GR) as j:
                n = NU + 2 * j
                for c in range(CHUNKS):
                    act.wait_ge(s_mm, 3 * n + c + 1)
                    for (a, pos, w) in runs(c, HIST):
                        op = act.activation(V[:, bass.ds(j, 1), pos:pos + w], ps[:, c:c + 1, a:a + w], ACT.Sigmoid)
                op.then_inc(s_free[0], 1)
                with act.If(j < GR - 1):
                    split_hi(n + 2, 0)
                with act.Else():
                    split_hi(n + 2, 0, GR)
                act.wait_ge(s_mm, 3 * (n + 2))
                split_hi(n + 3, 1)

            act.wait_ge(s_diff, GR)
            for g in range(GR):
                act.wait_ge(s_grp, g + 1)
                for c in range(CHUNKS):
                    op = act.activation(y_hi[:, g, c * CH:(c + 1) * CH], ps[:, 3 * (g % 2) + c, 0:CH], ACT.Copy,
                                        scale=vecs[:, SCALE + g:SCALE + g + 1])
                op.then_inc(s_yhi, 1)
            split_hi(NB + 1, 0, GR)

            def gate(n, jj, j, free0, last=False):
                act.wait_ge(s_free[0], free0)
                for c in range(CHUNKS):
                    act.wait_ge(s_mm, 3 * n + c + 1)
                    op = act.activation(S[:, jj, c * CH:(c + 1) * CH], ps[:, 3 + c, 0:CH], ACT.Sigmoid)
                op.then_inc(s_free[1], 1)

            act.wait_ge(s_tail, 64)

            def gate_p(i, jj):
                j = 2 * i + jj
                n = NB + 2 * j
                gate(n, jj, j, NG // 2 + j)
                split_hi(n + 2, 1)

            def w_after(i, jj):
                n = NB + 2 * (2 * i + jj)
                act.wait_ge(s_mm, 3 * (n + 2))
                split_hi(n + 3, 0, GR)

            with act.Fori(0, KD // 2 - 1) as i:
                for jj in range(2):
                    gate_p(i, jj)
                    w_after(i, jj)
            gate_p(KD // 2 - 1, 0)
            w_after(KD // 2 - 1, 0)
            gate_p(KD // 2 - 1, 1)

            def ln_square(p):
                a, w = LN_PIECES[p]
                act.wait_ge(s_cen, p + 1)
                wait(act, s_var, p)
                act.activation(ln_sq[:, :, 0:w], C[:, :, a:a + w], ACT.Square).then_inc(s_csq, 1)

            def ln_root(p):
                w = LN_PIECES[p][1]
                act.wait_ge(s_var, p + 1)
                wait(act, s_norm, p)
                act.activation(ln_rstd[:, 0:w], ps[:, 7, 0:w], ACT.Sqrt, bias=eps_ln[:]).then_inc(s_lstd, 1)

            for p in range(len(LN_PIECES)):
                ln_square(p)
                if p == 1:
                    w_after(KD // 2 - 1, 1)
                ln_root(p)
            for p, (a, w) in enumerate(LN_PIECES):
                act.wait_ge(s_norm, p + 1)
                pieces = [(a, a, w)] if a + w <= SEQ else [(a, a, SEQ - a), (SEQ + HIST, SEQ, DEC)]
                for g in range(GR):
                    for (x, y, n) in pieces:
                        op = act.activation(C[:, g, y:y + n], C[:, g, x:x + n], ACT.Silu,
                                            scale=vecs[:, LN_G + g:LN_G + g + 1], bias=vecs[:, LN_B + g:LN_B + g + 1])
                op.then_inc(s_silu, 1)

            def pair(i):
                for jj in range(2):
                    j = 2 * i + jj
                    n = NC + 2 * j
                    gate(n, jj, j, NC // 2 + j)
                    if isinstance(i, int):
                        if jj == 0:
                            split_hi(n + 2, 1)
                            act.wait_ge(s_mm, 3 * (n + 2))
                            split_hi(n + 3, 0, GR)
                    else:
                        split_hi(n + 2, 1)
                        act.wait_ge(s_mm, 3 * (n + 2))
                        split_hi(n + 3, 0, GR)
                act.wait_ge(s_wo, 16 * i + 16)
                act.activation(wo_hi[0][:, bass.ds(2 * i, 2), :], wo_raw[:], ACT.Copy).then_inc(s_wohi, 1)

            with act.Fori(0, KD // 2 - 1) as i:
                pair(i)
            pair(KD // 2 - 1)

            act.wait_ge(s_mm, 3 * (NP - 1))
            for k in range(KD):
                act.wait_ge(s_free[0], (NP - 1) // 2 - KD + k + 2)
                act.activation(h_hi[:, k, :], M[:, k, :], ACT.Copy).then_inc(s_mhi, 1)
            with act.Fori(0, 4) as q:
                act.wait_ge(s_wo, 16 * q + 80)
                act.activation(wo_hi[1][:, bass.ds(2 * q, 2), :], wo_raw[:], ACT.Copy).then_inc(s_wohi, 1)

            def h2_turned(t):
                n = P if t < TILES - 1 else LAST
                act.wait_ge(s_h2T, t + 1)
                wait(act, s_lg, t - 1)
                for q in range(2):
                    src = ps[:, 4 + q, :].rearrange("p (k t) -> p k t", k=4)[:, :, 0:n]
                    a = act.activation(h2T[:, t % 2, 4 * q:4 * q + 4, 0:n], src, ACT.Copy)
                a.then_inc(s_h2c, 1)

            for t in range(TILES):
                n = P if t < TILES - 1 else LAST
                act.wait_ge(s_res, TILES + t + 1)
                wait(act, s_sq2, t)
                act.activation(squares2[0:n, :], x1[0:n, t, :], ACT.Square, accum_out=sumsq[0:n, t:t + 1]).then_inc(s_sq2, 1)
                act.wait_ge(s_sq2, t + 1)
                act.activation(rstd[0:n, t:t + 1], sumsq[0:n, t:t + 1], ACT.Sqrt, scale=1.0 / D,
                               bias=eps_rms[0:n, :]).then_inc(s_std2, 1)
                if t >= 1:
                    h2_turned(t - 1)
            h2_turned(TILES - 1)
            act.wait_ge(s_ra, 1)
            act.activation(dg[:], dg[:], ACT.Exp).then_inc(s_re, 1)
            act.wait_ge(s_ra, 2)
            act.activation(ex[:], ex[:], ACT.Exp).then_inc(s_re, 1)

            def x_turned(it, b):
                act.wait_ge(s_tx, it + 1)
                wait(act, s_gu, it - 1)
                act.activation(XT[:, b, 0:4, 0:CAP], ps[:, 0, :].rearrange("p (c t) -> p c t", c=4)[:, :, 0:CAP], ACT.Copy).then_inc(s_xtA, 1)

            def y_out(it, b, half):
                act.wait_ge(s_down, it + 1)
                wait(act, s_ys[b], 16 * half)
                act.activation(Y[0:CAP, b, 0:512], ps[0:CAP, 4 + 2 * b, :], ACT.Copy).then_inc(s_yA, 1)

            def step(p, i, u):
                it = p * GE + i * WB + u
                b = u % 2
                act.wait_ge(s_gu, it + 1)
                wait(act, s_act, it - 1)
                act.activation(sg[:, b, :, 0:CAP], ps[:, 2 + b, 0:KF * CAP].rearrange("p (c t) -> p c t", c=KF), ACT.Silu).then_inc(s_sg, 1)
                if not (isinstance(i, int) and i == GE // WB - 1 and u == WB - 1):
                    x_turned(it + 1, 1 - b)
                if not (isinstance(i, int) and i == 0 and u == 0):
                    y_out(it - 1, 1 - b, p * (GE // 2) + 2 * i + (u - 1) // 2)

            def one(p):
                x_turned(p * GE, 0)
                groups(act, step, p)
                y_out(p * GE + GE - 1, 1, p * (GE // 2) + GE // 2 - 1)

            rounds(act, one)

            def scaled(t):
                n = P if t < TILES - 1 else LAST
                act.wait_ge(s_fr, t + 1)
                act.activation(x1[0:n, t, :], x1[0:n, t, :], ACT.Copy, scale=rstd[0:n, t:t + 1]).then_inc(s_fx, 1)

            for t in range(TILES):
                n = P if t < TILES - 1 else LAST
                act.wait_ge(s_fa, t + 1)
                wait(act, s_fq, t - 1)
                act.activation(sq3[0:n, t % 2, :], x1[0:n, t, :], ACT.Square, accum_out=sumsq[0:n, t:t + 1]).then_inc(s_fq, 1)
                act.wait_ge(s_fq, t + 1)
                act.activation(rstd[0:n, t:t + 1], sumsq[0:n, t:t + 1], ACT.Sqrt, scale=1.0 / D,
                               bias=eps_rms[0:n, :]).then_inc(s_fs, 1)
                if t >= 1:
                    scaled(t - 1)
            scaled(TILES - 1)

        @block.vector
        def _(dve):
            def h_lo_split(t):
                n = P if t < TILES - 1 else LAST
                dve.wait_ge(s_hhi, t + 1)
                b = 2 * (t % 3)
                for q in range(2):
                    src = ps[:, b + q, :].rearrange("p (k t) -> p k t", k=4)[:, :, 0:n]
                    d = dve.tensor_tensor(h_lo[:, 4 * q:4 * q + 4, t * P:t * P + n], src,
                                          h_hi[:, 4 * q:4 * q + 4, t * P:t * P + n].bitcast(F32), ALU.subtract)
                d.then_inc(s_hlo, 1)

            dve.wait_ge(s_const, 16)
            for t in range(TILES):
                n = P if t < TILES - 1 else LAST
                dve.wait_ge(s_std, t + 1)
                dve.reciprocal(rstd[0:n, t:t + 1], rstd[0:n, t:t + 1]).then_inc(s_rstd, 1)
                dve.wait_ge(s_rstd, t + 1)
                if t >= 2:
                    dve.wait_ge(s_xT, t - 1)
                dve.scalar_tensor_tensor(out=xn[0:n, t % 2, :], in0=xs[0:n, t % 2, :], scalar=rstd[0:n, t:t + 1],
                                         in1=g_mix_b[0:n, :], op0=ALU.mult, op1=ALU.mult).then_inc(s_xn, 1)
                if t >= 1:
                    h_lo_split(t - 1)
            h_lo_split(TILES - 1)
            dve.memset(hT[:, 2 * HT:].bitcast(F32), 0.0)

            dve.wait_ge(s_histT, 1)
            dve.wait_ge(s_ident, 2)
            dve.tensor_copy(U[:, :, PH + SEQ:PH + SEQ + PH],
                            ps[:, 6, :].rearrange("p (g t) -> p g t", g=GR)[:, :, 0:PH])
            dve.tensor_copy(w_dw[:], ps[:, 6, :].rearrange("p (g t) -> p g t", g=GR)[:, :, 32:32 + CW])
            dve.tensor_copy(vecs[:], ps[:, 7, 64:64 + 4 * GR])
            dve.tensor_copy(V[:, :, HIST + SEQ:HIST + SEQ + HIST],
                            ps[:, 7, :].rearrange("p (g t) -> p g t", g=GR)[:, :, 0:HIST]).then_inc(s_histC, 1)

            def split_lo(n, s, K=KD):
                dve.wait_ge(s_whi, n + 1)
                dve.tensor_tensor(w_lo[:, s, 0:K], w_raw[:, s, 0:K], w_hi[:, s, 0:K].bitcast(F32),
                                  ALU.subtract).then_inc(s_wlo, 1)

            split_lo(0, 0)
            split_lo(1, 1)
            with dve.Fori(0, NU // 2) as i:
                for s in range(2):
                    split_lo(2 * i + s + 2, s)
            dve.wait_ge(s_sT, 1)
            dve.tensor_copy(state_out[0:PH, 0, :], ps[0:PH, 6, :])
            dve.tensor_copy(state_out[0:PH, 1, :], ps[0:PH, 7, :]).then_inc(s_sC, 1)

            def glu(j):
                n = NU + 2 * j
                split_lo(n + 2, 0, KD if not isinstance(j, int) else GR)
                for c in range(CHUNKS):
                    dve.wait_ge(s_mm, 3 * (n + 1) + c + 1)
                    if c == 0:
                        dve.wait_ge(s_free[0], j + NU // 2 + 1)
                    for (a, pos, w) in runs(c, HIST):
                        op = dve.tensor_tensor(V[:, bass.ds(j, 1), pos:pos + w], V[:, bass.ds(j, 1), pos:pos + w],
                                               ps[:, 3 + c:4 + c, a:a + w], ALU.mult)
                op.then_inc(s_free[1], 1)
                split_lo(n + 3, 1)

            def first_taps(j):
                dve.wait_ge(s_diff, j + 1)
                dve.wait_ge(s_sT, 1)
                dve.wait_ge(s_free[1], j + NU // 2 + 1)
                cj = C[:, bass.ds(j, 1), :]
                for k in range(A_TAPS):
                    v = V[:, bass.ds(j, 1), k:k + CWID]
                    tap = w_dw[:, bass.ds(j, 1), k]
                    if k == 0:
                        op = dve.tensor_scalar(cj, v, tap, vecs[:, bass.ds(BIAS + j, 1)], ALU.mult, ALU.add)
                    else:
                        dve.wait_ge(s_conv, A_TAPS * j + k)
                        op = dve.scalar_tensor_tensor(out=cj, in0=v, scalar=tap, in1=cj, op0=ALU.mult, op1=ALU.add)
                    op.then_inc(s_conv, 1)

            with dve.Fori(0, GR - 1) as j:
                glu(j)
                first_taps(j)
            glu(GR - 1)
            dve.wait_ge(s_sT, 2)
            dve.tensor_copy(state_out[0:HIST, 2, :], ps[0:HIST, 6, :])
            dve.tensor_copy(state_out[0:HIST, 3, :], ps[0:HIST, 7, :]).then_inc(s_sC, 1)
            for g in range(GR):
                dve.wait_ge(s_yhi, g + 1)
                for c in range(CHUNKS):
                    op = dve.scalar_tensor_tensor(out=y_lo[:, g, c * CH:(c + 1) * CH], in0=ps[:, 3 * (g % 2) + c, 0:CH],
                                                  scalar=vecs[:, SCALE + g:SCALE + g + 1],
                                                  in1=y_hi[:, g, c * CH:(c + 1) * CH].bitcast(F32),
                                                  op0=ALU.mult, op1=ALU.subtract)
                op.then_inc(s_ylo, 1)
            dve.wait_ge(s_ylo, GR)
            dve.sem_inc(s_free[0], 1)
            first_taps(GR - 1)

            def taps(k0, k, base):
                for g in range(GR):
                    dve.wait_ge(s_conv, base + g + 1)
                    dve.scalar_tensor_tensor(out=C[:, g, :], in0=V[:, g, bass.ds(k0 + k, CWID)],
                                             scalar=w_dw[:, g, bass.ds(k0 + k, 1)], in1=C[:, g, :],
                                             op0=ALU.mult, op1=ALU.add).then_inc(s_conv, 1)

            def later_taps(i, jj):
                k0 = A_TAPS + sum(B_TAPS) * i
                for k in range(jj * B_TAPS[0], jj * B_TAPS[0] + B_TAPS[jj]):
                    taps(k0, k, GR * (k0 + k - 1))

            def gated_p(j, jj):
                n = NB + 2 * j
                dve.wait_ge(s_free[1], NG // 2 + 1 + j)
                for c in range(CHUNKS):
                    dve.wait_ge(s_mm, 3 * (n + 1) + c + 1)
                    op = dve.tensor_tensor(M[:, bass.ds(j, 1), c * CH:(c + 1) * CH], S[:, jj:jj + 1, c * CH:(c + 1) * CH],
                                           ps[:, c:c + 1, 0:CH], ALU.mult)
                op.then_inc(s_free[0], 1)

            def step_p(i, jj):
                j = 2 * i + jj
                later_taps(i, jj)
                gated_p(j, jj)

            with dve.Fori(0, KD // 2 - 1) as i:
                for jj in range(2):
                    step_p(i, jj)
            step_p(KD // 2 - 1, 0)
            later_taps(KD // 2 - 1, 1)
            dve.wait_ge(s_wlo, NC)
            split_lo(NC, 1)

            def wide(ap, w):
                return ap.unsqueeze(1).to_broadcast((P, GR, w))

            def ln_centre(p):
                a, w = LN_PIECES[p]
                dve.wait_ge(s_mean, p + 1)
                dve.tensor_tensor(C[:, :, a:a + w], C[:, :, a:a + w], wide(ps[:, 6, 0:w], w), ALU.subtract).then_inc(s_cen, 1)

            def ln_scale(p):
                a, w = LN_PIECES[p]
                dve.wait_ge(s_lstd, p + 1)
                dve.reciprocal(ln_rstd[:, 0:w], ln_rstd[:, 0:w]).then_inc(s_lrec, 1)
                dve.wait_ge(s_lrec, p + 1)
                dve.tensor_tensor(C[:, :, a:a + w], C[:, :, a:a + w], wide(ln_rstd[:, 0:w], w), ALU.mult).then_inc(s_norm, 1)

            ln_centre(0)
            ln_scale(0)
            ln_centre(1)
            gated_p(KD - 1, 1)
            split_lo(NC + 1, 0, GR)
            ln_scale(1)
            for p in range(2, len(LN_PIECES)):
                ln_centre(p)
                ln_scale(p)
            for p, (a, w) in enumerate(LN_PIECES):
                e = min(a + w, T)
                dve.wait_ge(s_silu, p + 1)
                dve.tensor_copy(a_hi[:, :, a:e], C[:, :, a:e]).then_inc(s_ahi, 1)
                dve.wait_ge(s_ahi, p + 1)
                dve.tensor_tensor(a_lo[:, :, a:e], C[:, :, a:e], a_hi[:, :, a:e].bitcast(F32), ALU.subtract).then_inc(s_alo, 1)

            def m_lo(k):
                dve.wait_ge(s_mhi, k + 1)
                dve.tensor_tensor(h_lo[:, k, :], M[:, k, :], h_hi[:, k, :].bitcast(F32), ALU.subtract).then_inc(s_mlo, 1)

            def wo_lo_quarter(h, q):
                dve.wait_ge(s_wohi, 4 * h + q + 1)
                dve.tensor_tensor(wo_lo[h][:, bass.ds(2 * q, 2), :], wo_raw[:], wo_hi[h][:, bass.ds(2 * q, 2), :].bitcast(F32),
                                  ALU.subtract).then_inc(s_wolo, 1)

            def pair(i):
                for jj in range(2):
                    j = 2 * i + jj
                    n = NC + 2 * j
                    last = isinstance(i, int) and jj == 1
                    if not last:
                        split_lo(n + 2, 1)
                    else:
                        wo_lo_quarter(0, i)
                        for k in range(KD - 1):
                            m_lo(k)
                    dve.wait_ge(s_free[1], NC // 2 + 1 + j)
                    for c in range(CHUNKS):
                        dve.wait_ge(s_mm, 3 * (n + 1) + c + 1)
                        sc = S[:, jj:jj + 1, c * CH:(c + 1) * CH]
                        dve.tensor_tensor(sc, sc, ps[:, c:c + 1, 0:CH], ALU.mult).then_inc(s_sy, 1)
                    for c in range(CHUNKS):
                        sc = S[:, jj:jj + 1, c * CH:(c + 1) * CH]
                        mc = M[:, bass.ds(j, 1), c * CH:(c + 1) * CH]
                        dve.wait_ge(s_sy, 3 * j + c + 1)
                        op = dve.tensor_tensor(mc, mc, sc, ALU.add)
                    op.then_inc(s_free[0], 1)
                    if not last:
                        split_lo(n + 3, 0, GR)
                if not isinstance(i, int):
                    wo_lo_quarter(0, i)

            with dve.Fori(0, KD // 2 - 1) as i:
                pair(i)
            pair(KD // 2 - 1)
            m_lo(KD - 1)
            with dve.Fori(0, 4) as q:
                wo_lo_quarter(1, q)
            def h2_tile(t):
                n = P if t < TILES - 1 else LAST
                dve.wait_ge(s_std2, t + 1)
                dve.reciprocal(rstd[0:n, t:t + 1], rstd[0:n, t:t + 1]).then_inc(s_rs2, 1)
                dve.wait_ge(s_rs2, t + 1)
                if t == 0:
                    dve.wait_ge(s_rc, 16 * 5)
                wait(dve, s_h2T, t - 1)
                wait(dve, s_h2st[t % 2], 16 * (t // 2))
                dve.scalar_tensor_tensor(out=h2[0:n, t % 2, :].rearrange("r (c p) -> r p c", c=KD),
                                         in0=x1[0:n, t, :].rearrange("r (p c) -> r p c", c=KD), scalar=rstd[0:n, t:t + 1],
                                         in1=g_ffn_b[0:n, :].rearrange("r (p c) -> r p c", c=KD),
                                         op0=ALU.mult, op1=ALU.mult).then_inc(s_h2, 1)

            for n in range(2 * TILES):
                h, t = divmod(n, TILES)
                rows = P if t < TILES - 1 else LAST
                dve.wait_ge(s_o, n + 1)
                dve.wait_ge(s_xr[n % 2], 16 * (n // 2 + 1))
                dve.tensor_tensor(x1[0:rows, t, h * 512:(h + 1) * 512], xr[0:rows, n % 2, :], ps[0:rows, (n + 3) % 4, :],
                                  ALU.add).then_inc(s_res, 1)
                if h == 1:
                    h2_tile(t)

            done = [0]

            def link(op):
                done[0] += 1
                op.then_inc(s_rt, 1)
                dve.wait_ge(s_rt, done[0])

            def b3(ap, n):
                return ap.unsqueeze(2).to_broadcast((P, TILES, n))

            def row(ap, n):
                return ap[:, 0:n].unsqueeze(1).to_broadcast((P, TILES, n))

            link(dve.memset(L[:], 0.0))
            dve.wait_ge(s_lg, TILES)
            dve.wait_ge(s_tri, 1)
            lview = ps[:, 6, 0:TILES * NR].rearrange("p (t r) -> p t r", r=NR)
            dve.tensor_tensor(L[:, 0:TILES - 1, :], lview[:, 0:TILES - 1, :],
                              b_r[:].unsqueeze(1).to_broadcast((P, TILES - 1, NR)), ALU.add)
            link(dve.tensor_tensor(L[0:LAST, TILES - 1, :], lview[0:LAST, TILES - 1, :], b_r[0:LAST, :], ALU.add))
            lg = L[:, :, 0:G]
            le = L[:, :, G:NR].rearrange("p t (g e) -> p t g e", g=G)

            def first_max(vals, best, eq, pick, n):
                link(dve.tensor_reduce(best[:], vals, AX.X, ALU.max))
                link(dve.tensor_tensor(eq[:], vals, b3(best[:], n), ALU.is_equal))
                link(dve.scalar_tensor_tensor(out=eq[:], in0=eq[:], scalar=-2.0 * n, in1=row(io, n),
                                              op0=ALU.mult, op1=ALU.add))
                link(dve.tensor_reduce(gmin[:], eq[:], AX.X, ALU.min))
                link(dve.tensor_tensor(pick[:], eq[:], b3(gmin[:], n), ALU.is_equal))

            first_max(lg, gmax, tg, og, G)
            dve.tensor_tensor(dg[:], lg, b3(gmax[:], G), ALU.subtract).then_inc(s_ra, 1)
            link(dve.tensor_tensor(tmp32[:], le, og[:].unsqueeze(3).to_broadcast((P, TILES, G, E)), ALU.mult))
            link(dve.tensor_reduce(les[:], tmp32[:].rearrange("p t g e -> p t e g"), AX.X, ALU.add))
            first_max(les[:], m1, te, oe[0], E)
            link(dve.scalar_tensor_tensor(out=les[:], in0=oe[0][:], scalar=-1.0e30, in1=les[:], op0=ALU.mult, op1=ALU.add))
            first_max(les[:], m2, te, oe[1], E)
            dve.tensor_tensor(ex[:], m2[:], m1[:], ALU.subtract).then_inc(s_ra, 1)
            for k in range(2):
                link(dve.tensor_tensor(Ek[k][:], og[:].unsqueeze(3).to_broadcast((P, TILES, G, E)),
                                       oe[k][:].unsqueeze(2).to_broadcast((P, TILES, G, E)), ALU.mult))
            flat = [e[:].rearrange("p t g e -> p t (g e)") for e in Ek]
            link(dve.tensor_tensor(A[:], flat[0], flat[1], ALU.add))
            dve.tensor_scalar(A[:, TILES - 1, :], A[:, TILES - 1, :], valid[:], None, ALU.mult).then_inc(s_cum, 1)
            for k in range(2):
                link(dve.tensor_scalar(flat[k][:, TILES - 1, :], flat[k][:, TILES - 1, :], valid[:], None, ALU.mult))
            dve.wait_ge(s_re, 2)
            link(dve.tensor_reduce(zsum[:], dg[:], AX.X, ALU.add))
            link(dve.tensor_scalar(den[:], ex[:], 1.0, None, ALU.add))
            link(dve.tensor_tensor(den[:], den[:], zsum[:], ALU.mult))
            link(dve.reciprocal(wts[:, :, 0], den[:]))
            link(dve.tensor_tensor(wts[:, :, 1], wts[:, :, 0], ex[:], ALU.mult))
            dve.wait_ge(s_rk, 1)
            link(dve.tensor_reduce(nmax[:], ps[:, 5, 0:GE], AX.X, ALU.max))
            link(dve.tensor_tensor(ge8[:], nmax[:].to_broadcast((P, PASSES - 1)), thr[:], ALU.is_gt))
            link(dve.tensor_reduce(np_f[:], ge8[:], AX.X, ALU.add))
            dve.tensor_scalar(np_i[:], np_f[:], 1.0, None, ALU.add).then_inc(s_np, 1)
            ranks = ps[:, 7, 0:TILES * GE].rearrange("p (t e) -> p t e", e=GE)
            tmpf = tmp32[:].rearrange("p t g e -> p t (g e)")
            for k in range(2):
                link(dve.tensor_tensor(tmpf, flat[k], ranks, ALU.mult))
                link(dve.tensor_reduce(rank[:, :, k], tmpf, AX.X, ALU.add))
            for k in range(2):
                dve.tensor_tensor(slot_rows[:, k, :, 0], flat[k], b3(row_hi[:, :, k], GE), ALU.mult)
                link(dve.tensor_tensor(slot_rows[:, k, :, 1], flat[k], b3(row_lo[:, :, k], GE), ALU.mult))

            def x_turned(it, b):
                dve.wait_ge(s_tx, it + 1)
                wait(dve, s_gu, it - 1)
                dve.tensor_copy(XT[:, b, 4:8, 0:CAP], ps[:, 1, :].rearrange("p (c t) -> p c t", c=4)[:, :, 0:CAP]).then_inc(s_xtD, 1)

            def column(ap, e):
                return ap[0:CAP, e:e + 1] if isinstance(e, int) else ap[0:CAP, bass.ds(e, 1)]

            def g_column(e, u):
                dve.tensor_copy(g_now[0:CAP, u:u + 1], column(g_idx, e)).then_inc(s_gc, 1)

            def y_out(it, b, half, e):
                dve.wait_ge(s_down, it + 1)
                wait(dve, s_ys[b], 16 * half)
                dve.tensor_copy(s_now[0:CAP, b:b + 1], column(s_idx, e))
                dve.tensor_copy(Y[0:CAP, b, 512:1024], ps[0:CAP, 5 + 2 * b, :]).then_inc(s_yD, 1)

            def step(p, i, u):
                it = p * GE + i * WB + u
                b = u % 2
                if not (isinstance(i, int) and i == GE // WB - 1 and u > 0):
                    g_column(i * WB + u + 3, (u + 3) % WB)
                dve.wait_ge(s_sg, it + 1)
                wait(dve, s_down, it - 1)
                dve.tensor_tensor(AT[:, b, :, 0:CAP], sg[:, b, :, 0:CAP],
                                  ps[:, 2 + b, KF * CAP:2 * KF * CAP].rearrange("p (c t) -> p c t", c=KF),
                                  ALU.mult).then_inc(s_act, 1)
                if not (isinstance(i, int) and i == GE // WB - 1 and u == WB - 1):
                    x_turned(it + 1, 1 - b)
                if not (isinstance(i, int) and i == 0 and u == 0):
                    y_out(it - 1, 1 - b, p * (GE // 2) + 2 * i + (u - 1) // 2, i * WB + u - 1)

            PREP = 6

            def one(p):
                step_no = [0]

                def prep(op):
                    step_no[0] += 1
                    op.then_inc(s_prep, 1)
                    dve.wait_ge(s_prep, p * PREP + step_no[0])

                dve.tensor_tensor(where[:].rearrange("p t k s -> p (t k) s"),
                                  slot_f[:].unsqueeze(1).to_broadcast((P, 2 * TILES, CAP)),
                                  rank[:].rearrange("p t k -> p (t k)").unsqueeze(2).to_broadcast((P, 2 * TILES, CAP)),
                                  ALU.is_equal).then_inc(s_where, 1)
                dve.wait_ge(s_rows, p + 1)
                prep(dve.tensor_reduce(found[0:CAP], ps[0:CAP, 7, 0:2 * GE].rearrange("p (h e) -> p e h", h=2), AX.X, ALU.add))
                prep(dve.tensor_scalar(wrap[0:CAP], found[0:CAP], 0.0, NOWHERE, ALU.is_equal, ALU.mult))
                prep(dve.scalar_tensor_tensor(out=s_idx[0:CAP], in0=found[0:CAP], scalar=-1.0, in1=wrap[0:CAP], op0=ALU.add, op1=ALU.add))
                prep(dve.tensor_scalar(wrap[0:CAP], s_idx[0:CAP], float(T), -float(T), ALU.is_ge, ALU.mult))
                prep(dve.tensor_tensor(g_idx[0:CAP], s_idx[0:CAP], wrap[0:CAP], ALU.add))
                prep(dve.tensor_scalar(rank[:], rank[:], -float(CAP), None, ALU.add))
                for u in range(3):
                    g_column(u, u)
                x_turned(p * GE, 0)
                groups(dve, step, p)
                y_out(p * GE + GE - 1, 1, p * (GE // 2) + GE // 2 - 1, GE - 1)

            rounds(dve, one)

            def root(t):
                n = P if t < TILES - 1 else LAST
                dve.wait_ge(s_fs, t + 1)
                dve.reciprocal(rstd[0:n, t:t + 1], rstd[0:n, t:t + 1]).then_inc(s_fr, 1)

            for t in range(TILES):
                n = P if t < TILES - 1 else LAST
                dve.wait_ge(s_yy[t], 16)
                for k in range(2):
                    wait(dve, s_f1, t + k)
                    dve.scalar_tensor_tensor(out=x1[0:n, t, :], in0=yy[0:n, t, k, :], scalar=wts[0:n, t, k:k + 1],
                                             in1=x1[0:n, t, :], op0=ALU.mult, op1=ALU.add).then_inc((s_f1, s_fa)[k], 1)
                    if k == 0 and t >= 1:
                        root(t - 1)
            root(TILES - 1)

        @block.tensor
        def _(pe):
            pe.wait_ge(s_ident, 1)
            for t in range(TILES):
                n = P if t < TILES - 1 else LAST
                pe.wait_ge(s_xn, t + 1)
                if t >= 3:
                    pe.wait_ge(s_hlo, t - 2)
                for k in range(KD):
                    m = pe.transpose(ps[:, 2 * (t % 3) + k // 4, (k % 4) * P:(k % 4) * P + n],
                                     xn[0:n, t % 2, k * P:(k + 1) * P], ident[0:n, 0:n])
                m.then_inc(s_xT, 1)
            pe.wait_ge(s_hist, 16 * 7)
            for g in range(GR):
                pe.transpose(ps[:, 6, g * P:g * P + PH], hist_in[0:PH, 0, g * P:(g + 1) * P], ident[0:PH, 0:PH])
            for g in range(GR):
                pe.transpose(ps[:, 6, g * P + 32:g * P + 32 + CW], hist_in[:, 2, g * P:(g + 1) * P], ident[0:CW, 0:CW])
            pe.transpose(ps[:, 7, 64:64 + 4 * GR], vec_in[:], ident[0:4 * GR, 0:4 * GR])
            for g in range(GR):
                m = pe.transpose(ps[:, 7, g * P:g * P + HIST], hist_in[0:HIST, 1, g * P:(g + 1) * P], ident[0:HIST, 0:HIST])
            m.then_inc(s_histT, 1)
            pe.wait_ge(s_hlo, TILES)

            def product(bank, w, s, hi, lo, K, c):
                for k in range(K):
                    for q, (a, r) in enumerate(((w_hi, hi), (w_hi, lo), (w_lo, hi))):
                        m = pe.matmul(ps[:, bank, 0:CH], a[:, s, w + k, :], r[:, w + k, c * CH:(c + 1) * CH],
                                      start=(k == 0 and q == 0), stop=(k == K - 1 and q == 2))
                return m

            def panel(n, half, s, hi, lo, K):
                pe.wait_ge(s_whi, n + 1)
                pe.wait_ge(s_wlo, n + 1)
                if half is not None:
                    pe.wait_ge(s_free[s], half)
                for c in range(CHUNKS):
                    product(3 * s + c, 0, s, hi, lo, K, c).then_inc(s_mm, 1)

            def tails(src, n, starts):
                for q in range(2):
                    for g in range(GR):
                        m = pe.transpose(ps[0:n, 6 + q, g * P:(g + 1) * P], src[:, g, starts[q]:starts[q] + n], ident[:])
                m.then_inc(s_sT, 1)

            for s in range(2):
                panel(s, None, s, h_hi, h_lo, KD)
            for s in range(2):
                panel(2 + s, 1, s, h_hi, h_lo, KD)
            pe.wait_ge(s_free[0], NU // 2)
            pe.wait_ge(s_free[1], NU // 2)
            pe.wait_ge(s_histC, 1)
            tails(U, PH, (SEQ, UW - PH))
            with pe.Fori(NU // 2, NG // 2) as i:
                for s in range(2):
                    panel(2 * i + s, i, s, h_hi, h_lo, KD)
            pe.wait_ge(s_free[0], NG // 2)
            pe.wait_ge(s_free[1], NG // 2)
            pe.wait_ge(s_sC, 1)
            tails(V, HIST, (SEQ, VW - HIST))
            pe.wait_ge(s_whi, NG + 1)
            pe.wait_ge(s_wlo, NG + 1)
            for g in range(GR):
                pe.wait_ge(s_diff, g + 1)
                if g >= 2:
                    pe.wait_ge(s_ylo, g - 1)
                for c in range(CHUNKS):
                    m = product(3 * (g % 2) + c, g, 0, d_hi, d_lo, 1, c)
                m.then_inc(s_grp, 1)
            pe.sem_inc(s_mm, 3)
            pe.wait_ge(s_ylo, GR)
            with pe.Fori(0, KD - 1) as j:
                panel(NB + 2 * j, NG // 2 + j, 1, h_hi, h_lo, KD)
                panel(NB + 1 + 2 * j, NG // 2 + 1 + j, 0, y_hi, y_lo, GR)

            def ln_sum(src, bank, p, s_done):
                w = LN_PIECES[p][1]
                for g in range(GR):
                    m = pe.matmul(ps[:, bank, 0:w], ln_mean[:], src(g), start=(g == 0), stop=(g == GR - 1))
                m.then_inc(s_done, 1)

            def mean(p):
                a, w = LN_PIECES[p]
                wait(pe, s_cen, p)
                ln_sum(lambda g: C[:, g, a:a + w], 6, p, s_mean)

            def variance(p):
                w = LN_PIECES[p][1]
                pe.wait_ge(s_csq, p + 1)
                wait(pe, s_lstd, p)
                ln_sum(lambda g: ln_sq[:, g, 0:w], 7, p, s_var)

            n = NC - 2
            panel(n, NG // 2 + KD - 1, 1, h_hi, h_lo, KD)
            pe.wait_ge(s_conv, CW * GR)
            mean(0)
            between = {(NC - 1, 0): (0, 1), (NC - 1, 2): (1, 2), (NC, 0): (2, 3), (NC, 1): (3, None)}
            for n, s, a, r_hi, r_lo, K in ((NC - 1, 0, NC // 2, y_hi, y_lo, GR), (NC, 1, NC // 2, h_hi, h_lo, KD)):
                pe.wait_ge(s_whi, n + 1)
                pe.wait_ge(s_wlo, n + 1)
                pe.wait_ge(s_free[s], a)
                for c in range(CHUNKS):
                    product(3 * s + c, 0, s, r_hi, r_lo, K, c).then_inc(s_mm, 1)
                    v, m = between.get((n, c), (None, None))
                    if v is not None:
                        variance(v)
                    if m is not None:
                        mean(m)
            assert len(LN_PIECES) == 4
            pe.wait_ge(s_alo, len(LN_PIECES))
            panel(NC + 1, NC // 2 + 1, 0, a_hi, a_lo, GR)
            with pe.Fori(1, KD) as j:
                panel(NC + 2 * j, NC // 2 + j, 1, h_hi, h_lo, KD)
                panel(NC + 1 + 2 * j, NC // 2 + 1 + j, 0, a_hi, a_lo, GR)
            pe.wait_ge(s_free[1], NP // 2)

            def h2_turn(t):
                n = P if t < TILES - 1 else LAST
                pe.wait_ge(s_h2, t + 1)
                wait(pe, s_h2c, t)
                for c in range(KD):
                    m = pe.transpose(ps[:, 4 + c // 4, (c % 4) * P:(c % 4) * P + n], h2[0:n, t % 2, c * P:(c + 1) * P],
                                     ident[0:n, 0:n])
                m.then_inc(s_h2T, 1)

            def logits(t):
                n = P if t < TILES - 1 else LAST
                pe.wait_ge(s_h2c, t + 1)
                for c in range(KD):
                    m = pe.matmul(ps[0:n, 6, t * NR:(t + 1) * NR], h2T[:, t % 2, c, 0:n], w_r[:, c, :],
                                  start=(c == 0), stop=(c == KD - 1))
                m.then_inc(s_lg, 1)

            for n in range(2 * TILES):
                h, t = divmod(n, TILES)
                if t == 0:
                    pe.wait_ge(s_wohi, 4 * h + 4)
                    pe.wait_ge(s_wolo, 4 * h + 4)
                if n == 1:
                    pe.wait_ge(s_free[0], (NP + 1) // 2)
                if n >= 4:
                    pe.wait_ge(s_res, n - 3)
                for k in range(KD):
                    if n == 0:
                        pe.wait_ge(s_mhi, k + 1)
                        pe.wait_ge(s_mlo, k + 1)
                    o = k * T + t * P
                    hi, lo = hT[:, o:o + P], hT[:, HT + o:HT + o + P]
                    for q, (a, w) in enumerate(((hi, wo_hi), (lo, wo_hi), (hi, wo_lo))):
                        m = pe.matmul(ps[:, (n + 3) % 4, :], a, w[h][:, k, :], start=(k == 0 and q == 0),
                                      stop=(k == KD - 1 and q == 2))
                m.then_inc(s_o, 1)
                if h == 1 and t >= 1:
                    h2_turn(t - 1)
                if h == 1 and t >= 2:
                    logits(t - 2)
            logits(TILES - 2)
            h2_turn(TILES - 1)
            logits(TILES - 1)
            pe.wait_ge(s_cum, 1)
            aflat = A[:].rearrange("p t e -> p (t e)")
            pe.matmul(ps[:, 7, 0:TILES * GE], tri_b[:], aflat, start=True, stop=False)
            for t in range(TILES - 1):
                rest = TILES - 1 - t
                pe.matmul(ps[:, 7, (t + 1) * GE:TILES * GE].rearrange("p (t e) -> p t e", e=GE), one_b[:],
                          A[:, t:t + 1, :].to_broadcast((P, rest, GE)), start=False, stop=(rest == 1))
            for t in range(TILES):
                m = pe.matmul(ps[:, 5, 0:GE], one_b[:], A[:, t, :], start=(t == 0), stop=(t == TILES - 1))
            m.then_inc(s_rk, 1)

            def x_turn(it, u, quarter):
                pe.wait_ge(s_xg[u], 16 * (quarter + 1))
                wait(pe, s_xtA, it)
                wait(pe, s_xtD, it)
                for c in range(KD):
                    r = P if c == 0 else CAP
                    m = pe.transpose(ps[:, c // 4, (c % 4) * P:(c % 4) * P + r], X[0:r, u, c * P:(c + 1) * P], ident[0:r, 0:r])
                m.then_inc(s_tx, 1)

            def down(it, u):
                b = u % 2
                pe.wait_ge(s_act, it + 1)
                wait(pe, s_yA, it - 1)
                wait(pe, s_yD, it - 1)
                for h in range(2):
                    for c in range(KF):
                        m = pe.matmul(ps[0:CAP, 4 + 2 * b + h, :], AT[:, b, c, 0:CAP],
                                      wdn[u][:, c, h * 512:(h + 1) * 512], start=(c == 0), stop=(c == KF - 1))
                m.then_inc(s_down, 1)

            def step(p, i, u):
                it = p * GE + i * WB + u
                b = u % 2
                pe.wait_ge(s_xtA, it + 1)
                pe.wait_ge(s_xtD, it + 1)
                wait(pe, s_act, it - 1)
                pe.wait_ge(s_wl[u], 48 * (p * (GE // WB) + i + 1))
                for h in range(2):
                    for f in range(KF):
                        o = (h * KF + f) * CAP
                        for c in range(KD):
                            m = pe.matmul(ps[:, 2 + b, o:o + CAP], wgu[u][:, h, c, f * P:(f + 1) * P], XT[:, b, c, 0:CAP],
                                          start=(c == 0), stop=(c == KD - 1))
                m.then_inc(s_gu, 1)
                if not (isinstance(i, int) and i == GE // WB - 1 and u == WB - 1):
                    x_turn(it + 1, (u + 1) % WB, p * (GE // WB) + i + (u + 1) // WB)
                if not (isinstance(i, int) and i == 0 and u == 0):
                    down(it - 1, (u - 1) % WB)

            def one(p):
                pe.wait_ge(s_where, p + 1)
                for t in range(TILES):
                    for k in range(2):
                        m = pe.matmul(ps[0:CAP, 7, 0:2 * GE], where[:, t, k, :], slot_rows[:, k, t].rearrange("p h e -> p (h e)"),
                                      start=(t + k == 0), stop=(t == TILES - 1 and k == 1))
                m.then_inc(s_rows, 1)
                x_turn(p * GE, 0, p * (GE // WB))
                groups(pe, step, p)
                down(p * GE + GE - 1, WB - 1)

            rounds(pe, one)


_INS = ['x_prompt', 'x_sample', 'state_pool', 'state_conv', 'g_mix', 'w_in', 'w_pool_grp', 'pool_scale',
        'w_pool_out', 'w_dw', 'b_dw', 'ln_g', 'ln_b', 'w_conv_out', 'w_out', 'g_ffn', 'w_rg', 'b_rg', 'w_re',
        'b_re', 'w_gate', 'w_up', 'w_down', 'g_final']
_OUTS = [('y_prompt', (1, SEQ, D)), ('y_sample', (1, DEC, D)), ('new_pool_prompt', (1, 1, PH, D_POOL)),
         ('new_conv_prompt', (1, 1, HIST, D_CONV)), ('new_pool_sample', (1, 1, PH, D_POOL)),
         ('new_conv_sample', (1, 1, HIST, D_CONV))]


def kernel(**inputs):
    import numpy as _np
    import concourse.bacc as _bacc
    from concourse.bass_utils import run_bass_kernel_spmd as _run

    nc = _bacc.Bacc("TRN2", target_bir_lowering=False, num_devices=1)
    arrays, ins, outs = {}, {}, {}
    for name in _INS:
        a = _np.ascontiguousarray(inputs[name])
        arrays[f"in_{name}"] = a
        ins[name] = nc.dram_tensor(f"in_{name}", a.shape, mybir.dt.from_np(a.dtype), kind="ExternalInput").ap()
    for name, shape in _OUTS:
        outs[name] = nc.dram_tensor(f"out_{name}", shape, F32, kind="ExternalOutput").ap()
    build(nc, ins, outs)
    r = _run(nc, [arrays], core_ids=[0])
    return tuple(r.results[0][f"out_{name}"] for name, _ in _OUTS)
```

```python
from contextlib import ExitStack

import concourse.bass as bass
from concourse import mybir

ACT = mybir.ActivationFunctionType
ALU = mybir.AluOpType
AX = mybir.AxisListType
F32 = mybir.dt.float32
F32R = mybir.dt.float32r
BF16 = mybir.dt.bfloat16
U32 = mybir.dt.uint32
I32 = mybir.dt.int32

P = 128
D = 1024
KD = D // P
SEQ = 1024
DEC = 32
LN_W = 272
T = SEQ + DEC
TILES = (T + P - 1) // P
LAST = T - (TILES - 1) * P
XS, XN = 4, 3
CH = T // 3
CHUNKS = 3
D_POOL = 512
D_CONV = 512
GR = D_POOL // P
PH = 15
CW = 31
HIST = CW - 1
UW = PH + SEQ + PH + DEC
VW = HIST + SEQ + HIST + DEC
CWID = SEQ + HIST + DEC
G = 4
E = 8
GE = G * E
F = 256
KF = F // P
NR = G + GE
CAP = 104
PASSES = (T + CAP - 1) // CAP
NOWHERE = 1.0e6
WB = 4
RMS_EPS = 1e-6
LN_EPS = 1e-5


def build(nc, I, O):
    with ExitStack() as ctx:
        def sem(name):
            return ctx.enter_context(nc.semaphore(name))

        cursor = [16512]

        def region(nbytes):
            o = cursor[0]
            cursor[0] += (nbytes + 31) // 32 * 32
            assert cursor[0] <= 229344, cursor
            return o

        def at(name, shape, dt, offset):
            return nc.alloc_sbuf_tensor_at(name, shape, dt, offset=offset)

        def small(name, shape, dt=F32):
            n = 4
            for s in shape[1:]:
                n *= s
            return at(name, shape, dt, region(n))

        HT = KD * T
        r_h = region((2 * HT + P - DEC) * 4)
        r_m = region(max(KD * T, TILES * D) * 4)
        r_uv = region(GR * (UW + VW) * 4)
        r_yp = region(2 * GR * T * 4)
        r_w = region(6 * KD * P * 4)
        r_s = region(2 * T * 4)
        r_wo = region(KD * P * 4)

        hT = at("hT", [P, 2 * HT + P - DEC], F32R, r_h)
        h_hi = hT[:, 0:HT].rearrange("p (k t) -> p k t", k=KD)
        h_lo = hT[:, HT:2 * HT].rearrange("p (k t) -> p k t", k=KD)

        U = at("U", [P, GR, UW], F32, r_uv)
        V = at("V", [P, GR, VW], F32, r_uv + GR * UW * 4)
        C = at("C", [P, GR, CWID], F32, r_uv)

        xs = at("xs", [P, XS, D], F32, r_yp)
        xn = at("xn", [P, XN, D], F32, r_yp + XS * D * 4)
        g_mix_b = at("g_mix_b", [P, D], F32, r_yp + (XS + XN) * D * 4)
        squares = at("squares", [P, D], F32, r_s)
        first_root = at("first_root", [P, 1], F32, r_s + 2 * D * 4)

        w_raw = at("w_raw", [P, 2, KD, P], F32, r_w)
        w_hi = at("w_hi", [P, 2, KD, P], F32R, r_w + 2 * KD * P * 4)
        w_lo = at("w_lo", [P, 2, KD, P], F32R, r_w + 4 * KD * P * 4)

        hist_in = at("hist_in", [CW, 3, D_CONV], F32, r_m)
        vec_in = at("vec_in", [4 * GR, P], F32, r_m + 3 * D_CONV * 4)
        win = at("win", [P, 2, UW], F32, r_yp)
        diff = at("diff", [P, T], F32, r_yp + (8 * UW + 31) // 32 * 32)
        d_hi = at("d_hi", [P, GR, T], F32R, r_m)
        d_lo = at("d_lo", [P, GR, T], F32R, r_m + GR * T * 4)
        y_hi = at("y_hi", [P, GR, T], F32R, r_yp)
        y_lo = at("y_lo", [P, GR, T], F32R, r_yp + GR * T * 4)
        a_hi = at("a_hi", [P, GR, T], F32R, r_uv + GR * UW * 4)
        a_lo = at("a_lo", [P, GR, CWID], F32R, r_uv)
        M = at("M", [P, KD, T], F32, r_m)
        x1 = at("x1", [P, TILES, D], F32, r_m)
        S = at("S", [P, 2, T], F32, r_s)
        r_v = r_uv + GR * UW * 4
        ln_sq = at("ln_sq", [P, GR, T], F32, r_v)[:, :, SEQ - LN_W:SEQ]
        ln_rstd = at("ln_rstd", [P, LN_W], F32, r_v + (GR * VW - LN_W) * 4)
        xr = at("xr", [P, 2, 512], F32, r_s)
        wo_raw = at("wo_raw", [P, 2, 512], F32, r_wo)
        wo_hi = [at("wo_hi0", [P, KD, 512], F32R, r_yp), at("wo_hi1", [P, KD, 512], F32R, r_uv)]
        wo_lo = [at("wo_lo0", [P, KD, 512], F32R, r_yp + KD * 2048), at("wo_lo1", [P, KD, 512], F32R, r_uv + KD * 2048)]
        state_out = at("state_out", [32, 4, D_CONV], F32, r_s)

        ident = small("ident", [P, P])
        w_dw = small("w_dw", [P, GR, CW])
        vecs = small("vecs", [P, 4 * GR])
        ln_mean = small("ln_mean", [P, P])
        inv_cnt = small("inv_cnt", [P, 16])
        eps_ln = small("eps_ln", [P, 1])
        sumsq = small("sumsq", [P, TILES])
        rstd = small("rstd", [P, TILES])
        eps_rms = small("eps_rms", [P, 1])

        h2 = at("h2", [P, 2, D], F32, r_w)
        h2T = at("h2T", [P, 2, KD, P], F32, r_w + 8192)
        g_ffn_b = at("g_ffn_b", [P, D], F32, r_w + 16384)
        w_r = at("w_r", [P, KD, NR], F32, r_w + 20480)
        b_r = at("b_r", [P, NR], F32, r_w + 21632)
        L = at("L", [P, TILES, NR], F32, r_w + 21792)
        squares2 = at("squares2", [P, D], F32, r_s + 4096)
        cur = [r_wo]

        def const(name, shape, dt=F32, start=None):
            if start is not None:
                cur[0] = start
            n = 2 if dt is BF16 else 4
            for v in shape[1:]:
                n *= v
            o = cur[0]
            cur[0] += (n + 31) // 32 * 32
            return at(name, shape, dt, o)

        tri = const("tri", [P, P], start=r_wo)
        io_i = const("io_i", [P, GE], I32)
        io = const("io", [P, GE])
        thr = const("thr", [P, PASSES - 1])
        tri_b = const("tri_b", [P, P], BF16)
        one_b = const("one_b", [P, P], BF16)
        row_i = const("row_i", [P, TILES, 2], I32)
        row_f = const("row_f", [P, TILES, 2])
        row_hi = const("row_hi", [P, TILES, 2], BF16)
        row_lo = const("row_lo", [P, TILES, 2])
        slot_i = const("slot_i", [P, CAP], I32)
        valid = const("valid", [P, 1])
        assert cur[0] <= r_wo + 4096
        N9 = [P, TILES]
        gmax = const("gmax", N9, start=r_w + 8192)
        gmin = const("gmin", N9)
        zsum = const("zsum", N9)
        m1 = const("m1", N9)
        m2 = const("m2", N9)
        ex = const("ex", N9)
        den = const("den", N9)
        rank = const("rank", [P, TILES, 2])
        tg = const("tg", [P, TILES, G])
        og = const("og", [P, TILES, G])
        dg = const("dg", [P, TILES, G])
        les = const("les", [P, TILES, E])
        te = const("te", [P, TILES, E])
        oe = [const("oe0", [P, TILES, E]), const("oe1", [P, TILES, E])]
        ge8 = const("ge8", [P, PASSES - 1])
        nmax = const("nmax", [P, 1])
        np_f = const("np_f", [P, 1])
        assert cur[0] <= r_w + 12288
        slot_rows = const("slot_rows", [P, 2, TILES, 2, GE], BF16, start=r_s)
        Ek = [const("Ek0", [P, TILES, G, E]), const("Ek1", [P, TILES, G, E])]
        A = const("A", [P, TILES, GE], BF16)
        tmp32 = const("tmp32", [P, TILES, G, E])
        assert cur[0] <= r_s + 8448
        w_off = [r_yp, r_h, r_h + 24576, r_uv]
        wgu = [at(f"wgu{u}", [P, 2, KD, F], F32, w_off[u]) for u in range(WB)]
        wdn = [at(f"wdn{u}", [P, KF, D], F32, w_off[u] + 16384) for u in range(WB)]
        X = at("X", [P, 4, D], F32, r_h + 49152)
        Y = [at(f"Y{u}", [P, D], F32, o) for u, o in enumerate((r_uv + 24576, r_uv + 28672, r_s + 4352, r_wo))]
        XT = at("XT", [P, 2, KD, P], F32, r_yp + 24576)
        where = at("where", [P, 2, TILES, CAP], BF16, r_yp + 24576)
        sg = at("sg", [P, 2, KF, P], F32, r_w)
        AT_hi = at("AT_hi", [P, 2, KF, P], F32R, r_w + 2048)
        AT_lo = at("AT_lo", [P, 2, KF, P], F32R, r_w + 4096)
        AT = at("AT", [P, KF, P], F32, r_w + 6144)
        wdn_hi = [at("wdn_hi0", [P, D], F32R, r_w + 20480), at("wdn_hi1", [P, D], F32R, r_w + 12288)]
        wdn_lo = [at(f"wdn_lo{u}", [P, KF, D], F32R, w_off[u] + 16384) for u in range(WB)]
        yy = at("yy", [P, TILES, 2, D], F32, r_uv)
        assert r_uv + TILES * 2 * D * 4 <= r_w + 24576
        wts = const("wts", [P, TILES, 2], start=r_h + 65536)
        g_idx = const("g_idx", [P, GE])
        wrap = const("wrap", [P, GE])
        found = const("found", [P, GE])
        s_idx = const("s_idx", [P, GE])
        slot_f = const("slot_f", [P, CAP])
        g_now = const("g_now", [P, 4], U32)
        s_now = const("s_now", [P, WB], U32)
        np_i = const("np_i", [P, 1], I32)
        assert cur[0] <= r_m
        g_fin_b = at("g_fin_b", [P, D], F32, r_w + 16384)
        sq3 = at("sq3", [P, 2, D], F32, r_s)

        H2 = nc.dram_tensor("H2", (T, D), F32, kind="Internal").ap()
        YK = nc.dram_tensor("YK", (2 * T, D), F32, kind="Internal").ap()

        ps = ctx.enter_context(nc.psum_tensor("ps", [P, 8, 512], F32))

        s_const = sem("s_const")
        s_x = [sem(f"s_x{b}") for b in range(XS)]
        s_w = [sem("s_w0"), sem("s_w1")]
        s_hist = sem("s_hist")
        s_ident = sem("s_ident")
        s_eps = sem("s_eps")
        s_zero = sem("s_zero")
        s_std = sem("s_std")
        s_sq = sem("s_sq")
        s_rstd = sem("s_rstd")
        s_xn = sem("s_xn")
        s_xT = sem("s_xT")
        s_hhi = sem("s_hhi")
        s_hlo = sem("s_hlo")
        s_histT = sem("s_histT")
        s_histC = sem("s_histC")
        s_whi = sem("s_whi")
        s_wlo = sem("s_wlo")
        s_mm = sem("s_mm")
        s_free = [sem("s_free0"), sem("s_free1")]
        s_sT = sem("s_sT")
        s_sC = sem("s_sC")
        s_out = sem("s_out")
        s_tail = sem("s_tail")
        s_pool = sem("s_pool")
        s_diff = sem("s_diff")
        s_conv = sem("s_conv")
        s_grp = sem("s_grp")
        s_yhi = sem("s_yhi")
        s_ylo = sem("s_ylo")
        s_mean = sem("s_mean")
        s_cen = sem("s_cen")
        s_csq = sem("s_csq")
        s_var = sem("s_var")
        s_lstd = sem("s_lstd")
        s_lrec = sem("s_lrec")
        s_norm = sem("s_norm")
        s_silu = sem("s_silu")
        s_ahi = sem("s_ahi")
        s_alo = sem("s_alo")
        s_sy = sem("s_sy")
        s_mhi = sem("s_mhi")
        s_mlo = sem("s_mlo")
        s_wo = sem("s_wo")
        s_wohi = sem("s_wohi")
        s_wolo = sem("s_wolo")
        s_o = sem("s_o")
        s_xr = [sem("s_xr0"), sem("s_xr1")]
        s_res = sem("s_res")
        s_rc = sem("s_rc")
        s_sq2 = sem("s_sq2")
        s_std2 = sem("s_std2")
        s_rs2 = sem("s_rs2")
        s_h2 = sem("s_h2")
        s_h2st = [sem("s_h2st0"), sem("s_h2st1")]
        s_h2T = sem("s_h2T")
        s_h2c = sem("s_h2c")
        s_lg = sem("s_lg")
        s_rt = sem("s_rt")
        s_ra = sem("s_ra")
        s_re = sem("s_re")
        s_cum = sem("s_cum")
        s_rk = sem("s_rk")
        s_np = sem("s_np")
        s_where = sem("s_where")
        s_rows = sem("s_rows")
        s_prep = sem("s_prep")
        s_tx = sem("s_tx")
        s_xtA = sem("s_xtA")
        s_xtD = sem("s_xtD")
        s_gu = sem("s_gu")
        s_sg = sem("s_sg")
        s_act = sem("s_act")
        s_prod = sem("s_prod")
        s_athi = sem("s_athi")
        s_dnhi = sem("s_dnhi")
        s_dnlo = sem("s_dnlo")
        s_down = sem("s_down")
        s_yA = sem("s_yA")
        s_yD = sem("s_yD")
        s_gc = sem("s_gc")
        s_f1 = sem("s_f1")
        s_gfin = sem("s_gfin")
        s_fq = sem("s_fq")
        s_fs = sem("s_fs")
        s_fr = sem("s_fr")
        s_fa = sem("s_fa")
        s_fo = sem("s_fo")
        s_tri = sem("s_tri")
        s_ct = sem("s_ct")
        s_wl = [sem(f"s_wl{u}") for u in range(WB)]
        s_xg = [sem(f"s_xg{u}") for u in range(4)]
        s_ys = [sem(f"s_ys{u}") for u in range(WB)]
        s_yy = [sem(f"s_yy{t}") for t in range(TILES)]
        s_fx = sem("s_fx")

        w_in_v = I["w_in"][0].rearrange("(k p) m -> p k m", p=P)
        xp = I["x_prompt"][0]
        block = ctx.enter_context(nc.Block())

        def x_rows(t):
            return (xp[t * P:(t + 1) * P, :], P) if t < TILES - 1 else (I["x_sample"][0], LAST)

        def wait(eng, s, v):
            if not isinstance(v, int) or v > 0:
                eng.wait_ge(s, v)

        def groups(eng, step, p):
            for i in range(2):
                for u in range(WB):
                    step(p, i, u)
            with eng.Fori(2, GE // WB - 1) as i:
                for u in range(WB):
                    step(p, i, u)
            for u in range(WB):
                step(p, GE // WB - 1, u)

        def rounds(eng, one):
            one(0)
            eng.wait_ge(s_np, 1)
            n = eng.value_load(np_i[0:1, 0:1], min_val=1, max_val=PASSES)
            with eng.If(n > 1):
                with eng.Fori(1, n) as p:
                    one(p)
            return n

        def runs(c, hist):
            a, b = c * CH, (c + 1) * CH
            out = []
            if a < SEQ:
                e = min(b, SEQ)
                out.append((0, hist + a, e - a))
            if b > SEQ:
                s = max(a, SEQ)
                out.append((s - a, 2 * hist + s, b - s))
            return out

        def turned(t, q, n):
            bank = (2 * t if t < 3 else 6) + q
            return ps[:, bank, :].rearrange("p (k t) -> p k t", k=4)[:, :, 0:n]

        NU, NV = GR, 2 * GR
        NG = NU + NV
        NB = NG + 1
        NC = NB + 2 * KD
        NP = NC + 2 * KD
        GATE_P = D_POOL + 2 * D_CONV
        GATE_C = GATE_P + D
        A_TAPS = 11
        B_TAPS = (3, 2)
        assert A_TAPS + sum(B_TAPS) * KD // 2 == CW
        w_po_v = I["w_pool_out"][0].rearrange("(k p) m -> p k m", p=P)
        w_co_v = I["w_conv_out"][0].rearrange("(k p) m -> p k m", p=P)
        w_out_v = I["w_out"][0].rearrange("(k p) m -> p k m", p=P)
        LN_PIECES = [(a, min(LN_W, CWID - a)) for a in range(0, CWID, LN_W)]
        BIAS, LN_G, LN_B, SCALE = 0, GR, 2 * GR, 3 * GR

        @block.sync
        def _(sp):
            def first_weights(s):
                sp.dma_start(w_raw[:, s], w_in_v[:, :, s * P:(s + 1) * P]).then_inc(s_w[s], 16)

            for t in range(TILES):
                src, n = x_rows(t)
                if t >= XS:
                    sp.wait_ge(s_xn, t - XS + 1)
                sp.dma_start(xs[0:n, t % XS, :], src).then_inc(s_x[t % XS], 16)
                if t == 0:
                    sp.dma_start(g_mix_b[:], I["g_mix"][0].partition_broadcast(P)).then_inc(s_const, 16)
                if t in (2, 3):
                    first_weights(t - 2)
                if t == XS:
                    for q, v in enumerate(("b_dw", "ln_g", "ln_b", "pool_scale")):
                        sp.dma_start(vec_in[q * GR:(q + 1) * GR, :],
                                     I[v][0].rearrange("(g p) -> g p", p=P)).then_inc(s_hist, 16)
                    sp.dma_start(hist_in[:, 2, :], I["w_dw"][0]).then_inc(s_hist, 16)
                    sp.dma_start(hist_in[0:PH, 0, :], I["state_pool"][0, 0]).then_inc(s_hist, 16)
                    sp.dma_start(hist_in[0:HIST, 1, :], I["state_conv"][0, 0]).then_inc(s_hist, 16)

            def panel(n, s, col, src=w_in_v, K=KD):
                sp.wait_ge(s_wlo, n - 1)
                sp.dma_start(w_raw[:, s, 0:K], src[:, :, bass.ds(col, P)]).then_inc(s_w[s], 16)

            panel(2, 0, 2 * P)
            panel(3, 1, 3 * P)
            with sp.Fori(1, GR + 1) as j:
                panel(NU - 2 + 2 * j, 0, 2 * GR * P - P + j * P)
                panel(NU - 1 + 2 * j, 1, GR * P - P + j * P)
            sp.wait_ge(s_whi, NG - 1)
            sp.wait_ge(s_wlo, NG - 1)
            sp.dma_start(w_raw[:, 0, 0:GR], I["w_pool_grp"][0].rearrange("g c d -> c g d")).then_inc(s_w[0], 16)
            sp.wait_ge(s_sC, 1)
            sp.dma_start(O["new_pool_prompt"][0, 0], state_out[0:PH, 0, :]).then_inc(s_tail, 16)
            sp.dma_start(O["new_pool_sample"][0, 0], state_out[0:PH, 1, :]).then_inc(s_tail, 16)
            with sp.Fori(1, KD + 1) as j:
                panel(NB - 2 + 2 * j, 1, GATE_P - P + j * P)
                panel(NB - 1 + 2 * j, 0, j * P - P, w_po_v, GR)
                with sp.If(j < 2):
                    sp.wait_ge(s_sC, 2)
                    sp.dma_start(O["new_conv_prompt"][0, 0], state_out[0:HIST, 2, :]).then_inc(s_tail, 16)
                    sp.dma_start(O["new_conv_sample"][0, 0], state_out[0:HIST, 3, :]).then_inc(s_tail, 16)

            def wo_quarter(h, q):
                n = 4 * h + q - 1
                sp.wait_ge(s_wolo, n)
                sp.dma_start(wo_raw[:], w_out_v[:, bass.ds(2 * q - 2, 2), h * 512:(h + 1) * 512]).then_inc(s_wo, 16)

            with sp.Fori(1, KD // 2 + 1) as i:
                for jj in range(2):
                    j = 2 * i + jj - 1
                    panel(NC - 2 + 2 * j, 1, GATE_C - P + j * P)
                    panel(NC - 1 + 2 * j, 0, j * P - P, w_co_v, GR)
                wo_quarter(0, i)
            wo_quarter(1, 1)
            sp.wait_ge(s_free[0], (NP + 1) // 2)
            sp.dma_start(g_ffn_b[:], I["g_ffn"][0].partition_broadcast(P)).then_inc(s_rc, 16)
            sp.dma_start(w_r[:, :, 0:G], I["w_rg"][0].rearrange("(p c) g -> p c g", p=P)).then_inc(s_rc, 16)
            sp.dma_start(w_r[:, :, G:NR], I["w_re"][0].rearrange("(p c) g -> p c g", p=P)).then_inc(s_rc, 16)
            sp.dma_start(b_r[:, 0:G], I["b_rg"][0].partition_broadcast(P)).then_inc(s_rc, 16)
            sp.dma_start(b_r[:, G:NR], I["b_re"][0].partition_broadcast(P)).then_inc(s_rc, 16)

            def h2_store(t):
                n = P if t < TILES - 1 else LAST
                sp.wait_ge(s_h2, t + 1)
                sp.dma_start(H2[t * P:t * P + n, :], h2[0:n, t % 2, :]).then_inc(s_h2st[t % 2], 16)

            def store(t):
                n = P if t < TILES - 1 else LAST
                dst = O["y_prompt"][0, t * P:(t + 1) * P, :] if t < TILES - 1 else O["y_sample"][0]
                sp.wait_ge(s_fo, t + 1)
                sp.dma_start(dst, x1[0:n, t, :]).then_inc(s_out, 16)

            gate_v = I["w_gate"][0].rearrange("g e (p c) f -> (g e) p c f", p=P)
            up_v = I["w_up"][0].rearrange("g e (p c) f -> (g e) p c f", p=P)
            down_v = I["w_down"][0].rearrange("g e (c p) d -> (g e) p c d", p=P)

            def load(e, it, u, part=None):
                parts = ((gate_v, wgu[u][:, 0], s_gu), (up_v, wgu[u][:, 1], s_gu), (down_v, wdn[u][:], s_down))
                for src, dst, s_used in parts if part is None else parts[part:part + 1]:
                    if part is None:
                        wait(sp, s_used, it - WB + 1)
                    s1 = src[e] if isinstance(e, int) else src[bass.ds(e, 1)].rearrange("a p k f -> (a p) k f")
                    sp.dma_start(dst, s1).then_inc(s_wl[u], 16)

            for n in range(2 * TILES):
                h, t = divmod(n, TILES)
                src, rows = x_rows(t)
                if n >= 2:
                    sp.wait_ge(s_res, n - 1)
                sp.dma_start(xr[0:rows, n % 2, :], src[:, h * 512:(h + 1) * 512]).then_inc(s_xr[n % 2], 16)
                if 1 <= n < 4:
                    wo_quarter(1, n + 1)
                if h == 1 and t >= 2:
                    h2_store(t - 2)
                    if t % 2 == 0:
                        if t == 2:
                            sp.wait_ge(s_o, TILES)
                        if t < 8:
                            load(0, 0, 0, t // 2 - 1)
            h2_store(TILES - 2)
            h2_store(TILES - 1)
            sp.wait_ge(s_o, 2 * TILES)
            for u in range(1, WB - 1):
                load(u, u, u)
            load(WB - 1, 0, WB - 1, 0)
            sp.wait_ge(s_xg[1], 16)
            for part in (1, 2):
                load(WB - 1, 0, WB - 1, part)
            sp.dma_start(g_fin_b[:], I["g_final"].partition_broadcast(P)).then_inc(s_gfin, 16)
            with sp.Fori(1, GE // WB) as i:
                for u in range(WB):
                    load(i * WB + u, i * WB + u, u)
            sp.wait_ge(s_np, 1)
            n_pass = sp.value_load(np_i[0:1, 0:1], min_val=1, max_val=PASSES)
            with sp.If(n_pass > 1):
                with sp.Fori(1, n_pass) as p:
                    with sp.Fori(0, GE // WB) as i:
                        for u in range(WB):
                            load(i * WB + u, p * GE + i * WB + u, u)
            for u in range(WB):
                sp.wait_ge(s_ys[u], n_pass * (16 * (GE // WB)))
            for t in range(TILES):
                n = P if t < TILES - 1 else LAST
                sp.dma_start(yy[0:n, t], YK.rearrange("(k t) d -> t k d", k=2)[t * P:t * P + n]).then_inc(s_yy[t], 16)
            for t in range(TILES):
                store(t)
            sp.wait_ge(s_out, 16 * TILES)
            sp.wait_ge(s_tail, 64)

        @block.gpsimd
        def _(pool):
            pool.memset(ident[:], 0.0).then_inc(s_zero, 1)
            pool.wait_ge(s_zero, 1)
            pool.affine_select(out=ident[:], in_=ident[:], compare_op=ALU.not_equal, fill=1.0,
                               base=0, pattern=[[-1, P]], channel_multiplier=1).then_inc(s_ident, 1)
            pool.memset(eps_rms[:], RMS_EPS).then_inc(s_eps, 1)
            pool.memset(U[:, :, 0:PH], 0.0)
            pool.memset(V[:, :, 0:HIST], 0.0).then_inc(s_ident, 1)
            pool.memset(eps_ln[:], LN_EPS)
            pool.memset(ln_mean[:], 1.0 / D_CONV).then_inc(s_ident, 1)
            for c in range(16):
                pool.memset(inv_cnt[:, c:c + 1], 1.0 / (c + 1))

            pool.wait_ge(s_hlo, TILES)
            pool.wait_ge(s_free[0], NU // 2)
            pool.wait_ge(s_free[1], NU // 2)
            pool.wait_ge(s_histC, 1)
            done = [0]

            def link(op):
                done[0] += 1
                op.then_inc(s_pool, 1)
                pool.wait_ge(s_pool, done[0])

            for g in range(GR):
                w = 2 << g
                src = U[:, g, :]
                for k in range(g + 1):
                    lag, lo = 1 << k, (2 << k) - 1
                    link(pool.tensor_tensor(win[:, k % 2, lo:UW], src[:, lo:UW], src[:, lo - lag:UW - lag], ALU.add))
                    src = win[:, k % 2, :]
                link(pool.tensor_tensor(diff[:, 0:w - 1], src[:, PH:PH + w - 1], inv_cnt[:, 0:w - 1], ALU.mult))
                pool.tensor_scalar(diff[:, w - 1:SEQ], src[:, PH + w - 1:PH + SEQ], 1.0 / w, None, ALU.mult)
                link(pool.tensor_scalar(diff[:, SEQ:T], src[:, UW - DEC:UW], 1.0 / w, None, ALU.mult))
                pool.tensor_tensor(diff[:, 0:SEQ], diff[:, 0:SEQ], U[:, g, PH:PH + SEQ], ALU.subtract)
                link(pool.tensor_tensor(diff[:, SEQ:T], diff[:, SEQ:T], U[:, g, UW - DEC:UW], ALU.subtract))
                link(pool.tensor_copy(d_hi[:, g, :], diff[:]))
                link(pool.tensor_tensor(d_lo[:, g, :], diff[:], d_hi[:, g, :].bitcast(F32), ALU.subtract))
                pool.sem_inc(s_diff, 1)

            def split_lo(n, s, K):
                pool.wait_ge(s_whi, n + 1)
                pool.tensor_tensor(w_lo[:, s, 0:K], w_raw[:, s, 0:K], w_hi[:, s, 0:K].bitcast(F32),
                                   ALU.subtract).then_inc(s_wlo, 1)

            pool.wait_ge(s_wlo, NB + 1)
            with pool.Fori(0, KD - 1) as j:
                split_lo(NB + 1 + 2 * j, 0, GR)
                split_lo(NB + 2 + 2 * j, 1, KD)
            split_lo(NC - 1, 0, GR)

            pool.wait_ge(s_wolo, 8)
            link(pool.memset(tri[:], 1.0))
            pool.affine_select(out=tri[:], in_=tri[:], compare_op=ALU.is_gt, fill=0.0, base=0,
                               pattern=[[1, P]], channel_multiplier=-1)
            pool.iota(io_i[:], pattern=[[1, GE]], base=0, channel_multiplier=0)
            pool.iota(row_i[:], pattern=[[P, TILES], [T, 2]], base=1, channel_multiplier=1)
            link(pool.iota(slot_i[:], pattern=[[1, CAP]], base=0, channel_multiplier=0))
            pool.tensor_copy(io[:], io_i[:])
            pool.tensor_copy(tri_b[:], tri[:])
            pool.memset(one_b[:], 1.0)
            link(pool.tensor_copy(row_f[:], row_i[:]))
            pool.tensor_scalar(thr[:], io[:, 0:PASSES - 1], float(CAP), float(CAP), ALU.mult, ALU.add)
            link(pool.tensor_copy(row_hi[:], row_f[:]))
            link(pool.tensor_tensor(row_lo[:], row_f[:], row_hi[:], ALU.subtract))
            link(pool.tensor_scalar(valid[:], row_f[:, TILES - 1, 0:1], float(T + 1), None, ALU.is_lt))
            pool.wait_ge(s_o, 2 * TILES)
            link(pool.tensor_copy(slot_f[:], slot_i[:]))
            pool.sem_inc(s_tri, 1)
            pool.memset(X[:], 0.0).then_inc(s_ct, 1)

            pool.wait_ge(s_h2st[0], 16 * ((TILES + 1) // 2))
            pool.wait_ge(s_h2st[1], 16 * (TILES // 2))
            pool.wait_ge(s_ct, 1)

            g_bound = pool.alloc_register("g_bound")
            s_bound = pool.alloc_register("s_bound")

            def gather(p, i, u):
                pool.wait_ge(s_gc, p * GE + i * WB + u + 1)
                pool.reg_add(g_bound, pool.zero_reg, T - 1)
                pool.indirect_dma_start(out=X[0:CAP, u, :], out_offset=None, in_=H2,
                                        in_offset=bass.IndirectOffsetOnAxis(ap=g_now[0:CAP, u:u + 1], axis=0),
                                        bounds_check=g_bound, oob_is_err=False).then_inc(s_xg[u], 16)

            def scatter(p, i, u):
                it = p * GE + i * WB + u
                pool.wait_ge(s_yA, it + 1)
                pool.wait_ge(s_yD, it + 1)
                pool.reg_add(s_bound, pool.zero_reg, 2 * T - 1)
                pool.indirect_dma_start(out=YK, out_offset=bass.IndirectOffsetOnAxis(ap=s_now[0:CAP, u:u + 1], axis=0),
                                        in_=Y[u][0:CAP, :], in_offset=None,
                                        bounds_check=s_bound, oob_is_err=False).then_inc(s_ys[u], 16)

            def ahead(p, i, u):
                gather(p, i + 1, u)
                scatter(p, i, u)

            def one(p):
                for u in range(WB):
                    gather(p, 0, u)
                for u in range(WB):
                    ahead(p, 0, u)
                with pool.Fori(1, GE // WB - 1) as i:
                    for u in range(WB):
                        ahead(p, i, u)
                for u in range(WB):
                    scatter(p, GE // WB - 1, u)

            rounds(pool, one)
            pool.wait_ge(s_gfin, 16)
            for t in range(TILES):
                n = P if t < TILES - 1 else LAST
                pool.wait_ge(s_fx, t + 1)
                pool.tensor_tensor(x1[0:n, t, :], x1[0:n, t, :], g_fin_b[0:n, :], ALU.mult).then_inc(s_fo, 1)

        @block.scalar
        def _(act):
            def h_hi_copy(t):
                n = P if t < TILES - 1 else LAST
                act.wait_ge(s_xT, t + 1)
                for q in range(2):
                    a = act.activation(h_hi[:, 4 * q:4 * q + 4, t * P:t * P + n], turned(t, q, n), ACT.Copy)
                a.then_inc(s_hhi, 1)

            def split_hi(n, s, K=KD):
                act.wait_ge(s_w[s], 8 * (n - s) + 16)
                act.activation(w_hi[:, s, 0:K], w_raw[:, s, 0:K], ACT.Copy).then_inc(s_whi, 1)

            act.wait_ge(s_eps, 1)
            act.activation(first_root[:], eps_rms[:], ACT.Sqrt)
            for t in range(TILES):
                n = P if t < TILES - 1 else LAST
                act.wait_ge(s_x[t % XS], 16 * (t // XS + 1))
                if t >= 1:
                    act.wait_ge(s_sq, t)
                act.activation(squares[0:n, :], xs[0:n, t % XS, :], ACT.Square,
                               accum_out=sumsq[0:n, t:t + 1]).then_inc(s_sq, 1)
                act.wait_ge(s_sq, t + 1)
                act.activation(rstd[0:n, t:t + 1], sumsq[0:n, t:t + 1], ACT.Sqrt, scale=1.0 / D, bias=eps_rms[0:n, :]).then_inc(s_std, 1)
                if t >= 1:
                    h_hi_copy(t - 1)
                if t in (2, 3):
                    split_hi(t - 2, t - 2)
            h_hi_copy(TILES - 1)

            def pool_input(n, c):
                for (a, pos, w) in runs(c, PH):
                    op = act.activation(U[:, n, pos:pos + w], ps[:, 3 * (n % 2) + c, a:a + w], ACT.Copy)
                return op

            for c in range(CHUNKS):
                for n in range(2):
                    act.wait_ge(s_mm, 2 * c + n + 1)
                    op = pool_input(n, c)
                    if c == CHUNKS - 1:
                        op.then_inc(s_free[n], 1)
                        split_hi(n + 2, n)
            for n in range(2, NU):
                for c in range(CHUNKS):
                    act.wait_ge(s_mm, 3 * n + c + 1)
                    op = pool_input(n, c)
                op.then_inc(s_free[n % 2], 1)
                split_hi(n + 2, n % 2)
            with act.Fori(0, GR) as j:
                n = NU + 2 * j
                for c in range(CHUNKS):
                    act.wait_ge(s_mm, 3 * n + c + 1)
                    for (a, pos, w) in runs(c, HIST):
                        op = act.activation(V[:, bass.ds(j, 1), pos:pos + w], ps[:, c:c + 1, a:a + w], ACT.Sigmoid)
                op.then_inc(s_free[0], 1)
                with act.If(j < GR - 1):
                    split_hi(n + 2, 0)
                with act.Else():
                    split_hi(n + 2, 0, GR)
                act.wait_ge(s_mm, 3 * (n + 2))
                split_hi(n + 3, 1)

            act.wait_ge(s_diff, GR)
            for g in range(GR):
                act.wait_ge(s_grp, g + 1)
                for c in range(CHUNKS):
                    op = act.activation(y_hi[:, g, c * CH:(c + 1) * CH], ps[:, 3 * (g % 2) + c, 0:CH], ACT.Copy,
                                        scale=vecs[:, SCALE + g:SCALE + g + 1])
                op.then_inc(s_yhi, 1)
            split_hi(NB + 1, 0, GR)

            def gate(n, jj, j, free0):
                act.wait_ge(s_free[0], free0)
                for c in range(CHUNKS):
                    act.wait_ge(s_mm, 3 * n + c + 1)
                    op = act.activation(S[:, jj, c * CH:(c + 1) * CH], ps[:, 3 + c, 0:CH], ACT.Sigmoid)
                op.then_inc(s_free[1], 1)

            act.wait_ge(s_tail, 64)

            def gate_p(i, jj):
                j = 2 * i + jj
                n = NB + 2 * j
                gate(n, jj, j, NG // 2 + j)
                split_hi(n + 2, 1)

            def w_after(i, jj):
                n = NB + 2 * (2 * i + jj)
                act.wait_ge(s_mm, 3 * (n + 2))
                split_hi(n + 3, 0, GR)

            with act.Fori(0, KD // 2 - 1) as i:
                for jj in range(2):
                    gate_p(i, jj)
                    w_after(i, jj)
            gate_p(KD // 2 - 1, 0)
            w_after(KD // 2 - 1, 0)
            gate_p(KD // 2 - 1, 1)

            def ln_square(p):
                a, w = LN_PIECES[p]
                act.wait_ge(s_cen, p + 1)
                wait(act, s_var, p)
                act.activation(ln_sq[:, :, 0:w], C[:, :, a:a + w], ACT.Square).then_inc(s_csq, 1)

            def ln_root(p):
                w = LN_PIECES[p][1]
                act.wait_ge(s_var, p + 1)
                wait(act, s_norm, p)
                act.activation(ln_rstd[:, 0:w], ps[:, 7, 0:w], ACT.Sqrt, bias=eps_ln[:]).then_inc(s_lstd, 1)

            def swish(p):
                act.wait_ge(s_norm, p + 1)
                a, w = LN_PIECES[p]
                pieces = [(a, a, w)] if a + w <= SEQ else [(a, a, SEQ - a), (SEQ + HIST, SEQ, DEC)]
                for g in range(GR):
                    for (x, y, n) in pieces:
                        op = act.activation(C[:, g, y:y + n], C[:, g, x:x + n], ACT.Silu,
                                            scale=vecs[:, LN_G + g:LN_G + g + 1], bias=vecs[:, LN_B + g:LN_B + g + 1])
                op.then_inc(s_silu, 1)

            for p in range(len(LN_PIECES)):
                ln_square(p)
                if p == 1:
                    w_after(KD // 2 - 1, 1)
                if p >= 1:
                    swish(p - 1)
                ln_root(p)
            swish(len(LN_PIECES) - 1)

            def pair(i):
                for jj in range(2):
                    j = 2 * i + jj
                    n = NC + 2 * j
                    gate(n, jj, j, NC // 2 + j)
                    if not isinstance(i, int) or jj == 0:
                        split_hi(n + 2, 1)
                        act.wait_ge(s_mm, 3 * (n + 2))
                        split_hi(n + 3, 0, GR)
                act.wait_ge(s_wo, 16 * i + 16)
                act.activation(wo_hi[0][:, bass.ds(2 * i, 2), :], wo_raw[:], ACT.Copy).then_inc(s_wohi, 1)

            with act.Fori(0, KD // 2 - 1) as i:
                pair(i)
            pair(KD // 2 - 1)

            act.wait_ge(s_mm, 3 * (NP - 1))
            for k in range(KD):
                act.wait_ge(s_free[0], (NP - 1) // 2 - KD + k + 2)
                act.activation(h_hi[:, k, :], M[:, k, :], ACT.Copy).then_inc(s_mhi, 1)
            with act.Fori(0, 4) as q:
                act.wait_ge(s_wo, 16 * q + 80)
                act.activation(wo_hi[1][:, bass.ds(2 * q, 2), :], wo_raw[:], ACT.Copy).then_inc(s_wohi, 1)

            def h2_turned(t):
                n = P if t < TILES - 1 else LAST
                act.wait_ge(s_h2T, t + 1)
                wait(act, s_lg, t - 1)
                for q in range(2):
                    src = ps[:, 4 + q, :].rearrange("p (k t) -> p k t", k=4)[:, :, 0:n]
                    a = act.activation(h2T[:, t % 2, 4 * q:4 * q + 4, 0:n], src, ACT.Copy)
                a.then_inc(s_h2c, 1)

            for t in range(TILES):
                n = P if t < TILES - 1 else LAST
                act.wait_ge(s_res, TILES + t + 1)
                wait(act, s_sq2, t)
                act.activation(squares2[0:n, :], x1[0:n, t, :], ACT.Square, accum_out=sumsq[0:n, t:t + 1]).then_inc(s_sq2, 1)
                act.wait_ge(s_sq2, t + 1)
                act.activation(rstd[0:n, t:t + 1], sumsq[0:n, t:t + 1], ACT.Sqrt, scale=1.0 / D,
                               bias=eps_rms[0:n, :]).then_inc(s_std2, 1)
                if t >= 1:
                    h2_turned(t - 1)
            h2_turned(TILES - 1)
            act.wait_ge(s_ra, 1)
            act.activation(dg[:], dg[:], ACT.Exp).then_inc(s_re, 1)
            act.wait_ge(s_ra, 2)
            act.activation(ex[:], ex[:], ACT.Exp).then_inc(s_re, 1)

            def x_turned(it, b):
                act.wait_ge(s_tx, it + 1)
                wait(act, s_gu, it - 1)
                act.activation(XT[:, b, 0:4, 0:CAP], ps[:, 0, :].rearrange("p (c t) -> p c t", c=4)[:, :, 0:CAP], ACT.Copy).then_inc(s_xtA, 1)

            def y_out(it, u, uses):
                act.wait_ge(s_down, it + 1)
                wait(act, s_ys[u], 16 * uses)
                act.activation(Y[u][0:CAP, 0:512], ps[0:CAP, 4 + 2 * (u % 2), :], ACT.Copy).then_inc(s_yA, 1)

            def step(p, i, u):
                it = p * GE + i * WB + u
                b = u % 2
                act.wait_ge(s_gu, it + 1)
                wait(act, s_act, it - 1)
                act.activation(sg[:, b, :, 0:CAP], ps[:, 2 + b, 0:KF * CAP].rearrange("p (c t) -> p c t", c=KF), ACT.Silu).then_inc(s_sg, 1)
                if not (isinstance(i, int) and i == GE // WB - 1 and u == WB - 1):
                    x_turned(it + 1, 1 - b)
                if not (isinstance(i, int) and i == 0 and u == 0):
                    y_out(it - 1, (u - 1) % WB, p * (GE // WB) + i + (u - 1) // WB)
                act.wait_ge(s_wl[u], 48 * (p * (GE // WB) + i + 1))
                wait(act, s_down, it)
                for c in range(KF):
                    op = act.activation(wdn_hi[c][:], wdn[u][:, c, :], ACT.Copy)
                op.then_inc(s_dnhi, 1)

            def one(p):
                x_turned(p * GE, 0)
                groups(act, step, p)
                y_out(p * GE + GE - 1, WB - 1, (p + 1) * (GE // WB) - 1)

            rounds(act, one)

            def scaled(t):
                n = P if t < TILES - 1 else LAST
                act.wait_ge(s_fr, t + 1)
                act.activation(x1[0:n, t, :], x1[0:n, t, :], ACT.Copy, scale=rstd[0:n, t:t + 1]).then_inc(s_fx, 1)

            for t in range(TILES):
                n = P if t < TILES - 1 else LAST
                act.wait_ge(s_fa, t + 1)
                wait(act, s_fq, t - 1)
                act.activation(sq3[0:n, t % 2, :], x1[0:n, t, :], ACT.Square, accum_out=sumsq[0:n, t:t + 1]).then_inc(s_fq, 1)
                act.wait_ge(s_fq, t + 1)
                act.activation(rstd[0:n, t:t + 1], sumsq[0:n, t:t + 1], ACT.Sqrt, scale=1.0 / D,
                               bias=eps_rms[0:n, :]).then_inc(s_fs, 1)
                if t >= 1:
                    scaled(t - 1)
            scaled(TILES - 1)

        @block.vector
        def _(dve):
            def h_lo_split(t):
                n = P if t < TILES - 1 else LAST
                dve.wait_ge(s_hhi, t + 1)
                for q in range(2):
                    d = dve.tensor_tensor(h_lo[:, 4 * q:4 * q + 4, t * P:t * P + n], turned(t, q, n),
                                          h_hi[:, 4 * q:4 * q + 4, t * P:t * P + n].bitcast(F32), ALU.subtract)
                d.then_inc(s_hlo, 1)

            def split_lo(n, s, K=KD):
                dve.wait_ge(s_whi, n + 1)
                dve.tensor_tensor(w_lo[:, s, 0:K], w_raw[:, s, 0:K], w_hi[:, s, 0:K].bitcast(F32),
                                  ALU.subtract).then_inc(s_wlo, 1)

            dve.wait_ge(s_const, 16)
            for t in range(TILES):
                n = P if t < TILES - 1 else LAST
                dve.wait_ge(s_std, t + 1)
                dve.reciprocal(rstd[0:n, t:t + 1], rstd[0:n, t:t + 1]).then_inc(s_rstd, 1)
                dve.wait_ge(s_rstd, t + 1)
                if t >= XN:
                    dve.wait_ge(s_xT, t - XN + 1)
                dve.scalar_tensor_tensor(out=xn[0:n, t % XN, :], in0=xs[0:n, t % XS, :], scalar=rstd[0:n, t:t + 1],
                                         in1=g_mix_b[0:n, :], op0=ALU.mult, op1=ALU.mult).then_inc(s_xn, 1)
                if t >= 1:
                    h_lo_split(t - 1)
                if t in (2, 3):
                    split_lo(t - 2, t - 2)
            h_lo_split(TILES - 1)
            dve.memset(hT[:, 2 * HT:].bitcast(F32), 0.0)

            dve.wait_ge(s_histT, 1)
            dve.wait_ge(s_ident, 2)
            dve.tensor_copy(U[:, :, PH + SEQ:PH + SEQ + PH],
                            ps[:, 6, :].rearrange("p (g t) -> p g t", g=GR)[:, :, 0:PH])
            dve.tensor_copy(w_dw[:], ps[:, 6, :].rearrange("p (g t) -> p g t", g=GR)[:, :, 32:32 + CW])
            dve.tensor_copy(vecs[:], ps[:, 7, 64:64 + 4 * GR])
            dve.tensor_copy(V[:, :, HIST + SEQ:HIST + SEQ + HIST],
                            ps[:, 7, :].rearrange("p (g t) -> p g t", g=GR)[:, :, 0:HIST]).then_inc(s_histC, 1)

            with dve.Fori(0, NU // 2) as i:
                for s in range(2):
                    split_lo(2 * i + s + 2, s)
            dve.wait_ge(s_sT, 1)
            dve.tensor_copy(state_out[0:PH, 0, :], ps[0:PH, 6, :])
            dve.tensor_copy(state_out[0:PH, 1, :], ps[0:PH, 7, :]).then_inc(s_sC, 1)

            def glu(j):
                n = NU + 2 * j
                split_lo(n + 2, 0, KD if not isinstance(j, int) else GR)
                for c in range(CHUNKS):
                    dve.wait_ge(s_mm, 3 * (n + 1) + c + 1)
                    if c == 0:
                        dve.wait_ge(s_free[0], j + NU // 2 + 1)
                    for (a, pos, w) in runs(c, HIST):
                        op = dve.tensor_tensor(V[:, bass.ds(j, 1), pos:pos + w], V[:, bass.ds(j, 1), pos:pos + w],
                                               ps[:, 3 + c:4 + c, a:a + w], ALU.mult)
                op.then_inc(s_free[1], 1)
                split_lo(n + 3, 1)

            def first_taps(j):
                dve.wait_ge(s_diff, j + 1)
                dve.wait_ge(s_sT, 1)
                dve.wait_ge(s_free[1], j + NU // 2 + 1)
                cj = C[:, bass.ds(j, 1), :]
                for k in range(A_TAPS):
                    v = V[:, bass.ds(j, 1), k:k + CWID]
                    tap = w_dw[:, bass.ds(j, 1), k]
                    if k == 0:
                        op = dve.tensor_scalar(cj, v, tap, vecs[:, bass.ds(BIAS + j, 1)], ALU.mult, ALU.add)
                    else:
                        dve.wait_ge(s_conv, A_TAPS * j + k)
                        op = dve.scalar_tensor_tensor(out=cj, in0=v, scalar=tap, in1=cj, op0=ALU.mult, op1=ALU.add)
                    op.then_inc(s_conv, 1)

            with dve.Fori(0, GR - 1) as j:
                glu(j)
                first_taps(j)
            glu(GR - 1)
            dve.wait_ge(s_sT, 2)
            dve.tensor_copy(state_out[0:HIST, 2, :], ps[0:HIST, 6, :])
            dve.tensor_copy(state_out[0:HIST, 3, :], ps[0:HIST, 7, :]).then_inc(s_sC, 1)
            for g in range(GR):
                dve.wait_ge(s_yhi, g + 1)
                for c in range(CHUNKS):
                    op = dve.scalar_tensor_tensor(out=y_lo[:, g, c * CH:(c + 1) * CH], in0=ps[:, 3 * (g % 2) + c, 0:CH],
                                                  scalar=vecs[:, SCALE + g:SCALE + g + 1],
                                                  in1=y_hi[:, g, c * CH:(c + 1) * CH].bitcast(F32),
                                                  op0=ALU.mult, op1=ALU.subtract)
                op.then_inc(s_ylo, 1)
            dve.wait_ge(s_ylo, GR)
            dve.sem_inc(s_free[0], 1)
            first_taps(GR - 1)

            def taps(k0, k, base):
                for g in range(GR):
                    dve.wait_ge(s_conv, base + g + 1)
                    dve.scalar_tensor_tensor(out=C[:, g, :], in0=V[:, g, bass.ds(k0 + k, CWID)],
                                             scalar=w_dw[:, g, bass.ds(k0 + k, 1)], in1=C[:, g, :],
                                             op0=ALU.mult, op1=ALU.add).then_inc(s_conv, 1)

            def later_taps(i, jj):
                k0 = A_TAPS + sum(B_TAPS) * i
                for k in range(jj * B_TAPS[0], jj * B_TAPS[0] + B_TAPS[jj]):
                    taps(k0, k, GR * (k0 + k - 1))

            def gated_p(j, jj):
                n = NB + 2 * j
                dve.wait_ge(s_free[1], NG // 2 + 1 + j)
                for c in range(CHUNKS):
                    dve.wait_ge(s_mm, 3 * (n + 1) + c + 1)
                    op = dve.tensor_tensor(M[:, bass.ds(j, 1), c * CH:(c + 1) * CH], S[:, jj:jj + 1, c * CH:(c + 1) * CH],
                                           ps[:, c:c + 1, 0:CH], ALU.mult)
                op.then_inc(s_free[0], 1)

            def step_p(i, jj):
                j = 2 * i + jj
                later_taps(i, jj)
                gated_p(j, jj)

            gated_p(0, 0)
            later_taps(0, 0)
            step_p(0, 1)
            with dve.Fori(1, KD // 2 - 1) as i:
                for jj in range(2):
                    step_p(i, jj)
            step_p(KD // 2 - 1, 0)
            later_taps(KD // 2 - 1, 1)
            dve.wait_ge(s_wlo, NC)
            split_lo(NC, 1)

            def wide(ap, w):
                return ap.unsqueeze(1).to_broadcast((P, GR, w))

            def ln_centre(p):
                a, w = LN_PIECES[p]
                dve.wait_ge(s_mean, p + 1)
                dve.tensor_tensor(C[:, :, a:a + w], C[:, :, a:a + w], wide(ps[:, 6, 0:w], w), ALU.subtract).then_inc(s_cen, 1)

            def ln_scale(p):
                a, w = LN_PIECES[p]
                dve.wait_ge(s_lstd, p + 1)
                dve.reciprocal(ln_rstd[:, 0:w], ln_rstd[:, 0:w]).then_inc(s_lrec, 1)
                dve.wait_ge(s_lrec, p + 1)
                dve.tensor_tensor(C[:, :, a:a + w], C[:, :, a:a + w], wide(ln_rstd[:, 0:w], w), ALU.mult).then_inc(s_norm, 1)

            def swish_split(p):
                a, w = LN_PIECES[p]
                e = min(a + w, T)
                dve.wait_ge(s_silu, p + 1)
                dve.tensor_copy(a_hi[:, :, a:e], C[:, :, a:e]).then_inc(s_ahi, 1)
                dve.wait_ge(s_ahi, p + 1)
                dve.tensor_tensor(a_lo[:, :, a:e], C[:, :, a:e], a_hi[:, :, a:e].bitcast(F32), ALU.subtract).then_inc(s_alo, 1)

            ln_centre(0)
            ln_centre(1)
            ln_scale(0)
            gated_p(KD - 1, 1)
            split_lo(NC + 1, 0, GR)
            for p in range(2, len(LN_PIECES)):
                ln_centre(p)
                ln_scale(p - 1)
                swish_split(p - 2)
            ln_scale(len(LN_PIECES) - 1)
            for p in range(len(LN_PIECES) - 2, len(LN_PIECES)):
                swish_split(p)

            def m_lo(k):
                dve.wait_ge(s_mhi, k + 1)
                dve.tensor_tensor(h_lo[:, k, :], M[:, k, :], h_hi[:, k, :].bitcast(F32), ALU.subtract).then_inc(s_mlo, 1)

            def wo_lo_quarter(h, q):
                dve.wait_ge(s_wohi, 4 * h + q + 1)
                dve.tensor_tensor(wo_lo[h][:, bass.ds(2 * q, 2), :], wo_raw[:], wo_hi[h][:, bass.ds(2 * q, 2), :].bitcast(F32),
                                  ALU.subtract).then_inc(s_wolo, 1)

            def pair(i):
                for jj in range(2):
                    j = 2 * i + jj
                    n = NC + 2 * j
                    last = isinstance(i, int) and jj == 1
                    if not last:
                        split_lo(n + 2, 1)
                    else:
                        wo_lo_quarter(0, i)
                        for k in range(KD - 1):
                            m_lo(k)
                    dve.wait_ge(s_free[1], NC // 2 + 1 + j)
                    for c in range(CHUNKS):
                        dve.wait_ge(s_mm, 3 * (n + 1) + c + 1)
                        sc = S[:, jj:jj + 1, c * CH:(c + 1) * CH]
                        dve.tensor_tensor(sc, sc, ps[:, c:c + 1, 0:CH], ALU.mult).then_inc(s_sy, 1)
                    for c in range(CHUNKS):
                        sc = S[:, jj:jj + 1, c * CH:(c + 1) * CH]
                        mc = M[:, bass.ds(j, 1), c * CH:(c + 1) * CH]
                        dve.wait_ge(s_sy, 3 * j + c + 1)
                        op = dve.tensor_tensor(mc, mc, sc, ALU.add)
                    op.then_inc(s_free[0], 1)
                    if not last:
                        split_lo(n + 3, 0, GR)
                if not isinstance(i, int):
                    wo_lo_quarter(0, i)

            with dve.Fori(0, KD // 2 - 1) as i:
                pair(i)
            pair(KD // 2 - 1)
            m_lo(KD - 1)
            def h2_tile(t):
                n = P if t < TILES - 1 else LAST
                dve.wait_ge(s_std2, t + 1)
                dve.reciprocal(rstd[0:n, t:t + 1], rstd[0:n, t:t + 1]).then_inc(s_rs2, 1)
                dve.wait_ge(s_rs2, t + 1)
                if t == 0:
                    dve.wait_ge(s_rc, 16 * 5)
                wait(dve, s_h2T, t - 1)
                wait(dve, s_h2st[t % 2], 16 * (t // 2))
                dve.scalar_tensor_tensor(out=h2[0:n, t % 2, :].rearrange("r (c p) -> r p c", c=KD),
                                         in0=x1[0:n, t, :].rearrange("r (p c) -> r p c", c=KD), scalar=rstd[0:n, t:t + 1],
                                         in1=g_ffn_b[0:n, :].rearrange("r (p c) -> r p c", c=KD),
                                         op0=ALU.mult, op1=ALU.mult).then_inc(s_h2, 1)

            for n in range(2 * TILES):
                h, t = divmod(n, TILES)
                rows = P if t < TILES - 1 else LAST
                dve.wait_ge(s_o, n + 1)
                dve.wait_ge(s_xr[n % 2], 16 * (n // 2 + 1))
                dve.tensor_tensor(x1[0:rows, t, h * 512:(h + 1) * 512], xr[0:rows, n % 2, :], ps[0:rows, (n + 3) % 4, :],
                                  ALU.add).then_inc(s_res, 1)
                if n < 4:
                    wo_lo_quarter(1, n)
                if h == 1:
                    h2_tile(t)

            done = [0]

            def link(op):
                done[0] += 1
                op.then_inc(s_rt, 1)
                dve.wait_ge(s_rt, done[0])

            def b3(ap, n):
                return ap.unsqueeze(2).to_broadcast((P, TILES, n))

            def row(ap, n):
                return ap[:, 0:n].unsqueeze(1).to_broadcast((P, TILES, n))

            link(dve.memset(L[:], 0.0))
            dve.wait_ge(s_lg, TILES)
            dve.wait_ge(s_tri, 1)
            lview = ps[:, 6, 0:TILES * NR].rearrange("p (t r) -> p t r", r=NR)
            dve.tensor_tensor(L[:, 0:TILES - 1, :], lview[:, 0:TILES - 1, :],
                              b_r[:].unsqueeze(1).to_broadcast((P, TILES - 1, NR)), ALU.add)
            link(dve.tensor_tensor(L[0:LAST, TILES - 1, :], lview[0:LAST, TILES - 1, :], b_r[0:LAST, :], ALU.add))
            lg = L[:, :, 0:G]
            le = L[:, :, G:NR].rearrange("p t (g e) -> p t g e", g=G)

            def first_max(vals, best, eq, pick, n):
                link(dve.tensor_reduce(best[:], vals, AX.X, ALU.max))
                link(dve.tensor_tensor(eq[:], vals, b3(best[:], n), ALU.is_equal))
                link(dve.scalar_tensor_tensor(out=eq[:], in0=eq[:], scalar=-2.0 * n, in1=row(io, n),
                                              op0=ALU.mult, op1=ALU.add))
                link(dve.tensor_reduce(gmin[:], eq[:], AX.X, ALU.min))
                link(dve.tensor_tensor(pick[:], eq[:], b3(gmin[:], n), ALU.is_equal))

            first_max(lg, gmax, tg, og, G)
            dve.tensor_tensor(dg[:], lg, b3(gmax[:], G), ALU.subtract).then_inc(s_ra, 1)
            link(dve.tensor_tensor(tmp32[:], le, og[:].unsqueeze(3).to_broadcast((P, TILES, G, E)), ALU.mult))
            link(dve.tensor_reduce(les[:], tmp32[:].rearrange("p t g e -> p t e g"), AX.X, ALU.add))
            first_max(les[:], m1, te, oe[0], E)
            link(dve.scalar_tensor_tensor(out=les[:], in0=oe[0][:], scalar=-1.0e30, in1=les[:], op0=ALU.mult, op1=ALU.add))
            first_max(les[:], m2, te, oe[1], E)
            dve.tensor_tensor(ex[:], m2[:], m1[:], ALU.subtract).then_inc(s_ra, 1)
            for k in range(2):
                link(dve.tensor_tensor(Ek[k][:], og[:].unsqueeze(3).to_broadcast((P, TILES, G, E)),
                                       oe[k][:].unsqueeze(2).to_broadcast((P, TILES, G, E)), ALU.mult))
            flat = [e[:].rearrange("p t g e -> p t (g e)") for e in Ek]
            link(dve.tensor_tensor(A[:], flat[0], flat[1], ALU.add))
            dve.tensor_scalar(A[:, TILES - 1, :], A[:, TILES - 1, :], valid[:], None, ALU.mult).then_inc(s_cum, 1)
            for k in range(2):
                link(dve.tensor_scalar(flat[k][:, TILES - 1, :], flat[k][:, TILES - 1, :], valid[:], None, ALU.mult))
            dve.wait_ge(s_re, 2)
            link(dve.tensor_reduce(zsum[:], dg[:], AX.X, ALU.add))
            link(dve.tensor_scalar(den[:], ex[:], 1.0, None, ALU.add))
            link(dve.tensor_tensor(den[:], den[:], zsum[:], ALU.mult))
            link(dve.reciprocal(wts[:, :, 0], den[:]))
            link(dve.tensor_tensor(wts[:, :, 1], wts[:, :, 0], ex[:], ALU.mult))
            for k in range(2):
                dve.tensor_tensor(slot_rows[:, k, :, 0], flat[k], b3(row_hi[:, :, k], GE), ALU.mult)
                link(dve.tensor_tensor(slot_rows[:, k, :, 1], flat[k], b3(row_lo[:, :, k], GE), ALU.mult))
            dve.wait_ge(s_rk, 1)
            ranks = ps[:, 7, 0:TILES * GE].rearrange("p (t e) -> p t e", e=GE)
            tmpf = tmp32[:].rearrange("p t g e -> p t (g e)")

            def placed(k):
                return dve.tensor_tensor(where[:, k], slot_f[:].unsqueeze(1).to_broadcast((P, TILES, CAP)),
                                         b3(rank[:, :, k], CAP), ALU.is_equal)

            for k in range(2):
                link(dve.tensor_tensor(tmpf, flat[k], ranks, ALU.mult))
                link(dve.tensor_reduce(rank[:, :, k], tmpf, AX.X, ALU.add))
                placed(k).then_inc(s_where, 1)
            dve.wait_ge(s_h2st[0], 16 * ((TILES + 1) // 2))
            dve.wait_ge(s_h2st[1], 16 * (TILES // 2))
            for half in (AT_hi, AT_lo):
                link(dve.memset(half[:, :, :, CAP:P].bitcast(F32), 0.0))
            link(dve.tensor_reduce(nmax[:], ps[:, 5, 0:GE], AX.X, ALU.max))
            link(dve.tensor_tensor(ge8[:], nmax[:].to_broadcast((P, PASSES - 1)), thr[:], ALU.is_gt))
            link(dve.tensor_reduce(np_f[:], ge8[:], AX.X, ALU.add))
            dve.tensor_scalar(np_i[:], np_f[:], 1.0, None, ALU.add).then_inc(s_np, 1)

            def x_turned(it, b):
                dve.wait_ge(s_tx, it + 1)
                wait(dve, s_gu, it - 1)
                dve.tensor_copy(XT[:, b, 4:8, 0:CAP], ps[:, 1, :].rearrange("p (c t) -> p c t", c=4)[:, :, 0:CAP]).then_inc(s_xtD, 1)

            def column(ap, e):
                return ap[0:CAP, e:e + 1] if isinstance(e, int) else ap[0:CAP, bass.ds(e, 1)]

            def g_column(e, u):
                dve.tensor_copy(g_now[0:CAP, u:u + 1], column(g_idx, e)).then_inc(s_gc, 1)

            def y_out(it, u, uses, e):
                dve.wait_ge(s_down, it + 1)
                wait(dve, s_ys[u], 16 * uses)
                dve.tensor_copy(s_now[0:CAP, u:u + 1], column(s_idx, e))
                dve.tensor_copy(Y[u][0:CAP, 512:1024], ps[0:CAP, 5 + 2 * (u % 2), :]).then_inc(s_yD, 1)

            def step(p, i, u):
                it = p * GE + i * WB + u
                b = u % 2
                if not (isinstance(i, int) and i == GE // WB - 1):
                    g_column(i * WB + u + WB, u)
                dve.wait_ge(s_sg, it + 1)
                wait(dve, s_down, it - 1)
                wait(dve, s_act, it)
                dve.tensor_tensor(AT[:, :, 0:CAP], sg[:, b, :, 0:CAP],
                                  ps[:, 2 + b, KF * CAP:2 * KF * CAP].rearrange("p (c t) -> p c t", c=KF),
                                  ALU.mult).then_inc(s_prod, 1)
                dve.wait_ge(s_prod, it + 1)
                dve.tensor_copy(AT_hi[:, b, :, 0:CAP], AT[:, :, 0:CAP]).then_inc(s_athi, 1)
                dve.wait_ge(s_athi, it + 1)
                dve.tensor_tensor(AT_lo[:, b, :, 0:CAP], AT[:, :, 0:CAP], AT_hi[:, b, :, 0:CAP].bitcast(F32),
                                  ALU.subtract).then_inc(s_act, 1)
                if not (isinstance(i, int) and i == GE // WB - 1 and u == WB - 1):
                    x_turned(it + 1, 1 - b)
                if not (isinstance(i, int) and i == 0 and u == 0):
                    y_out(it - 1, (u - 1) % WB, p * (GE // WB) + i + (u - 1) // WB, i * WB + u - 1)
                dve.wait_ge(s_dnhi, it + 1)
                for c in range(KF):
                    op = dve.tensor_tensor(wdn_lo[u][:, c, :], wdn[u][:, c, :], wdn_hi[c][:].bitcast(F32), ALU.subtract)
                op.then_inc(s_dnlo, 1)

            PREP = 6

            def one(p):
                step_no = [0]

                def prep(op):
                    step_no[0] += 1
                    op.then_inc(s_prep, 1)
                    dve.wait_ge(s_prep, p * PREP + step_no[0])

                if not isinstance(p, int):
                    for k in range(2):
                        placed(k).then_inc(s_where, 1)
                dve.wait_ge(s_rows, p + 1)
                prep(dve.tensor_reduce(found[0:CAP], ps[0:CAP, 6, 0:2 * GE].rearrange("p (h e) -> p e h", h=2), AX.X, ALU.add))
                prep(dve.tensor_scalar(wrap[0:CAP], found[0:CAP], 0.0, NOWHERE, ALU.is_equal, ALU.mult))
                prep(dve.scalar_tensor_tensor(out=s_idx[0:CAP], in0=found[0:CAP], scalar=-1.0, in1=wrap[0:CAP], op0=ALU.add, op1=ALU.add))
                prep(dve.tensor_scalar(wrap[0:CAP], s_idx[0:CAP], float(T), -float(T), ALU.is_ge, ALU.mult))
                prep(dve.tensor_tensor(g_idx[0:CAP], s_idx[0:CAP], wrap[0:CAP], ALU.add))
                prep(dve.tensor_scalar(rank[:], rank[:], -float(CAP), None, ALU.add))
                for u in range(WB):
                    g_column(u, u)
                x_turned(p * GE, 0)
                groups(dve, step, p)
                y_out(p * GE + GE - 1, WB - 1, (p + 1) * (GE // WB) - 1, GE - 1)

            rounds(dve, one)

            def root(t):
                n = P if t < TILES - 1 else LAST
                dve.wait_ge(s_fs, t + 1)
                dve.reciprocal(rstd[0:n, t:t + 1], rstd[0:n, t:t + 1]).then_inc(s_fr, 1)

            for t in range(TILES):
                n = P if t < TILES - 1 else LAST
                dve.wait_ge(s_yy[t], 16)
                for k in range(2):
                    wait(dve, s_f1, t + k)
                    dve.scalar_tensor_tensor(out=x1[0:n, t, :], in0=yy[0:n, t, k, :], scalar=wts[0:n, t, k:k + 1],
                                             in1=x1[0:n, t, :], op0=ALU.mult, op1=ALU.add).then_inc((s_f1, s_fa)[k], 1)
                    if k == 0 and t >= 1:
                        root(t - 1)
            root(TILES - 1)

        @block.tensor
        def _(pe):
            def product(bank, w, s, hi, lo, K, c):
                for k in range(K):
                    for q, (a, r) in enumerate(((w_hi, hi), (w_hi, lo), (w_lo, hi))):
                        m = pe.matmul(ps[:, bank, 0:CH], a[:, s, w + k, :], r[:, w + k, c * CH:(c + 1) * CH],
                                      start=(k == 0 and q == 0), stop=(k == K - 1 and q == 2))
                return m

            def turn(t):
                n = P if t < TILES - 1 else LAST
                pe.wait_ge(s_xn, t + 1)
                if t >= 4:
                    pe.wait_ge(s_hlo, t)
                for k in range(KD):
                    m = pe.transpose(turned(t, k // 4, n)[:, k % 4, :], xn[0:n, t % XN, k * P:(k + 1) * P], ident[0:n, 0:n])
                m.then_inc(s_xT, 1)

            def first_panels(n, c):
                pe.wait_ge(s_hlo, min(TILES, ((c + 1) * CH + P - 1) // P))
                pe.wait_ge(s_whi, n + 1)
                pe.wait_ge(s_wlo, n + 1)
                product(3 * n + c, 0, n, h_hi, h_lo, KD, c).then_inc(s_mm, 1)

            pe.wait_ge(s_ident, 1)
            for t in range(4):
                turn(t)
            first_panels(0, 0)
            turn(4)
            first_panels(1, 0)
            turn(5)
            first_panels(0, 1)
            turn(6)
            first_panels(1, 1)
            turn(7)
            turn(8)
            pe.wait_ge(s_hist, 16 * 7)
            pe.wait_ge(s_hlo, TILES)
            for g in range(GR):
                pe.transpose(ps[:, 6, g * P:g * P + PH], hist_in[0:PH, 0, g * P:(g + 1) * P], ident[0:PH, 0:PH])
            for g in range(GR):
                pe.transpose(ps[:, 6, g * P + 32:g * P + 32 + CW], hist_in[:, 2, g * P:(g + 1) * P], ident[0:CW, 0:CW])
            pe.transpose(ps[:, 7, 64:64 + 4 * GR], vec_in[:], ident[0:4 * GR, 0:4 * GR])
            for g in range(GR):
                m = pe.transpose(ps[:, 7, g * P:g * P + HIST], hist_in[0:HIST, 1, g * P:(g + 1) * P], ident[0:HIST, 0:HIST])
            m.then_inc(s_histT, 1)
            for n in range(2):
                first_panels(n, 2)

            def panel(n, half, s, hi, lo, K):
                pe.wait_ge(s_whi, n + 1)
                pe.wait_ge(s_wlo, n + 1)
                pe.wait_ge(s_free[s], half)
                for c in range(CHUNKS):
                    product(3 * s + c, 0, s, hi, lo, K, c).then_inc(s_mm, 1)

            def tails(src, n, starts):
                for q in range(2):
                    for g in range(GR):
                        m = pe.transpose(ps[0:n, 6 + q, g * P:(g + 1) * P], src[:, g, starts[q]:starts[q] + n], ident[:])
                m.then_inc(s_sT, 1)

            for s in range(2):
                panel(2 + s, 1, s, h_hi, h_lo, KD)
            pe.wait_ge(s_free[0], NU // 2)
            pe.wait_ge(s_free[1], NU // 2)
            pe.wait_ge(s_histC, 1)
            tails(U, PH, (SEQ, UW - PH))
            with pe.Fori(NU // 2, NG // 2) as i:
                for s in range(2):
                    panel(2 * i + s, i, s, h_hi, h_lo, KD)
            pe.wait_ge(s_free[0], NG // 2)
            pe.wait_ge(s_free[1], NG // 2)
            pe.wait_ge(s_sC, 1)
            tails(V, HIST, (SEQ, VW - HIST))
            pe.wait_ge(s_whi, NG + 1)
            pe.wait_ge(s_wlo, NG + 1)
            for g in range(GR):
                pe.wait_ge(s_diff, g + 1)
                if g >= 2:
                    pe.wait_ge(s_ylo, g - 1)
                for c in range(CHUNKS):
                    m = product(3 * (g % 2) + c, g, 0, d_hi, d_lo, 1, c)
                m.then_inc(s_grp, 1)
            pe.sem_inc(s_mm, 3)
            pe.wait_ge(s_ylo, GR)
            with pe.Fori(0, KD - 1) as j:
                panel(NB + 2 * j, NG // 2 + j, 1, h_hi, h_lo, KD)
                panel(NB + 1 + 2 * j, NG // 2 + 1 + j, 0, y_hi, y_lo, GR)

            def ln_sum(src, bank, p, s_done):
                w = LN_PIECES[p][1]
                for g in range(GR):
                    m = pe.matmul(ps[:, bank, 0:w], ln_mean[:], src(g), start=(g == 0), stop=(g == GR - 1))
                m.then_inc(s_done, 1)

            def mean(p):
                a, w = LN_PIECES[p]
                wait(pe, s_cen, p)
                ln_sum(lambda g: C[:, g, a:a + w], 6, p, s_mean)

            def variance(p):
                w = LN_PIECES[p][1]
                pe.wait_ge(s_csq, p + 1)
                wait(pe, s_lstd, p)
                ln_sum(lambda g: ln_sq[:, g, 0:w], 7, p, s_var)

            n = NC - 2
            panel(n, NG // 2 + KD - 1, 1, h_hi, h_lo, KD)
            pe.wait_ge(s_conv, CW * GR)
            mean(0)
            between = {(NC - 1, 0): (0, 1), (NC - 1, 2): (1, 2), (NC, 0): (2, 3), (NC, 1): (3, None)}
            for n, s, a, r_hi, r_lo, K in ((NC - 1, 0, NC // 2, y_hi, y_lo, GR), (NC, 1, NC // 2, h_hi, h_lo, KD)):
                pe.wait_ge(s_whi, n + 1)
                pe.wait_ge(s_wlo, n + 1)
                pe.wait_ge(s_free[s], a)
                for c in range(CHUNKS):
                    product(3 * s + c, 0, s, r_hi, r_lo, K, c).then_inc(s_mm, 1)
                    v, m = between.get((n, c), (None, None))
                    if v is not None:
                        variance(v)
                    if m is not None:
                        mean(m)
            assert len(LN_PIECES) == 4
            n = NC + 1
            pe.wait_ge(s_whi, n + 1)
            pe.wait_ge(s_wlo, n + 1)
            pe.wait_ge(s_free[0], NC // 2 + 1)
            for c in range(CHUNKS):
                pe.wait_ge(s_alo, min(len(LN_PIECES), ((c + 1) * CH + LN_W - 1) // LN_W))
                product(c, 0, 0, a_hi, a_lo, GR, c).then_inc(s_mm, 1)
            with pe.Fori(1, KD) as j:
                panel(NC + 2 * j, NC // 2 + j, 1, h_hi, h_lo, KD)
                panel(NC + 1 + 2 * j, NC // 2 + 1 + j, 0, a_hi, a_lo, GR)
            pe.wait_ge(s_free[1], NP // 2)

            def h2_turn(t):
                n = P if t < TILES - 1 else LAST
                pe.wait_ge(s_h2, t + 1)
                wait(pe, s_h2c, t)
                for c in range(KD):
                    m = pe.transpose(ps[:, 4 + c // 4, (c % 4) * P:(c % 4) * P + n], h2[0:n, t % 2, c * P:(c + 1) * P],
                                     ident[0:n, 0:n])
                m.then_inc(s_h2T, 1)

            def logits(t):
                n = P if t < TILES - 1 else LAST
                pe.wait_ge(s_h2c, t + 1)
                for c in range(KD):
                    m = pe.matmul(ps[0:n, 6, t * NR:(t + 1) * NR], h2T[:, t % 2, c, 0:n], w_r[:, c, :],
                                  start=(c == 0), stop=(c == KD - 1))
                m.then_inc(s_lg, 1)

            for n in range(2 * TILES):
                h, t = divmod(n, TILES)
                if t == 0:
                    pe.wait_ge(s_wohi, 4 * h + 4)
                    pe.wait_ge(s_wolo, 4 * h + 4)
                if n == 1:
                    pe.wait_ge(s_free[0], (NP + 1) // 2)
                if n >= 4:
                    pe.wait_ge(s_res, n - 3)
                for k in range(KD):
                    if n == 0:
                        pe.wait_ge(s_mhi, k + 1)
                        pe.wait_ge(s_mlo, k + 1)
                    o = k * T + t * P
                    hi, lo = hT[:, o:o + P], hT[:, HT + o:HT + o + P]
                    for q, (a, w) in enumerate(((hi, wo_hi), (lo, wo_hi), (hi, wo_lo))):
                        m = pe.matmul(ps[:, (n + 3) % 4, :], a, w[h][:, k, :], start=(k == 0 and q == 0),
                                      stop=(k == KD - 1 and q == 2))
                m.then_inc(s_o, 1)
                if h == 1 and t >= 1:
                    h2_turn(t - 1)
                if h == 1 and t >= 2:
                    logits(t - 2)
            logits(TILES - 2)
            h2_turn(TILES - 1)
            logits(TILES - 1)
            pe.wait_ge(s_cum, 1)
            aflat = A[:].rearrange("p t e -> p (t e)")
            pe.matmul(ps[:, 7, 0:TILES * GE], tri_b[:], aflat, start=True, stop=False)
            for t in range(TILES - 1):
                rest = TILES - 1 - t
                pe.matmul(ps[:, 7, (t + 1) * GE:TILES * GE].rearrange("p (t e) -> p t e", e=GE), one_b[:],
                          A[:, t:t + 1, :].to_broadcast((P, rest, GE)), start=False, stop=(rest == 1))
            for t in range(TILES):
                m = pe.matmul(ps[:, 5, 0:GE], one_b[:], A[:, t, :], start=(t == 0), stop=(t == TILES - 1))
            m.then_inc(s_rk, 1)

            def x_turn(it, u, quarter):
                pe.wait_ge(s_xg[u], 16 * (quarter + 1))
                wait(pe, s_xtA, it)
                wait(pe, s_xtD, it)
                for c in range(KD):
                    r = P if c == 0 else CAP
                    m = pe.transpose(ps[:, c // 4, (c % 4) * P:(c % 4) * P + r], X[0:r, u, c * P:(c + 1) * P], ident[0:r, 0:r])
                m.then_inc(s_tx, 1)

            def down(it, u):
                b = u % 2
                pe.wait_ge(s_act, it + 1)
                wait(pe, s_yA, it - 1)
                wait(pe, s_yD, it - 1)
                pe.wait_ge(s_dnlo, it + 1)
                for h in range(2):
                    cols = slice(h * 512, (h + 1) * 512)
                    for c in range(KF):
                        for q, (a, w) in enumerate(((AT_hi, wdn_hi[c][:, cols]), (AT_lo, wdn_hi[c][:, cols]),
                                                    (AT_hi, wdn_lo[u][:, c, cols]))):
                            m = pe.matmul(ps[:, 4 + 2 * b + h, :], a[:, b, c, :], w, start=(c + q == 0),
                                          stop=(c == KF - 1 and q == 2))
                m.then_inc(s_down, 1)

            def step(p, i, u):
                it = p * GE + i * WB + u
                b = u % 2
                pe.wait_ge(s_xtA, it + 1)
                pe.wait_ge(s_xtD, it + 1)
                wait(pe, s_act, it - 1)
                pe.wait_ge(s_wl[u], 48 * (p * (GE // WB) + i + 1))
                for h in range(2):
                    for f in range(KF):
                        o = (h * KF + f) * CAP
                        for c in range(KD):
                            m = pe.matmul(ps[:, 2 + b, o:o + CAP], wgu[u][:, h, c, f * P:(f + 1) * P], XT[:, b, c, 0:CAP],
                                          start=(c == 0), stop=(c == KD - 1))
                m.then_inc(s_gu, 1)
                if not (isinstance(i, int) and i == GE // WB - 1 and u == WB - 1):
                    x_turn(it + 1, (u + 1) % WB, p * (GE // WB) + i + (u + 1) // WB)
                if not (isinstance(i, int) and i == 0 and u == 0):
                    down(it - 1, (u - 1) % WB)

            def one(p):
                wait(pe, s_yA, p * GE)
                for k in range(2):
                    pe.wait_ge(s_where, 2 * p + k + 1)
                    for t in range(TILES):
                        m = pe.matmul(ps[0:CAP, 6, 0:2 * GE], where[:, k, t, :], slot_rows[:, k, t].rearrange("p h e -> p (h e)"),
                                      start=(t + k == 0), stop=(t == TILES - 1 and k == 1))
                m.then_inc(s_rows, 1)
                x_turn(p * GE, 0, p * (GE // WB))
                groups(pe, step, p)
                down(p * GE + GE - 1, WB - 1)

            rounds(pe, one)


_INS = ['x_prompt', 'x_sample', 'state_pool', 'state_conv', 'g_mix', 'w_in', 'w_pool_grp', 'pool_scale',
        'w_pool_out', 'w_dw', 'b_dw', 'ln_g', 'ln_b', 'w_conv_out', 'w_out', 'g_ffn', 'w_rg', 'b_rg', 'w_re',
        'b_re', 'w_gate', 'w_up', 'w_down', 'g_final']
_OUTS = [('y_prompt', (1, SEQ, D)), ('y_sample', (1, DEC, D)), ('new_pool_prompt', (1, 1, PH, D_POOL)),
         ('new_conv_prompt', (1, 1, HIST, D_CONV)), ('new_pool_sample', (1, 1, PH, D_POOL)),
         ('new_conv_sample', (1, 1, HIST, D_CONV))]


def kernel(**inputs):
    import numpy as _np
    import concourse.bacc as _bacc
    from concourse.bass_utils import run_bass_kernel_spmd as _run

    nc = _bacc.Bacc("TRN2", target_bir_lowering=False, num_devices=1)
    arrays, ins, outs = {}, {}, {}
    for name in _INS:
        a = _np.ascontiguousarray(inputs[name])
        arrays[f"in_{name}"] = a
        ins[name] = nc.dram_tensor(f"in_{name}", a.shape, mybir.dt.from_np(a.dtype), kind="ExternalInput").ap()
    for name, shape in _OUTS:
        outs[name] = nc.dram_tensor(f"out_{name}", shape, F32, kind="ExternalOutput").ap()
    build(nc, ins, outs)
    r = _run(nc, [arrays], core_ids=[0])
    return tuple(r.results[0][f"out_{name}"] for name, _ in _OUTS)
```
